# Optimizing a Trainium2 kernel written in Bass

```python
import jax, jax.numpy as jnp
from jax import lax
import numpy as np

D_MODEL = 2048
BATCH = 1
SEQ = 128
DEPTH = 2
DEC_BATCH = 1
DEC_SEQ = 256
PAST_LEN = 128

GRID_W = 64
HEAD_DIM = 64
ATTN_W = D_MODEL // 2
N_HEADS = ATTN_W // HEAD_DIM
N_KV_HEADS = 4
GQA_GROUP = N_HEADS // N_KV_HEADS
KV_W = N_KV_HEADS * HEAD_DIM
POOL_W = D_MODEL // 4
POOL_WINDOWS = (2, 4, 8, 16)
POOL_GROUPS = len(POOL_WINDOWS)
POOL_GW = POOL_W // POOL_GROUPS
CONV_W = D_MODEL // 4
CONV_K = 31
MIX_W = ATTN_W + POOL_W + CONV_W
IN_W = ATTN_W + 2 * KV_W + POOL_W + 2 * CONV_W
WINDOW = 128
BLOCK = 128
D_FF = 4 * D_MODEL
ROPE_BASE = 10000.0
EPS = 1e-6
NEG = -1e30

kernel_name = 'hybrid_pool_swa_conformer_flow_step'

def rms_norm(x, g):
    xf = x.astype(jnp.float32)
    y = xf * lax.rsqrt(jnp.mean(xf * xf, axis=-1, keepdims=True) + EPS)
    return (y * g.astype(jnp.float32)).astype(x.dtype)

def layer_norm(x, g, b):
    xf = x.astype(jnp.float32)
    mu = jnp.mean(xf, axis=-1, keepdims=True)
    var = jnp.mean(jnp.square(xf - mu), axis=-1, keepdims=True)
    y = (xf - mu) * lax.rsqrt(var + EPS)
    return (y * g.astype(jnp.float32) + b.astype(jnp.float32)).astype(x.dtype)

def rope_2d(x, rows):
    half = HEAD_DIM // 2
    quarter = half // 2
    inv_freq = 1.0 / (ROPE_BASE ** (jnp.arange(quarter, dtype=jnp.float32) / quarter))
    row_pos = jnp.repeat(jnp.arange(rows, dtype=jnp.float32), GRID_W)
    col_pos = jnp.tile(jnp.arange(GRID_W, dtype=jnp.float32), rows)

    def rotate(u, pos):
        ang = pos[:, None] * inv_freq[None, :]
        cos = jnp.cos(ang)[None, :, None, :]
        sin = jnp.sin(ang)[None, :, None, :]
        u1, u2 = u[..., :quarter], u[..., quarter:]
        return jnp.concatenate([u1 * cos - u2 * sin, u2 * cos + u1 * sin], axis=-1)

    xf = x.astype(jnp.float32)
    out = jnp.concatenate([rotate(xf[..., :half], row_pos), rotate(xf[..., half:], col_pos)], axis=-1)
    return out.astype(x.dtype)

def sink_softmax(s, sink_b):
    sk = jnp.broadcast_to(sink_b.astype(jnp.float32), s.shape[:-1] + (1,))
    return jax.nn.softmax(jnp.concatenate([s, sk], axis=-1), axis=-1)[..., :-1]

def ctx_attention(q, k, v, sink):
    B, S = q.shape[0], q.shape[1]
    qg = q.reshape(B, S, N_KV_HEADS, GQA_GROUP, HEAD_DIM)
    s = jnp.einsum('bqkgd,bpkd->bkgqp', qg, k).astype(jnp.float32) * (HEAD_DIM ** -0.5)
    p = sink_softmax(s, sink.reshape(1, N_KV_HEADS, GQA_GROUP, 1, 1))
    o = jnp.einsum('bkgqp,bpkd->bqkgd', p.astype(v.dtype), v)
    return o.reshape(B, S, ATTN_W)

def latent_attention(q, k, v, ck, cv, sink):
    B, T = q.shape[0], q.shape[1]
    nb = T // BLOCK
    qb = q.reshape(B, nb, BLOCK, N_KV_HEADS, GQA_GROUP, HEAD_DIM)
    pad = ((0, 0), (BLOCK, BLOCK), (0, 0), (0, 0))
    kp = jnp.pad(k, pad).reshape(B, nb + 2, BLOCK, N_KV_HEADS, HEAD_DIM)
    vp = jnp.pad(v, pad).reshape(B, nb + 2, BLOCK, N_KV_HEADS, HEAD_DIM)
    kw = jnp.concatenate([kp[:, :-2], kp[:, 1:-1], kp[:, 2:]], axis=2)
    vw = jnp.concatenate([vp[:, :-2], vp[:, 1:-1], vp[:, 2:]], axis=2)
    qi = jnp.arange(BLOCK)
    kj = jnp.arange(3 * BLOCK)
    bi = jnp.arange(nb)
    rel = kj[None, :] - BLOCK - qi[:, None]
    kpos = bi[:, None] * BLOCK - BLOCK + kj[None, :]
    valid = (jnp.abs(rel) <= WINDOW)[None] & ((kpos >= 0) & (kpos < T))[:, None, :]
    scale = HEAD_DIM ** -0.5
    s_loc = jnp.einsum('bnqkgd,bnskd->bnkgqs', qb, kw).astype(jnp.float32) * scale
    s_loc = jnp.where(valid[None, :, None, None], s_loc, NEG)
    s_ctx = jnp.einsum('bnqkgd,bpkd->bnkgqp', qb, ck).astype(jnp.float32) * scale
    n_loc = 3 * BLOCK
    p = sink_softmax(jnp.concatenate([s_loc, s_ctx], axis=-1),
                     sink.reshape(1, 1, N_KV_HEADS, GQA_GROUP, 1, 1)).astype(v.dtype)
    o = (jnp.einsum('bnkgqs,bnskd->bnqkgd', p[..., :n_loc], vw)
         + jnp.einsum('bnkgqp,bpkd->bnqkgd', p[..., n_loc:], cv))
    return o.reshape(B, T, ATTN_W)

def pool_mixer(u, w_pool, pool_scale):
    B, S = u.shape[0], u.shape[1]
    uf = u.astype(jnp.float32).reshape(B, S, POOL_GROUPS, POOL_GW)
    cs = jnp.concatenate([jnp.zeros((B, 1, POOL_GROUPS, POOL_GW), jnp.float32),
                          lax.cumsum(uf, axis=1)], axis=1)
    t = jnp.arange(S)
    halfw = jnp.array([w // 2 for w in POOL_WINDOWS])
    wins = jnp.array(POOL_WINDOWS)
    lo = jnp.clip(t[:, None] - halfw[None, :], 0, S)
    hi = jnp.clip(t[:, None] - halfw[None, :] + wins[None, :], 0, S)
    gidx = jnp.arange(POOL_GROUPS)[None, :]
    wsum = cs[:, hi, gidx] - cs[:, lo, gidx]
    mean = wsum / (hi - lo).astype(jnp.float32)[None, :, :, None]
    pooled = (mean - uf).astype(u.dtype)
    y = jnp.einsum('bsgc,gcd->bsgd', pooled, w_pool).reshape(B, S, POOL_W)
    return y * pool_scale

def conv_mixer(u, conv_dw, conv_b, ln_g, ln_b, w_pw):
    a, g = jnp.split(u, 2, axis=-1)
    h = a * jax.nn.sigmoid(g)
    h = lax.conv_general_dilated(h, conv_dw[:, None, :], window_strides=(1,),
                                 padding=[(CONV_K // 2, CONV_K // 2)],
                                 dimension_numbers=('NWC', 'WIO', 'NWC'),
                                 feature_group_count=CONV_W) + conv_b
    h = jax.nn.silu(layer_norm(h, ln_g, ln_b))
    return h @ w_pw

def trunk_layer(x, cvec, ctx_kv, lp):
    mods = jnp.split(jax.nn.silu(cvec) @ lp['w_ada'] + lp['b_ada'], 6, axis=-1)
    sh1, sc1, g1, sh2, sc2, g2 = [m[:, None, :] for m in mods]
    B, S = x.shape[0], x.shape[1]
    h = rms_norm(x, lp['g_pre1']) * (1.0 + sc1) + sh1
    z = h @ lp['w_in']
    o1 = ATTN_W
    o2 = o1 + KV_W
    o3 = o2 + KV_W
    o4 = o3 + POOL_W
    q = z[..., :o1].reshape(B, S, N_HEADS, HEAD_DIM)
    k = z[..., o1:o2].reshape(B, S, N_KV_HEADS, HEAD_DIM)
    v = z[..., o2:o3].reshape(B, S, N_KV_HEADS, HEAD_DIM)
    pu = z[..., o3:o4]
    cu = z[..., o4:]
    if ctx_kv is None:
        attn = ctx_attention(q, k, v, lp['sink'])
        kv_out = (k, v)
    else:
        rows = S // GRID_W
        attn = latent_attention(rope_2d(q, rows), rope_2d(k, rows), v, ctx_kv[0], ctx_kv[1], lp['sink'])
        kv_out = None
    pool = pool_mixer(pu, lp['w_pool'], lp['pool_scale'])
    conv = conv_mixer(cu, lp['conv_dw'], lp['conv_b'], lp['conv_ln_g'], lp['conv_ln_b'], lp['w_conv_pw'])
    mix = jnp.concatenate([attn, pool, conv], axis=-1) @ lp['w_out']
    x = x + g1 * rms_norm(mix, lp['g_post1'])
    h = rms_norm(x, lp['g_pre2']) * (1.0 + sc2) + sh2
    f = jnp.square(jax.nn.relu(h @ lp['w_mlp1'])) @ lp['w_mlp2']
    x = x + g2 * rms_norm(f, lp['g_post2'])
    return x, kv_out

def setup_inputs(seed: int = 0) -> dict:
    key = jax.random.key(seed)
    ks = jax.random.split(key, 24)

    def nrm(k, shape, scale):
        return jax.random.normal(k, shape, jnp.float32) * scale

    return {
        'x_prompt': nrm(ks[0], (BATCH, SEQ, D_MODEL), 1.0),
        'x_sample': nrm(ks[1], (DEC_BATCH, DEC_SEQ, D_MODEL), 1.0),
        'cache_k': nrm(ks[2], (DEC_BATCH, DEPTH, PAST_LEN, N_KV_HEADS, HEAD_DIM), 1.0),
        'cache_v': nrm(ks[3], (DEC_BATCH, DEPTH, PAST_LEN, N_KV_HEADS, HEAD_DIM), 1.0),
        'c': nrm(ks[4], (DEC_BATCH, D_MODEL), 1.0),
        'c_ctx': nrm(ks[5], (D_MODEL,), 1.0),
        'w_ada': nrm(ks[6], (DEPTH, D_MODEL, 6 * D_MODEL), D_MODEL ** -0.5),
        'b_ada': nrm(ks[7], (DEPTH, 6 * D_MODEL), 0.02),
        'g_pre1': 1.0 + nrm(ks[8], (DEPTH, D_MODEL), 0.02),
        'g_post1': 1.0 + nrm(ks[9], (DEPTH, D_MODEL), 0.02),
        'g_pre2': 1.0 + nrm(ks[10], (DEPTH, D_MODEL), 0.02),
        'g_post2': 1.0 + nrm(ks[11], (DEPTH, D_MODEL), 0.02),
        'w_in': nrm(ks[12], (DEPTH, D_MODEL, IN_W), D_MODEL ** -0.5),
        'sink': nrm(ks[13], (DEPTH, N_HEADS), 0.5),
        'w_pool': nrm(ks[14], (DEPTH, POOL_GROUPS, POOL_GW, POOL_GW), POOL_GW ** -0.5),
        'pool_scale': 1.0 + nrm(ks[15], (DEPTH, POOL_W), 0.1),
        'conv_dw': nrm(ks[16], (DEPTH, CONV_K, CONV_W), CONV_K ** -0.5),
        'conv_b': nrm(ks[17], (DEPTH, CONV_W), 0.02),
        'conv_ln_g': 1.0 + nrm(ks[18], (DEPTH, CONV_W), 0.02),
        'conv_ln_b': nrm(ks[19], (DEPTH, CONV_W), 0.02),
        'w_conv_pw': nrm(ks[20], (DEPTH, CONV_W, CONV_W), CONV_W ** -0.5),
        'w_out': nrm(ks[21], (DEPTH, MIX_W, D_MODEL), MIX_W ** -0.5),
        'w_mlp1': nrm(ks[22], (DEPTH, D_MODEL, D_FF), D_MODEL ** -0.5),
        'w_mlp2': nrm(ks[23], (DEPTH, D_FF, D_MODEL), D_FF ** -0.5),
    }

def reference(x_prompt, x_sample, cache_k, cache_v, c, c_ctx, w_ada, b_ada, g_pre1, g_post1,
              g_pre2, g_post2, w_in, sink, w_pool, pool_scale, conv_dw, conv_b, conv_ln_g,
              conv_ln_b, w_conv_pw, w_out, w_mlp1, w_mlp2):
    xp = x_prompt
    xs = x_sample
    cvec_ctx = c_ctx[None, :]
    new_ks = []
    new_vs = []
    for l in range(DEPTH):
        lp = {
            'w_ada': w_ada[l], 'b_ada': b_ada[l],
            'g_pre1': g_pre1[l], 'g_post1': g_post1[l], 'g_pre2': g_pre2[l], 'g_post2': g_post2[l],
            'w_in': w_in[l], 'sink': sink[l], 'w_pool': w_pool[l], 'pool_scale': pool_scale[l],
            'conv_dw': conv_dw[l], 'conv_b': conv_b[l], 'conv_ln_g': conv_ln_g[l],
            'conv_ln_b': conv_ln_b[l], 'w_conv_pw': w_conv_pw[l], 'w_out': w_out[l],
            'w_mlp1': w_mlp1[l], 'w_mlp2': w_mlp2[l],
        }
        xp, (k_l, v_l) = trunk_layer(xp, cvec_ctx, None, lp)
        new_ks.append(k_l)
        new_vs.append(v_l)
        xs, _ = trunk_layer(xs, c, (cache_k[:, l], cache_v[:, l]), lp)
    new_k = jnp.stack(new_ks, axis=1)
    new_v = jnp.stack(new_vs, axis=1)
    return (xp, xs, new_k, new_v)


_drawn_inputs = setup_inputs


def setup_inputs(seed=0):
    import zlib

    import numpy as np

    out = dict(_drawn_inputs(seed))
    spreads = {}
    factors = {'g_pre1': 2.946,
     'g_post1': 4.326,
     'g_pre2': 4.622,
     'g_post2': 4.843,
     'sink': 64.0,
     'conv_b': 7.116,
     'conv_ln_g': 8.0,
     'conv_ln_b': 8.0,
     'cache_k': 8.0,
     'cache_v': 8.0}
    for name, (base, spread) in spreads.items():
        noise = np.random.default_rng([zlib.crc32(name.encode()), seed]).standard_normal(out[name].shape)
        drawn = base * np.exp(spread * noise) if base else spread * noise
        out[name] = __import__('jax').numpy.asarray(drawn.astype(out[name].dtype))
    for name, factor in factors.items():
        out[name] = (out[name] * factor).astype(out[name].dtype)
    return out
```

```python
from contextlib import ExitStack

import concourse.bass as bass
from concourse import mybir

F32 = mybir.dt.float32
F32R = mybir.dt.float32r
ALU = mybir.AluOpType
ACT = mybir.ActivationFunctionType
AX_X = mybir.AxisListType.X

P = 128
D = 2048
DEPTH = 2
CTX, LAT = 128, 256
TOK = CTX + LAT
GROUPS = ((0, 0, CTX), (1, CTX, TOK))
DT = D // P
HD = 64
HEADS, KV_HEADS = 16, 4
IN_W = 3072
D_FF = 4 * D
TAPS = 31
POOL_WINDOWS = (2, 4, 8, 16)
EPS = 1e-6
SCALE = HD ** -0.5

Q0, K0, V0, PU0, CA0, CG0 = 0, 8, 10, 12, 16, 20

SLOTS = 4
UC = 256
CHUNK = 8
CHUNKS = D_FF // P // CHUNK

Q_IN, Q_OUT, Q_MLP = 0, 12, 20
Q_CHUNK = 8
Q_LAYER = Q_MLP + CHUNKS * Q_CHUNK
B_IN, B_OUT, B_MLP = 0, 12, 20
B_CHUNK = 12
B_LAYER = B_MLP + CHUNKS * B_CHUNK

ADA_BLOCKS = 6 * D // UC
SH1, SC1, G1, SH2, SC2, G2 = (DT * i for i in range(6))
ADA_START, ADA_CU, ADA_QKV, ADA_MIX, ADA_OUT = 0, 16, 20, 28, 40

C_HALF = TAPS // 2
CONV_PAD = C_HALF + CTX + 2 * C_HALF + LAT + C_HALF
CONV_LAT = CTX + 2 * C_HALF
CONV_OUT = CONV_LAT + LAT
P_HALF = max(POOL_WINDOWS) // 2
POOL_PAD = P_HALF + CTX + 2 * P_HALF + LAT + P_HALF
POOL_LAT = P_HALF + CTX + 2 * P_HALF

BANK_SUM, BANK_VAR, BANK_ADA, BANK_MOD = 4, 5, 6, 7

G_PRE1, G_POST1, G_PRE2, G_POST2 = 0, 16, 32, 48
POOL_S, CONV_B, LN_G, LN_B = 64, 68, 72, 76
ROWS_A = 80

STEPS = [(pair, what) for pair in range(HEADS // 2) for what in range(3)]


class Chain:

    def __init__(self, engine, sem):
        self.engine, self.sem, self.n = engine, sem, 0

    def mark(self, instruction):
        instruction.then_inc(self.sem, 1)
        self.n = self.n + 1
        return self.n

    def wait(self, mark):
        self.engine.wait_ge(self.sem, mark)

    def link(self, instruction):
        self.wait(self.mark(instruction))


def backbone(nc, x_prompt, x_sample, cache_k, cache_v, c, c_ctx, w_ada, b_ada, g_pre1, g_post1, g_pre2,
             g_post2, w_in, sink, w_pool, pool_scale, conv_dw, conv_b, conv_ln_g, conv_ln_b, w_conv_pw,
             w_out, w_mlp1, w_mlp2, rope_cos, rope_sin, pool_edge, y_prompt, y_sample, new_k, new_v):
    ctx = ExitStack()
    with ctx:
        def sem(name):
            return ctx.enter_context(nc.semaphore(name))

        base = -(-nc.sbuf_base // 32) * 32
        arena_bytes = nc.sbuf_bytes_remaining // 32 * 32 - 32
        ctx.enter_context(nc.sbuf_tensor("arena", [P, arena_bytes // 4], F32))
        top = [0]

        def at(name, shape, dt, offset):
            return nc.alloc_sbuf_tensor_at(name, [P, *shape], dt, offset=base + offset)

        def new(name, shape, dt=F32):
            size = 4
            for n in shape:
                size *= n
            t = at(name, shape, dt, top[0])
            top[0] += -(-size // 32) * 32
            assert top[0] <= arena_bytes, (name, top[0], arena_bytes)
            return t

        x = new("x", [DT, TOK])
        h_hi = new("h_hi", [DT, TOK], F32R)
        h_lo = new("h_lo", [DT, TOK], F32R)
        z_at = top[0]
        z = new("z", [24, TOK])
        t_at = top[0]
        full = new("full", [DT, TOK])
        hid_hi = at("hid_hi", [CHUNK, TOK], F32R, t_at)
        hid_lo = at("hid_lo", [CHUNK, TOK], F32R, t_at + 4 * CHUNK * TOK)
        raw = new("raw", [SLOTS, 4, UC])
        w_hi = new("w_hi", [SLOTS, 4, UC], F32R)
        w_lo = new("w_lo", [SLOTS, 4, UC], F32R)
        ada_raw = new("ada_raw", [SLOTS, 4, UC])
        ident = new("ident", [P])
        ones = new("ones", [P])
        sel = new("sel", [2])
        cond = new("cond", [DT, 32])
        mods = new("mods", [DEPTH, 6 * DT, 2])
        rstd = new("rstd", [TOK])
        ada_s = new("ada_s", [UC])
        pa = new("pa", [DEPTH, ROWS_A])
        pb = new("pb", [DEPTH, 6 * DT])
        pc = new("pc", [DEPTH, 4 * TAPS])
        coef = new("coef", [4, DT, 2])
        masks = new("masks", [2, P])
        sinks = new("sinks", [DEPTH, HEADS])
        nsinks = new("nsinks", [DEPTH, HEADS])
        row_max = new("row_max", [2, 2])
        nbias = new("nbias", [2, 2])
        sink_in = new("sink_in", [2, 2])
        sink_e = new("sink_e", [2, 2])
        row_sum = new("row_sum", [2, 2])
        rden = new("rden", [2, 2])

        def t_off(n):
            return t_at + 4 * n

        o_acc = 4 * CONV_PAD
        o_pw = o_acc + 4 * CONV_OUT
        glu = at("glu", [4, CONV_PAD], F32, t_off(0))
        conv = at("conv", [4, CONV_OUT], F32, t_off(o_acc))
        pw_w = at("pw_w", [4, 512], F32, t_off(o_pw))
        pool_w = at("pool_w", [4, P], F32, t_off(o_pw + 2048))
        edge = at("edge", [4, 2, 2, P_HALF], F32, t_off(o_pw + 2560))
        assert o_pw + 2560 + 128 <= DT * TOK
        pool_a = at("pool_a", [4, POOL_PAD], F32, t_off(0))
        rot = at("rot", [4, LAT], F32, t_off(0))
        prob = at("prob", [2, 2, TOK], F32, t_off(0))
        cos_t = at("cos_t", [LAT], F32, t_off(o_acc))
        sin_t = at("sin_t", [LAT], F32, t_off(o_acc + 256))
        ck = at("ck", [256], F32, t_off(o_acc + 512))
        k_out = at("k_out", [256], F32, t_off(o_acc + 768))
        prob_t = at("prob_t", [2, 3, 256], F32, t_off(o_acc + 1024))
        kd = at("kd", [KV_HEADS, 512], F32, z_at + 4 * CA0 * TOK)
        vt = at("vt", [4, 256], F32, z_at + 4 * (CA0 * TOK + 2048))
        pool_b = at("pool_b", [2 * TOK], F32, z_at + 4 * 22 * TOK)
        staged = at("staged", [3, D], F32, z_at)
        rows = at("rows", [6, P], F32, z_at + 4 * 16 * TOK)
        cond_t = at("cond_t", [2, 2 * DT], F32, z_at + 4 * 18 * TOK)

        ps = ctx.enter_context(nc.psum_tensor("ps", [P, 8, 512], F32))

        def sems(names):
            return [sem(n) for n in names.split()]

        raw_landed = [sem(f"raw_landed{s}") for s in range(SLOTS)]
        ada_landed = [sem(f"ada_landed{s}") for s in range(SLOTS)]
        hi_ready, lo_ready, unit_used, acc_free = sems("hi_ready lo_ready unit_used acc_free")
        ada_used, ada_copied, ada_turned, mods_ready = sems("ada_used ada_copied ada_turned mods_ready")
        rows_landed, sinks_landed, x_landed, consts_ready = sems("rows_landed sinks_landed x_landed consts_ready")
        rows_turned, cond_raw, cond_sig, cond_ready, x_turned, x_copied = sems(
            "rows_turned cond_raw cond_sig cond_ready x_turned x_copied")
        sq_ready, sq_used, var_ready, std_ready = sems("sq_ready sq_used var_ready std_ready")
        x_updated, full_ready, h_hi_ready, h_ready = sems("x_updated full_ready h_hi_ready h_ready")
        conv_w_landed, pads_ready, sig_ready, conv_ready, ln_sum, cen_ready, csq_ready, csq_used = sems(
            "conv_w_landed pads_ready sig_ready conv_ready ln_sum cen_ready csq_ready csq_used")
        lnv_ready, lnstd_ready, ln_ready, silu_sig, conv_act, pw_ready, pw_hi, pw_done = sems(
            "lnv_ready lnstd_ready ln_ready silu_sig conv_act pw_ready pw_hi pw_done")
        pool_summed, pooled, pool_mm, pool_hi, pool_done = sems("pool_summed pooled pool_mm pool_hi pool_done")
        rope_landed, cachev_landed, kv_turned, v_ready, ck_turned, kd_ready, kv_out = sems(
            "rope_landed cachev_landed kv_turned v_ready ck_turned kd_ready kv_out")
        s_ready, nb_ready, p_ready, rden_ready, pn_ready, t_ready, pt_ready, o_ready, o_hi, o_done = sems(
            "s_ready nb_ready p_ready rden_ready pn_ready t_ready pt_ready o_ready o_hi o_done")
        sqh_ready, hidh_ready, hid_ready, added = sems("sqh_ready hidh_ready hid_ready added")
        y_turned, y_copied, y_stored = sems("y_turned y_copied y_stored")
        dve_chain, act_chain, pool_chain = sems("dve_chain act_chain pool_chain")

        def quad(layer, phase):
            return layer * Q_LAYER + phase

        def blk(layer, phase):
            return layer * B_LAYER + phase

        def per_token(t, n, lo=0, hi=TOK):
            return t[:, lo:hi].unsqueeze(1).to_broadcast([P, n, hi - lo])

        block = ctx.enter_context(nc.Block())

        @block.sync
        def _(sp):
            def load_unit(j, q, src, wait=True):
                if wait:
                    sp.wait_ge(lo_ready, 4 * q + j - 3)
                sp.dma_start(raw[:, j % 4, :, :], src).then_inc(raw_landed[j % 4], 16)

            def load_ada(layer, m, j, wait=True):
                n = layer * ADA_BLOCKS + m
                if wait:
                    sp.wait_ge(ada_used, 4 * n + j - 3)
                src = w_ada[layer, 512 * j:512 * j + 512, bass.ds(m * UC, UC)]
                sp.dma_start(ada_raw[:, j, :, :], src.rearrange("(k p) n -> p k n", p=P)).then_inc(ada_landed[j], 16)

            def part(w, layer, row, col):
                return w[layer, bass.ds(row, 512), bass.ds(col, UC)].rearrange("(k p) n -> p k n", p=P)

            def load_blocks(layer, w, q, col, ada):
                for j in range(8):
                    load_unit(j, q, part(w, layer, 512 * (j % 4), col + UC * (j // 4)))
                    if ada is not None:
                        load_ada(ada[0], ada[1] + j // 4, j % 4)

            sp.dma_start(staged[:, 0, :], x_prompt[0, :, :]).then_inc(x_landed, 16)
            sp.dma_start(staged[:, 1:3, :], x_sample[0, :, :].rearrange("(b p) n -> p b n", p=P)).then_inc(x_landed, 16)
            for j in range(4):
                load_ada(0, 0, j, wait=False)
            for j in range(4):
                load_unit(j, 0, part(w_in, 0, 512 * j, CA0 * P), wait=False)
            with sp.Fori(1, ADA_CU) as m:
                for j in range(4):
                    load_ada(0, m, j)
            for layer in range(DEPTH):
                first = layer == 0
                if first:
                    for j in range(4):
                        load_ada(0, ADA_CU, j)
                    for j in range(4, 8):
                        load_unit(j, 0, part(w_in, 0, 512 * (j - 4), CA0 * P + UC))
                        load_ada(0, ADA_CU + 1, j - 4)
                    load_blocks(0, w_in, 2, CA0 * P + 2 * UC, (0, ADA_CU + 2))
                else:
                    with sp.Fori(0, 2) as i:
                        load_blocks(layer, w_in, quad(layer, Q_IN) + i * 2, CA0 * P + i * 2 * UC, None)
                with sp.Fori(0, 4) as i:
                    load_blocks(layer, w_in, quad(layer, Q_IN + 4) + i * 2, i * 2 * UC,
                                (0, ADA_QKV + i * 2) if first else None)
                if first:
                    for j in range(4):
                        load_unit(j, Q_OUT, part(w_out, 0, 512 * j, 0))
                    with sp.Fori(ADA_MIX, ADA_OUT) as m:
                        for j in range(4):
                            load_ada(0, m, j)
                    for j in range(4):
                        load_ada(0, ADA_OUT, j)
                    for j in range(4, 8):
                        load_unit(j, Q_OUT, part(w_out, 0, 512 * (j - 4), UC))
                        load_ada(0, ADA_OUT + 1, j - 4)
                    with sp.Fori(1, 4) as i:
                        load_blocks(0, w_out, Q_OUT + i * 2, i * 2 * UC, (0, ADA_OUT + i * 2))
                else:
                    with sp.Fori(0, 4) as i:
                        load_blocks(layer, w_out, quad(layer, Q_OUT) + i * 2, i * 2 * UC, None)
                with sp.Fori(0, CHUNKS) as ch:
                    q = quad(layer, Q_MLP) + ch * Q_CHUNK
                    with sp.Fori(0, 2) as i:
                        load_blocks(layer, w_mlp1, q + i * 2, ch * (CHUNK * P) + i * (2 * UC),
                                    (1, ch * 6 + i * 2) if first else None)
                    with sp.Fori(0, 2) as i:
                        for j in range(8):
                            load_unit(j, q + 4 + i * 2, part(w_mlp2, layer, ch * (CHUNK * P) + 512 * (j % 2),
                                                             i * (4 * UC) + UC * (j // 2)))
                            if first and j < 4:
                                load_ada(1, ch * 6 + 4 + i, j)
            outs = [y_prompt[0, :, :], y_sample[0, 0:P, :], y_sample[0, P:2 * P, :]]
            for b in range(3):
                sp.wait_ge(y_copied, 4 * (b + 1))
                sp.dma_start(outs[b], staged[:, b, :]).then_inc(y_stored, 16)
            sp.wait_ge(y_stored, 48)

        @block.gpsimd
        def _(pool):
            chain = Chain(pool, pool_chain)

            def tiles(w):
                return w.rearrange("(t p) -> t p", p=P)

            for layer in range(DEPTH):
                a = 3 * layer
                for r, n, w in ((0, 16, g_pre1), (16, 16, g_post1), (32, 16, g_pre2), (48, 16, g_post2),
                                (64, 4, pool_scale), (68, 4, conv_b), (72, 4, conv_ln_g), (76, 4, conv_ln_b)):
                    pool.dma_start(rows[r:r + n, a, :], tiles(w[layer])).then_inc(rows_landed, 16)
                pool.dma_start(rows[0:96, a + 1, :], tiles(b_ada[layer])).then_inc(rows_landed, 16)
                pool.dma_start(rows[0:124, a + 2, :], conv_dw[layer].rearrange("k (t p) -> (k t) p", p=P)).then_inc(rows_landed, 16)
                for g, w in enumerate((c_ctx, c[0])):
                    pool.dma_start(rows[80 + 16 * g:96 + 16 * g, a, :], tiles(w)).then_inc(rows_landed, 16)
            pool.dma_start(sinks[:, :, :], sink.unsqueeze(0).to_broadcast([P, DEPTH, HEADS])).then_inc(sinks_landed, 16)

            nc.gpsimd.memset(ones[:, :], 1.0).then_inc(consts_ready, 1)
            nc.gpsimd.memset(cond[:, :, :], 0.0).then_inc(consts_ready, 1)
            chain.link(nc.gpsimd.memset(ident[:, :], 0.0))
            chain.link(nc.gpsimd.memset(sel[:, :], 0.0))
            chain.link(nc.gpsimd.memset(masks[:, :, :], 0.0))
            nc.gpsimd.affine_select(out=ident[:, :], in_=ident[:, :], compare_op=ALU.not_equal, fill=1.0, base=0,
                                    pattern=[[-1, P]], channel_multiplier=1).then_inc(consts_ready, 1)
            for i in range(4):
                chain.link(nc.gpsimd.affine_select(out=sel[:, :], in_=sel[:, :], compare_op=ALU.not_equal, fill=1.0,
                                                   base=-32 * i, pattern=[[-1, 2]], channel_multiplier=1))
            for i in range(2):
                nc.gpsimd.affine_select(out=masks[:, i, :], in_=masks[:, i, :], compare_op=ALU.is_ge,
                                        fill=-1e30 / SCALE, base=0, pattern=[[2 * i - 1, P]],
                                        channel_multiplier=1 - 2 * i).then_inc(consts_ready, 1)
            nc.gpsimd.memset(rden[:, 0, 0:1], 0.0).then_inc(sqh_ready, 1)
            nc.gpsimd.memset(rden[:, 0, 1:2], 0.0).then_inc(hid_ready, 1)
            nc.gpsimd.memset(rden[:, 1, 0:1], 0.0).then_inc(added, 1)
            nc.gpsimd.memset(rden[:, 1, 1:2], 0.0).then_inc(added, 1)

            for layer in range(DEPTH):
                pool.wait_ge(h_ready, (2 * layer + 1) * 8)
                pool.dma_start(pw_w[:, :, :], w_conv_pw[layer].rearrange("(k p) n -> p k n", p=P)).then_inc(conv_w_landed, 16)
                pool.dma_start(pool_w[:, :, :], w_pool[layer].rearrange("g c d -> c g d")).then_inc(conv_w_landed, 16)
                pool.dma_start(edge[:, :, :, :], pool_edge.unsqueeze(0).to_broadcast([P, 4, 2, 2, P_HALF])).then_inc(conv_w_landed, 16)
                nc.gpsimd.memset(glu[:, :, 0:C_HALF], 0.0).then_inc(pads_ready, 1)
                nc.gpsimd.memset(glu[:, :, C_HALF + CTX:C_HALF + CONV_LAT], 0.0).then_inc(pads_ready, 1)
                nc.gpsimd.memset(glu[:, :, C_HALF + CONV_OUT:CONV_PAD], 0.0).then_inc(pads_ready, 1)
                pool.wait_ge(conv_ready, layer + 1)
                nc.gpsimd.memset(pool_a[:, :, 0:P_HALF], 0.0)
                nc.gpsimd.memset(pool_a[:, :, P_HALF + CTX:POOL_LAT], 0.0)
                nc.gpsimd.memset(pool_a[:, :, POOL_LAT + LAT:POOL_PAD], 0.0)
                pool.wait_ge(acc_free, blk(layer, B_OUT))
                nc.gpsimd.tensor_copy(pool_a[:, :, P_HALF:P_HALF + CTX], z[:, PU0:PU0 + 4, 0:CTX])
                chain.link(nc.gpsimd.tensor_copy(pool_a[:, :, POOL_LAT:POOL_LAT + LAT], z[:, PU0:PU0 + 4, CTX:TOK]))
                pool.wait_ge(conv_w_landed, 48 * (layer + 1))
                for g, w in enumerate(POOL_WINDOWS):
                    here, there, span = pool_a[:, g, :], pool_b[:, 0:POOL_PAD], 1
                    while span < w:
                        n = POOL_PAD - 2 * span + 1
                        chain.link(nc.gpsimd.tensor_tensor(there[:, 0:n], here[:, 0:n], here[:, span:span + n], ALU.add))
                        here, there, span = there, here, 2 * span
                    if g % 2 == 0:
                        chain.link(nc.gpsimd.tensor_copy(pool_a[:, g, 0:n], pool_b[:, 0:n]))
                    for s, (start, length) in enumerate(((P_HALF, CTX), (POOL_LAT, LAT))):
                        for e, off in enumerate((0, length - P_HALF)):
                            a = start + off - w // 2
                            chain.link(nc.gpsimd.tensor_tensor(pool_a[:, g, a:a + P_HALF], pool_a[:, g, a:a + P_HALF],
                                                               edge[:, g, s, e, :], ALU.mult))
                nc.gpsimd.memset(pool_b[:, 0:1], 0.0).then_inc(pool_summed, 1)
                pool.wait_ge(cen_ready, layer + 1)
                pool.dma_start(cos_t[:, :], rope_cos).then_inc(rope_landed, 16)
                pool.dma_start(sin_t[:, :], rope_sin).then_inc(rope_landed, 16)
                pool.dma_start(ck[:, :], cache_k[0, layer].rearrange("t h d -> t (h d)")).then_inc(rope_landed, 16)
                pool.wait_ge(pw_ready, layer + 1)
                pool.dma_start(vt[:, 3, :], cache_v[0, layer].rearrange("t h d -> t (h d)")).then_inc(cachev_landed, 16)
                pool.wait_ge(v_ready, 2 * (layer + 1))
                pool.dma_start(new_k[0, layer].rearrange("t h d -> t (h d)"), k_out[:, :]).then_inc(kv_out, 16)
                pool.dma_start(new_v[0, layer].rearrange("t h d -> t (h d)"), vt[:, 0, :]).then_inc(kv_out, 16)
                pool.wait_ge(x_updated, (2 * layer + 1) * 8)
                chain.link(nc.gpsimd.memset(z[:, 0:16, :], 0.0))
                with pool.Fori(0, CHUNKS) as ch:
                    with pool.Fori(0, 4) as i:
                        hidden = layer * 32 + ch * 4 + i
                        pool.wait_ge(acc_free, blk(layer, B_MLP + 1) + ch * B_CHUNK + i)
                        pool.wait_ge(hid_ready, hidden + 1)
                        nc.gpsimd.tensor_tensor(z[:, 18:20, :], z[:, 16:18, :], z[:, 16:18, :], ALU.mult).then_inc(sqh_ready, 1)
                    with pool.Fori(0, 4) as i:
                        for e in range(2):
                            pool.wait_ge(acc_free, blk(layer, B_MLP + 5 + e) + ch * B_CHUNK + i * 2)
                            dst = z[:, bass.ds(i * 4 + 2 * e, 2), :]
                            nc.gpsimd.tensor_tensor(dst, dst, z[:, 20 + 2 * e:22 + 2 * e, :], ALU.add).then_inc(added, 1)
                pool.wait_ge(added, 64 * (layer + 1) + 2)

        @block.scalar
        def _(act):
            chain = Chain(act, act_chain)

            def w_high(j, q):
                act.wait_ge(raw_landed[j % 4], 16 * (q + (j // 4 + 1)))
                nc.scalar.activation(w_hi[:, j % 4, :, :], raw[:, j % 4, :, :], ACT.Copy).then_inc(hi_ready, 1)

            def eight_units(q, evict, prefetch=8):
                for j in range(8):
                    act.wait_ge(unit_used, 4 * q + (j + 1))
                    if j in evict:
                        evict[j]()
                    if j < prefetch:
                        w_high(j, q + 1)

            def copy_out(pair, tile):
                nc.scalar.activation(z[:, bass.ds(tile, 2), :], ps[:, 2 * pair:2 * pair + 2, 0:TOK], ACT.Copy).then_inc(acc_free, 1)

            def two_out(tile):
                return {3: lambda: copy_out(0, tile), 7: lambda: copy_out(1, tile + 2)}

            def squares(n, src, ready):
                for i in range(8):
                    ready(i)
                    if n or i >= 2:
                        act.wait_ge(sq_used, max(8 * n, 8 * n + i - 1))
                    nc.scalar.activation(z[:, 20 + 2 * (i % 2):22 + 2 * (i % 2), :], src[:, 2 * i:2 * i + 2, :],
                                         ACT.Square).then_inc(sq_ready, 1)

            def root(n):
                act.wait_ge(var_ready, n + 1)
                nc.scalar.activation(rstd[:, :], rstd[:, :], ACT.Sqrt).then_inc(std_ready, 1)

            def h_high(m):
                for i in range(8):
                    act.wait_ge(full_ready, 8 * m + i + 1)
                    nc.scalar.activation(h_hi[:, 2 * i:2 * i + 2, :], full[:, 2 * i:2 * i + 2, :], ACT.Copy).then_inc(h_hi_ready, 1)

            act.wait_ge(cond_raw, 1)
            nc.scalar.activation(cond_t[:, 1, :], cond_t[:, 0, :], ACT.Sigmoid).then_inc(cond_sig, 1)
            for g in range(12):
                b, j = divmod(g, 4)
                act.wait_ge(x_turned, g + 1)
                nc.scalar.activation(x[:, 4 * j:4 * j + 4, P * b:P * b + P],
                                     ps[:, 2 + g % 2, :].rearrange("p (t n) -> p t n", n=P), ACT.Copy).then_inc(x_copied, 1)
            for j in range(4):
                w_high(j, 0)

            for layer in range(DEPTH):
                if layer == 0:
                    squares(0, x, lambda i: act.wait_ge(x_copied, 12))
                else:
                    squares(4 * layer, x, lambda i: act.wait_ge(x_updated, 8 * (2 * layer - 1) + i + 1))
                root(4 * layer)
                h_high(2 * layer)
                with act.Fori(0, 2) as i:
                    eight_units(quad(layer, Q_IN) + i * 2, two_out(i * 4 + CA0))
                act.wait_ge(acc_free, blk(layer, 4))
                nc.scalar.activation(z[:, CG0:CG0 + 4, :], z[:, CG0:CG0 + 4, :], ACT.Sigmoid).then_inc(sig_ready, 1)
                with act.Fori(0, 4) as i:
                    eight_units(quad(layer, Q_IN + 4) + i * 2, two_out(i * 4))
                act.wait_ge(cen_ready, layer + 1)
                for t in range(4):
                    if t >= 2:
                        act.wait_ge(csq_used, 4 * layer + t - 1)
                    nc.scalar.activation(z[:, 20 + t % 2, :], z[:, CA0 + t, :], ACT.Square).then_inc(csq_ready, 1)
                act.wait_ge(pool_mm, layer + 1)
                for g in range(4):
                    nc.scalar.activation(h_hi[:, 8 + g, :], ps[:, g, 0:TOK], ACT.Copy,
                                         scale=pa[:, layer, POOL_S + g:POOL_S + g + 1]).then_inc(pool_hi, 1)
                act.wait_ge(lnv_ready, layer + 1)
                nc.scalar.activation(rstd[:, :], rstd[:, :], ACT.Sqrt).then_inc(lnstd_ready, 1)
                act.wait_ge(ln_ready, layer + 1)
                act.wait_ge(pool_summed, layer + 1)
                nc.scalar.activation(z[:, CG0:CG0 + 4, :], z[:, CA0:CA0 + 4, :], ACT.Sigmoid).then_inc(silu_sig, 1)
                act.wait_ge(pw_ready, layer + 1)
                nc.scalar.activation(h_hi[:, 12:16, :], ps[:, 0:4, 0:TOK], ACT.Copy).then_inc(pw_hi, 1)
                act.wait_ge(kv_turned, layer + 1)
                nc.scalar.activation(vt[:, 0:2, :], ps[:, 4, :].rearrange("p (b n) -> p b n", n=256), ACT.Copy)
                nc.scalar.activation(vt[:, 2, :], ps[:, 5, 0:256], ACT.Copy).then_inc(v_ready, 1)
                nc.scalar.activation(k_out[:, :], ps[:, 5, 256:512], ACT.Copy).then_inc(v_ready, 1)

                def exps(s):
                    pair, what = STEPS[s]
                    n, k, done = (TOK if what else CTX), s % 2, layer * len(STEPS)
                    act.wait_ge(nb_ready, done + s + 1)
                    if done + s >= 2:
                        act.wait_ge(t_ready, done + s - 1)
                    for e in range(2):
                        nc.scalar.activation(prob[:, k, e, 0:n], ps[:, 2 * k + e, 0:n], ACT.Exp, bias=nbias[:, k, e:e + 1],
                                             scale=SCALE, accum_out=row_sum[:, k, e:e + 1])
                    nc.scalar.activation(sink_e[:, k, :], sink_in[:, k, :], ACT.Exp).then_inc(p_ready, 1)

                def normalise(s):
                    n, k, done = (TOK if STEPS[s][1] else CTX), s % 2, layer * len(STEPS)
                    act.wait_ge(rden_ready, done + s + 1)
                    for e in range(2):
                        last = nc.scalar.activation(prob[:, k, e, 0:n], prob[:, k, e, 0:n], ACT.Copy, scale=rden[:, k, e:e + 1])
                    last.then_inc(pn_ready, 1)

                def out_high(s):
                    pair, what = STEPS[s]
                    act.wait_ge(o_ready, layer * len(STEPS) + s + 1)
                    nc.scalar.activation(h_hi[:, pair, P * what:P * what + P], ps[:, 5, 256:384], ACT.Copy).then_inc(o_hi, 1)

                for s in range(len(STEPS) + 1):
                    if s:
                        normalise(s - 1)
                    if s < len(STEPS):
                        exps(s)
                    if s:
                        out_high(s - 1)

                with act.Fori(0, 4) as i:
                    eight_units(quad(layer, Q_OUT) + i * 2, two_out(i * 4))
                act.wait_ge(kv_out, 32 * (layer + 1))
                squares(4 * layer + 1, z, lambda i: act.wait_ge(acc_free, blk(layer, B_OUT) + i + 1))
                root(4 * layer + 1)
                squares(4 * layer + 2, x, lambda i: act.wait_ge(x_updated, 8 * (2 * layer) + i + 1))
                root(4 * layer + 2)
                h_high(2 * layer + 1)

                def relu_out(pair, tile, ch, b):
                    hidden = ch * 4 + b
                    act.wait_ge(sqh_ready, hidden + (32 * layer + 1))
                    nc.scalar.activation(z[:, 16:18, :], ps[:, 2 * pair:2 * pair + 2, 0:TOK], ACT.Relu).then_inc(acc_free, 1)
                    act.wait_ge(acc_free, blk(layer, B_MLP + 1) + ch * B_CHUNK + b)
                    nc.scalar.activation(hid_hi[:, bass.ds(tile, 2), :], z[:, 16:18, :], ACT.Square).then_inc(hidh_ready, 1)

                def sum_out(pair, n):
                    act.wait_ge(added, n + 1)
                    nc.scalar.activation(z[:, 20 + 2 * pair:22 + 2 * pair, :], ps[:, 2 * pair:2 * pair + 2, 0:TOK],
                                         ACT.Copy).then_inc(acc_free, 1)

                def up(ch, q):
                    with act.Fori(0, 2) as i:
                        eight_units(q + i * 2, {3: lambda: relu_out(0, i * 4, ch, i * 2),
                                                7: lambda: relu_out(1, i * 4 + 2, ch, i * 2 + 1)})

                def down(ch, q, i, prefetch=8):
                    n = 64 * layer + ch * 8 + i * 4
                    eight_units(q + 4 + i * 2, {2 * k + 1: (lambda k=k: sum_out(k % 2, n + k)) for k in range(4)}, prefetch)

                last = layer == DEPTH - 1
                with act.Fori(0, CHUNKS - 1 if last else CHUNKS) as ch:
                    q = quad(layer, Q_MLP) + ch * Q_CHUNK
                    up(ch, q)
                    with act.Fori(0, 2) as i:
                        down(ch, q, i)
                if last:
                    ch, q = CHUNKS - 1, quad(layer, Q_MLP) + (CHUNKS - 1) * Q_CHUNK
                    up(ch, q)
                    down(ch, q, 0)
                    down(ch, q, 1, prefetch=4)
                squares(4 * layer + 3, z, lambda i: act.wait_ge(added, 64 * (layer + 1) + 2))
                root(4 * layer + 3)
            for g in range(12):
                b, j = divmod(g, 4)
                act.wait_ge(y_turned, g + 1)
                nc.scalar.activation(staged[:, b, 512 * j:512 * j + 512], ps[:, g % 4, :], ACT.Copy).then_inc(y_copied, 1)

        @block.vector
        def _(dve):
            chain = Chain(dve, dve_chain)

            def w_low(j, q):
                dve.wait_ge(hi_ready, 4 * q + (j + 1))
                nc.vector.tensor_tensor(w_lo[:, j % 4, :, :], raw[:, j % 4, :, :], w_hi[:, j % 4, :, :].bitcast(F32),
                                        ALU.subtract).then_inc(lo_ready, 1)

            def ada_copy(n):
                dve.wait_ge(ada_used, 4 * n + 4)
                nc.vector.tensor_copy(ada_s[:, :], ps[:, BANK_ADA, 0:UC]).then_inc(ada_copied, 1)

            def ada_mods(layer, m, n):
                dve.wait_ge(ada_turned, n + 1)
                nc.vector.tensor_tensor(mods[:, layer, bass.ds(m * 2, 2), :],
                                        ps[:, BANK_MOD, 0:4].rearrange("p (t g) -> p t g", g=2),
                                        pb[:, layer, bass.ds(m * 2, 2)].unsqueeze(2).to_broadcast([P, 2, 2]),
                                        ALU.add).then_inc(mods_ready, 1)

            def eight_units(q, before=None, after=None, prefetch=8):
                for j in range(8):
                    for f in (before or {}).get(j, ()):
                        f()
                    if j < prefetch:
                        w_low(j, q + 1)
                    for f in (after or {}).get(j, ()):
                        f()

            def ada_pair(layer, m):
                n = layer * ADA_BLOCKS + m
                return ({3: [lambda: ada_copy(n)], 4: [lambda: ada_mods(layer, m, n)], 7: [lambda: ada_copy(n + 1)]},
                        {7: [lambda: ada_mods(layer, m + 1, n + 1)]})

            def inverse_root(n):
                dve.wait_ge(sq_used, 8 * (n + 1))
                nc.vector.tensor_scalar(rstd[:, :], ps[:, BANK_SUM, 0:TOK], 1.0 / D, EPS, ALU.mult, ALU.add).then_inc(var_ready, 1)
                dve.wait_ge(std_ready, n + 1)
                chain.link(nc.vector.reciprocal(rstd[:, :], rstd[:, :]))

            def residual(r, k):
                def normal(i):
                    t = z[:, 2 * i:2 * i + 2, :]
                    return chain.mark(nc.vector.tensor_tensor(t, t, per_token(rstd, 2), ALU.mult))

                marks = [normal(0)]
                for i in range(8):
                    if i < 7:
                        marks.append(normal(i + 1))
                    chain.wait(marks[i])
                    for t in (2 * i, 2 * i + 1):
                        for g, a, b in GROUPS:
                            last = nc.vector.scalar_tensor_tensor(out=x[:, t, a:b], in0=z[:, t, a:b], scalar=coef[:, k, t, g:g + 1],
                                                                  in1=x[:, t, a:b], op0=ALU.mult, op1=ALU.add)
                    last.then_inc(x_updated, 1)

            def build_h(m, layer, k, shift):
                def normal(i):
                    return chain.mark(nc.vector.tensor_tensor(full[:, 2 * i:2 * i + 2, :], x[:, 2 * i:2 * i + 2, :],
                                                              per_token(rstd, 2), ALU.mult))

                def low(i):
                    dve.wait_ge(h_hi_ready, 8 * m + i + 1)
                    nc.vector.tensor_tensor(h_lo[:, 2 * i:2 * i + 2, :], full[:, 2 * i:2 * i + 2, :],
                                            h_hi[:, 2 * i:2 * i + 2, :].bitcast(F32), ALU.subtract).then_inc(h_ready, 1)

                marks = [normal(0)]
                for i in range(8):
                    if i < 7:
                        marks.append(normal(i + 1))
                    chain.wait(marks[i])
                    for t in (2 * i, 2 * i + 1):
                        for g, a, b in GROUPS:
                            last = nc.vector.tensor_scalar(full[:, t, a:b], full[:, t, a:b], coef[:, k, t, g:g + 1],
                                                           mods[:, layer, shift + t, g:g + 1], ALU.mult, ALU.add)
                    last.then_inc(full_ready, 1)
                    if i:
                        low(i - 1)
                low(7)

            def gain(k, layer, g0):
                return pa[:, layer, g0:g0 + DT].unsqueeze(2).to_broadcast([P, DT, 2])

            def scale_coef(k, layer, sc, g0):
                chain.link(nc.vector.scalar_tensor_tensor(out=coef[:, k, :, :], in0=mods[:, layer, sc:sc + DT, :], scalar=1.0,
                                                          in1=gain(k, layer, g0), op0=ALU.add, op1=ALU.mult))

            def gate_coef(k, layer, g, g0):
                chain.link(nc.vector.tensor_tensor(coef[:, k, :, :], mods[:, layer, g:g + DT, :], gain(k, layer, g0), ALU.mult))

            dve.wait_ge(rows_turned, 1)
            nc.vector.tensor_copy(cond_t[:, 0, :], ps[:, 0, 80:112]).then_inc(cond_raw, 1)
            for layer in range(DEPTH):
                nc.vector.tensor_copy(pa[:, layer, :], ps[:, layer, 0:ROWS_A])
                nc.vector.tensor_copy(pb[:, layer, :], ps[:, layer, 128:224])
                chain.link(nc.vector.tensor_copy(pc[:, layer, :], ps[:, layer, 256:380]))
            dve.wait_ge(consts_ready, 5)
            dve.wait_ge(cond_sig, 1)
            for g in range(2):
                last = nc.vector.tensor_tensor(cond[:, :, g], cond_t[:, 0, DT * g:DT * g + DT], cond_t[:, 1, DT * g:DT * g + DT], ALU.mult)
            last.then_inc(cond_ready, 1)
            dve.wait_ge(sinks_landed, 16)
            chain.link(nc.vector.tensor_scalar(nsinks[:, :, :], sinks[:, :, :], -1.0, None, ALU.mult))
            for j in range(4):
                w_low(j, 0)
            with dve.Fori(0, ADA_CU) as m:
                ada_copy(m)
                ada_mods(0, m, m)

            for layer in range(DEPTH):
                first = layer == 0
                n_mods = ADA_BLOCKS * layer
                dve.wait_ge(mods_ready, n_mods + ADA_CU)
                scale_coef(0, layer, SC1, G_PRE1)
                inverse_root(4 * layer)
                build_h(2 * layer, layer, 0, SH1)
                with dve.Fori(0, 2) as i:
                    eight_units(quad(layer, Q_IN) + i * 2, *(ada_pair(0, i * 2 + ADA_CU) if first else ()))
                dve.wait_ge(sig_ready, layer + 1)
                dve.wait_ge(pads_ready, 3 * (layer + 1))
                chain.link(nc.vector.tensor_tensor(glu[:, :, C_HALF:C_HALF + CTX], z[:, CA0:CA0 + 4, 0:CTX], z[:, CG0:CG0 + 4, 0:CTX], ALU.mult))
                chain.link(nc.vector.tensor_tensor(glu[:, :, C_HALF + CONV_LAT:C_HALF + CONV_OUT], z[:, CA0:CA0 + 4, CTX:TOK],
                                                   z[:, CG0:CG0 + 4, CTX:TOK], ALU.mult))

                n0 = chain.n
                with dve.Fori(0, 4) as i:
                    chain.n = n0 + i * TAPS

                    def tap(k):
                        src, out = glu[:, bass.ds(i, 1), k:k + CONV_OUT], conv[:, bass.ds(i, 1), :]
                        w = pc[:, layer, bass.ds(i + 4 * k, 1)]
                        if k == 0:
                            chain.link(nc.vector.tensor_scalar(out, src, w, pa[:, layer, bass.ds(i + CONV_B, 1)], ALU.mult, ALU.add))
                        else:
                            chain.link(nc.vector.scalar_tensor_tensor(out=out, in0=src, scalar=w, in1=out, op0=ALU.mult, op1=ALU.add))

                    before, after = ada_pair(0, i * 2 + ADA_QKV) if first else ({}, {})
                    for j in range(8):
                        after[j] = [(lambda k=k: tap(k)) for k in range(4 * j, min(4 * j + 4, TAPS))] + list(after.get(j, []))
                    eight_units(quad(layer, Q_IN + 4) + i * 2, before, after)
                chain.n = n0 + 4 * TAPS
                nc.vector.memset(row_max[:, 0, :], 0.0).then_inc(conv_ready, 1)

                dve.wait_ge(ln_sum, layer + 1)
                chain.link(nc.vector.tensor_scalar(rstd[:, :], ps[:, BANK_SUM, 0:TOK], 1.0 / 512, None, ALU.mult))
                nc.vector.tensor_tensor(z[:, CA0:CA0 + 4, 0:CTX], conv[:, :, 0:CTX], per_token(rstd, 4, 0, CTX), ALU.subtract)
                nc.vector.tensor_tensor(z[:, CA0:CA0 + 4, CTX:TOK], conv[:, :, CONV_LAT:CONV_OUT], per_token(rstd, 4, CTX, TOK),
                                        ALU.subtract).then_inc(cen_ready, 1)
                dve.wait_ge(pool_summed, layer + 1)
                for g, w in enumerate(POOL_WINDOWS):
                    for start, a, b in ((P_HALF, 0, CTX), (POOL_LAT, CTX, TOK)):
                        o = start - w // 2
                        last = nc.vector.scalar_tensor_tensor(out=z[:, PU0 + g, a:b], in0=pool_a[:, g, o:o + b - a], scalar=1.0 / w,
                                                              in1=z[:, PU0 + g, a:b], op0=ALU.mult, op1=ALU.subtract)
                last.then_inc(pooled, 1)
                dve.wait_ge(csq_used, 4 * (layer + 1))
                nc.vector.tensor_scalar(rstd[:, :], ps[:, BANK_VAR, 0:TOK], 1.0 / 512, EPS, ALU.mult, ALU.add).then_inc(lnv_ready, 1)
                dve.wait_ge(lnstd_ready, layer + 1)
                chain.link(nc.vector.reciprocal(rstd[:, :], rstd[:, :]))
                cs = z[:, CA0:CA0 + 4, :]
                chain.link(nc.vector.tensor_tensor(cs, cs, per_token(rstd, 4), ALU.mult))
                for t in range(4):
                    last = nc.vector.tensor_scalar(z[:, CA0 + t, :], z[:, CA0 + t, :], pa[:, layer, LN_G + t:LN_G + t + 1],
                                                   pa[:, layer, LN_B + t:LN_B + t + 1], ALU.mult, ALU.add)
                last.then_inc(ln_ready, 1)
                dve.wait_ge(silu_sig, layer + 1)
                nc.vector.tensor_tensor(cs, cs, z[:, CG0:CG0 + 4, :], ALU.mult).then_inc(conv_act, 1)
                dve.wait_ge(pool_hi, 4 * (layer + 1))
                for g in range(4):
                    last = nc.vector.scalar_tensor_tensor(out=h_lo[:, 8 + g, :], in0=ps[:, g, 0:TOK],
                                                          scalar=pa[:, layer, POOL_S + g:POOL_S + g + 1],
                                                          in1=h_hi[:, 8 + g, :].bitcast(F32), op0=ALU.mult, op1=ALU.subtract)
                last.then_inc(pool_done, 1)
                dve.wait_ge(rope_landed, 48 * (layer + 1))
                swap = [p ^ 16 for p in range(32)]
                for a, b in ((0, 4), (4, 8), (8, 10)):
                    zz, rr = z[:, a:b, CTX:TOK], rot[:, 0:b - a, :]
                    chain.link(nc.vector.stream_shuffle(rr, zz, swap))
                    nc.vector.tensor_tensor(rr, rr, per_token(sin_t, b - a, 0, LAT), ALU.mult)
                    chain.link(nc.vector.tensor_tensor(zz, zz, per_token(cos_t, b - a, 0, LAT), ALU.mult))
                    chain.link(nc.vector.tensor_tensor(zz, zz, rr, ALU.add))
                dve.wait_ge(pw_hi, layer + 1)
                nc.vector.tensor_tensor(h_lo[:, 12:16, :], ps[:, 0:4, 0:TOK], h_hi[:, 12:16, :].bitcast(F32), ALU.subtract).then_inc(pw_done, 1)
                kdv = kd[:, :, :].rearrange("p (t s) n -> p t s n", s=2)
                for a in range(2):
                    for b in range(2):
                        nc.vector.tensor_copy(kdv[64 * b:64 * b + 64, :, a, 0:TOK], z[64 * a:64 * a + 64, K0:K0 + 2, :])
                dve.wait_ge(ck_turned, layer + 1)
                for a in range(2):
                    for b in range(2):
                        last = nc.vector.tensor_copy(kdv[64 * b:64 * b + 64, :, a, TOK:512],
                                                     ps[64 * a:64 * a + 64, 0, 0:256].rearrange("p (t n) -> p t n", n=P))
                last.then_inc(kd_ready, 1)

                done = layer * len(STEPS)

                def stats(s):
                    pair, what = STEPS[s]
                    k = s % 2
                    dve.wait_ge(s_ready, done + s + 1)
                    n = TOK if what else CTX
                    if what:
                        m = ps[:, 2 * k:2 * k + 2, (P if what == 1 else 0):][:, :, 0:P]
                        chain.link(nc.vector.tensor_tensor(m, m, masks[:, what - 1, :].unsqueeze(1).to_broadcast([P, 2, P]), ALU.add))
                    chain.link(nc.vector.reduce_max(row_max[:, k, :], ps[:, 2 * k:2 * k + 2, 0:n], AX_X))
                    chain.link(nc.vector.scalar_tensor_tensor(out=nbias[:, k, :], in0=row_max[:, k, :], scalar=-SCALE,
                                                              in1=nsinks[:, layer, 2 * pair:2 * pair + 2], op0=ALU.mult, op1=ALU.min))
                    nc.vector.tensor_tensor(sink_in[:, k, :], nbias[:, k, :], sinks[:, layer, 2 * pair:2 * pair + 2], ALU.add).then_inc(nb_ready, 1)

                def denominator(s):
                    k = s % 2
                    dve.wait_ge(p_ready, done + s + 1)
                    chain.link(nc.vector.tensor_tensor(row_sum[:, k, :], row_sum[:, k, :], sink_e[:, k, :], ALU.add))
                    nc.vector.reciprocal(rden[:, k, :], row_sum[:, k, :]).then_inc(rden_ready, 1)

                def turned_out(s):
                    pair, what = STEPS[s]
                    dve.wait_ge(t_ready, done + s + 1)
                    if what:
                        nc.vector.tensor_copy(prob_t[:, s % 2, 0:2, :], ps[:, 4, :].rearrange("p (b n) -> p b n", n=256))
                        nc.vector.tensor_copy(prob_t[:, s % 2, 2, :], ps[:, 5, 0:256]).then_inc(pt_ready, 1)
                    else:
                        nc.vector.tensor_copy(prob_t[:, s % 2, 0, :], ps[:, 4, 0:256]).then_inc(pt_ready, 1)

                def out_low(s):
                    pair, what = STEPS[s]
                    dve.wait_ge(o_hi, done + s + 1)
                    cols = slice(P * what, P * what + P)
                    nc.vector.tensor_tensor(h_lo[:, pair, cols], ps[:, 5, 256:384], h_hi[:, pair, cols].bitcast(F32),
                                            ALU.subtract).then_inc(o_done, 1)

                for s in range(len(STEPS) + 1):
                    if s:
                        denominator(s - 1)
                    if s < len(STEPS):
                        stats(s)
                    if s:
                        turned_out(s - 1)
                    if first and s and s % 2 == 0:
                        ada_copy(ADA_MIX + s // 2 - 1)
                    if s:
                        out_low(s - 1)
                    if first and s and s % 2 == 0:
                        ada_mods(0, ADA_MIX + s // 2 - 1, ADA_MIX + s // 2 - 1)

                with dve.Fori(0, 4) as i:
                    eight_units(quad(layer, Q_OUT) + i * 2, *(ada_pair(0, i * 2 + ADA_OUT) if first else ()))
                dve.wait_ge(mods_ready, n_mods + ADA_BLOCKS)
                gate_coef(1, layer, G1, G_POST1)
                scale_coef(2, layer, SC2, G_PRE2)
                gate_coef(3, layer, G2, G_POST2)
                inverse_root(4 * layer + 1)
                residual(2 * layer, 1)
                inverse_root(4 * layer + 2)
                dve.wait_ge(x_updated, 8 * (2 * layer + 1))
                build_h(2 * layer + 1, layer, 2, SH2)

                def hidden_low(tile, n):
                    dve.wait_ge(hidh_ready, n + 1)
                    dve.wait_ge(sqh_ready, n + 2)
                    nc.vector.tensor_tensor(hid_lo[:, bass.ds(tile, 2), :], z[:, 18:20, :], hid_hi[:, bass.ds(tile, 2), :].bitcast(F32),
                                            ALU.subtract).then_inc(hid_ready, 1)

                def up(ch, q):
                    with dve.Fori(0, 2) as i:
                        before, after = ada_pair(1, ch * 6 + i * 2) if first else ({}, {})
                        n = ch * 4 + i * 2 + 32 * layer
                        after[3] = [lambda: hidden_low(i * 4, n)]
                        after[7] = [lambda: hidden_low(i * 4 + 2, n + 1)] + list(after.get(7, []))
                        eight_units(q + i * 2, before, after)

                def down(ch, q, i, prefetch=8):
                    m = ch * 6 + i + 4
                    n = m + ADA_BLOCKS
                    before = {4: [lambda: ada_copy(n)], 6: [lambda: ada_mods(1, m, n)]} if first else {}
                    eight_units(q + 4 + i * 2, before, {}, prefetch)

                last_layer = layer == DEPTH - 1
                with dve.Fori(0, CHUNKS - 1 if last_layer else CHUNKS) as ch:
                    q = quad(layer, Q_MLP) + ch * Q_CHUNK
                    up(ch, q)
                    with dve.Fori(0, 2) as i:
                        down(ch, q, i)
                if last_layer:
                    ch, q = CHUNKS - 1, quad(layer, Q_MLP) + (CHUNKS - 1) * Q_CHUNK
                    up(ch, q)
                    down(ch, q, 0)
                    down(ch, q, 1, prefetch=4)
                inverse_root(4 * layer + 3)
                residual(2 * layer + 1, 3)
                dve.wait_ge(x_updated, 8 * (2 * layer + 2))

        @block.tensor
        def _(pe):
            def unit(j, q, pair, kt, hi, lo, begin, end):
                pe.wait_ge(lo_ready, 4 * q + (j + 1))
                for k in range(4):
                    for t in range(2):
                        for i, (w, v) in enumerate(((w_hi, hi), (w_hi, lo), (w_lo, hi))):
                            last = nc.tensor.matmul(ps[:, 2 * pair + t, 0:TOK], w[:, j % 4, k, P * t:P * t + P], v[:, kt + k, :],
                                                    start=begin and k == 0 and i == 0, stop=end and k == 3 and i == 2)
                last.then_inc(unit_used, 1)

            def ada_unit(n, j):
                pe.wait_ge(ada_landed[j], 16 * (n + 1))
                if j == 0 and not (isinstance(n, int) and n == 0):
                    pe.wait_ge(ada_copied, n)
                for g in range(4):
                    last = nc.tensor.matmul(ps[32 * g:32 * g + 32, BANK_ADA, 0:UC], cond[:, 4 * j + g, :], ada_raw[:, j, g, :],
                                            start=j == 0, stop=j == 3)
                last.then_inc(ada_used, 1)

            def ada_turn(n):
                pe.wait_ge(ada_copied, n + 1)
                if not (isinstance(n, int) and n == 0):
                    pe.wait_ge(mods_ready, n)
                for t in range(2):
                    last = nc.tensor.matmul(ps[:, BANK_MOD, 2 * t:2 * t + 2], ada_s[:, P * t:P * t + P], sel[:, :],
                                            start=True, stop=True)
                last.then_inc(ada_turned, 1)

            def two_blocks(q, b, ada=None, h_base=None):
                for j in range(8):
                    if j % 4 == 0 and not (isinstance(b, int) and b + j // 4 <= 1):
                        pe.wait_ge(acc_free, b + (j // 4 - 1))
                    if h_base is not None and j < 4:
                        pe.wait_ge(h_ready, h_base + 2 * j + 2)
                    unit(j, q, j // 4, 4 * (j % 4), h_hi, h_lo, j % 4 == 0, j % 4 == 3)
                    if ada is not None:
                        if j == 3:
                            ada_turn(ada)
                        for n, u in {0: ((0, 0), (0, 1)), 1: ((0, 2),), 2: ((0, 3),), 3: ((1, 0),), 4: ((1, 1),),
                                     5: ((1, 2),), 6: ((1, 3),), 7: ()}[j]:
                            ada_unit(ada + n, u)
                        if j == 7:
                            ada_turn(ada + 1)

            def sum_pair(n, i):
                pe.wait_ge(sq_ready, 8 * n + i + 1)
                for t in range(2):
                    last = nc.tensor.matmul(ps[:, BANK_SUM, 0:TOK], ones[:, :], z[:, 20 + 2 * (i % 2) + t, :],
                                            start=i == 0 and t == 0, stop=i == 7 and t == 1)
                last.then_inc(sq_used, 1)

            def sum_squares(n):
                for i in range(8):
                    sum_pair(n, i)

            pe.wait_ge(consts_ready, 5)
            pe.wait_ge(rows_landed, 16 * 12 * DEPTH)
            for layer in range(DEPTH):
                for i, n in enumerate((112, 96, 124)):
                    last = nc.tensor.transpose(ps[:, layer, P * i:P * i + n], rows[0:n, 3 * layer + i, :], ident[0:n, 0:n])
            last.then_inc(rows_turned, 1)
            pe.wait_ge(x_landed, 32)
            for g in range(12):
                b, j = divmod(g, 4)
                if g >= 2:
                    pe.wait_ge(x_copied, g - 1)
                for t in range(4):
                    last = nc.tensor.transpose(ps[:, 2 + g % 2, P * t:P * t + P], staged[:, b, P * (4 * j + t):P * (4 * j + t + 1)], ident[:, :])
                last.then_inc(x_turned, 1)
            pe.wait_ge(cond_ready, 1)
            for m in range(8):
                for j in range(4):
                    ada_unit(m, j)
                sum_pair(0, m)
                ada_turn(m)
            with pe.Fori(8, ADA_CU) as m:
                for j in range(4):
                    ada_unit(m, j)
                ada_turn(m)

            for layer in range(DEPTH):
                first = layer == 0
                if first:
                    two_blocks(0, 0, ADA_CU, 0)
                    two_blocks(2, 2, ADA_CU + 2)
                else:
                    sum_squares(4 * layer)
                    with pe.Fori(0, 2) as i:
                        two_blocks(quad(layer, Q_IN) + i * 2, blk(layer, B_IN) + i * 2, None, 16 * layer)
                with pe.Fori(0, 4) as i:
                    two_blocks(quad(layer, Q_IN + 4) + i * 2, blk(layer, B_IN + 4) + i * 2, i * 2 + ADA_QKV if first else None)
                pe.wait_ge(conv_ready, layer + 1)
                for a, b, src in ((0, CTX, 0), (CTX, TOK, CONV_LAT)):
                    for t in range(4):
                        last = nc.tensor.matmul(ps[:, BANK_SUM, a:b], ones[:, :], conv[:, t, src:src + b - a], start=t == 0, stop=t == 3)
                last.then_inc(ln_sum, 1)
                for t in range(4):
                    pe.wait_ge(csq_ready, 4 * layer + t + 1)
                    nc.tensor.matmul(ps[:, BANK_VAR, 0:TOK], ones[:, :], z[:, 20 + t % 2, :], start=t == 0, stop=t == 3).then_inc(csq_used, 1)
                pe.wait_ge(pooled, layer + 1)
                pe.wait_ge(acc_free, blk(layer, B_OUT))
                for g in range(4):
                    last = nc.tensor.matmul(ps[:, g, 0:TOK], pool_w[:, g, :], z[:, PU0 + g, :], start=True, stop=True)
                last.then_inc(pool_mm, 1)
                pe.wait_ge(conv_act, layer + 1)
                pe.wait_ge(pool_done, layer + 1)
                pe.wait_ge(conv_w_landed, 48 * (layer + 1))
                for t in range(4):
                    for k in range(4):
                        last = nc.tensor.matmul(ps[:, t, 0:TOK], pw_w[:, k, P * t:P * t + P], z[:, CA0 + k, :], start=k == 0, stop=k == 3)
                last.then_inc(pw_ready, 1)
                pe.wait_ge(lnv_ready, layer + 1)
                for i in range(2):
                    for b in range(3):
                        nc.tensor.transpose(ps[:, 4 + b // 2, 256 * (b % 2) + P * i:256 * (b % 2) + P * i + P],
                                            z[:, V0 + i, P * b:P * b + P], ident[:, :])
                    last = nc.tensor.transpose(ps[:, 5, 256 + P * i:256 + P * i + P], z[:, K0 + i, 0:P], ident[:, :])
                last.then_inc(kv_turned, 1)
                pe.wait_ge(rope_landed, 48 * (layer + 1))
                pe.wait_ge(pw_done, layer + 1)
                for i in range(2):
                    last = nc.tensor.transpose(ps[:, 0, P * i:P * i + P], ck[:, P * i:P * i + P], ident[:, :])
                last.then_inc(ck_turned, 1)

                done = layer * len(STEPS)

                def scores(s):
                    pair, what = STEPS[s]
                    a, b = (TOK - LAT, 512) if what else (0, CTX)
                    if done + s >= 2:
                        pe.wait_ge(p_ready, done + s - 1)
                    for e in range(2):
                        half = slice(64 * e, 64 * e + 64)
                        last = nc.tensor.matmul(ps[:, 2 * (s % 2) + e, 0:b - a], z[half, pair, P * what:P * what + P],
                                                kd[half, pair // 2, a:b], start=True, stop=True)
                    last.then_inc(s_ready, 1)

                def turn(s):
                    pair, what = STEPS[s]
                    pe.wait_ge(pn_ready, done + s + 1)
                    if done + s >= 1:
                        pe.wait_ge(o_done, done + s)
                    for kb in range(3 if what else 1):
                        for e in range(2):
                            o = 256 * (kb % 2) + P * e
                            last = nc.tensor.transpose(ps[:, 4 + kb // 2, o:o + P], prob[:, s % 2, e, P * kb:P * kb + P], ident[:, :])
                    last.then_inc(t_ready, 1)

                def mix(s):
                    pair, what = STEPS[s]
                    kv = pair // 2
                    blocks = (1, 2, 3) if what else (0,)
                    pe.wait_ge(pt_ready, done + s + 1)
                    for e in range(2):
                        for i, vb in enumerate(blocks):
                            last = nc.tensor.matmul(ps[64 * e:64 * e + 64, 5, 256:384], vt[:, vb, HD * kv:HD * kv + HD],
                                                    prob_t[:, s % 2, i, P * e:P * e + P], start=i == 0, stop=i == len(blocks) - 1)
                    last.then_inc(o_ready, 1)

                pe.wait_ge(kd_ready, layer + 1)
                pe.wait_ge(v_ready, 2 * (layer + 1))
                pe.wait_ge(cachev_landed, 16 * (layer + 1))
                for s in range(len(STEPS) + 1):
                    if s < len(STEPS):
                        scores(s)
                    if s:
                        turn(s - 1)
                    if first and s and s % 2 == 0:
                        ada_turn(ADA_MIX + s // 2 - 1)
                    if first and s < len(STEPS):
                        for u in range(2):
                            ada_unit(ADA_MIX + s // 2, 2 * (s % 2) + u)
                    if s:
                        mix(s - 1)
                pe.wait_ge(o_done, done + len(STEPS))
                with pe.Fori(0, 4) as i:
                    two_blocks(quad(layer, Q_OUT) + i * 2, blk(layer, B_OUT) + i * 2, i * 2 + ADA_OUT if first else None)
                sum_squares(4 * layer + 1)
                sum_squares(4 * layer + 2)
                with pe.Fori(0, CHUNKS) as ch:
                    q, b = quad(layer, Q_MLP) + ch * Q_CHUNK, blk(layer, B_MLP) + ch * B_CHUNK
                    with pe.Fori(0, 2) as i:
                        two_blocks(q + i * 2, b + i * 2, ch * 6 + i * 2 + ADA_BLOCKS if first else None, 16 * layer + 8)
                    with pe.Fori(0, 2) as i:
                        n = ch * 6 + i + (4 + ADA_BLOCKS)
                        for j in range(8):
                            if j % 2 == 0:
                                pe.wait_ge(acc_free, b + i * 4 + (4 + j // 2 - 1))
                            if j < 2:
                                pe.wait_ge(hid_ready, ch * 4 + (32 * layer + 1 + 2 * (j + 1)))
                            unit(j, q + 4 + i * 2, j // 2 % 2, 4 * (j % 2), hid_hi, hid_lo, j % 2 == 0, j % 2 == 1)
                            if first and j < 4:
                                ada_unit(n, j)
                            if first and j == 5:
                                ada_turn(n)
                sum_squares(4 * layer + 3)
            pe.wait_ge(x_updated, 32)
            for g in range(12):
                b, j = divmod(g, 4)
                if g >= 4:
                    pe.wait_ge(y_copied, g - 3)
                for t in range(4):
                    last = nc.tensor.transpose(ps[:, g % 4, P * t:P * t + P], x[:, 4 * j + t, P * b:P * b + P], ident[:, :])
                last.then_inc(y_turned, 1)


_INS = ["x_prompt", "x_sample", "cache_k", "cache_v", "c", "c_ctx", "w_ada", "b_ada", "g_pre1", "g_post1", "g_pre2",
        "g_post2", "w_in", "sink", "w_pool", "pool_scale", "conv_dw", "conv_b", "conv_ln_g", "conv_ln_b", "w_conv_pw",
        "w_out", "w_mlp1", "w_mlp2"]
_OUTS = [(1, CTX, D), (1, LAT, D), (1, DEPTH, CTX, KV_HEADS, HD), (1, DEPTH, CTX, KV_HEADS, HD)]


def shape_tables():
    import numpy as np

    grid_w, quarter = 64, HD // 4
    inv_freq = (1.0 / (np.float32(10000.0) ** (np.arange(quarter, dtype=np.float32) / np.float32(quarter)))).astype(np.float32)
    token = np.arange(LAT)
    pos = np.stack([token // grid_w, token % grid_w]).astype(np.float32)
    cos, sin = np.empty((P, LAT), np.float32), np.empty((P, LAT), np.float32)
    for p in range(P):
        angle = pos[p % HD // (HD // 2)] * inv_freq[p % quarter]
        cos[p] = np.cos(angle)
        sin[p] = np.sin(angle) * (-1 if p % (2 * quarter) < quarter else 1)
    edge = np.ones((4, 2, 2, P_HALF), np.float32)
    for g, w in enumerate(POOL_WINDOWS):
        for s, length in enumerate((CTX, LAT)):
            for e, first in enumerate((0, length - P_HALF)):
                t = first + np.arange(P_HALF)
                edge[g, s, e] = w / (np.clip(t - w // 2 + w, 0, length) - np.clip(t - w // 2, 0, length))
    return {"rope_cos": cos, "rope_sin": sin, "pool_edge": edge}


def kernel(**inputs):
    import numpy as _np
    import concourse.bacc as _bacc
    from concourse import mybir as _mybir
    from concourse.bass_utils import run_bass_kernel_spmd as _run

    nc = _bacc.Bacc("TRN2", target_bir_lowering=False, num_devices=1)
    arrays, args = {}, []
    for name, a in [(n, inputs[n]) for n in _INS] + list(shape_tables().items()):
        a = _np.ascontiguousarray(a)
        arrays[f"in_{name}_dram"] = a
        args.append(nc.dram_tensor(f"in_{name}_dram", a.shape, _mybir.dt.from_np(a.dtype), kind="ExternalInput").ap())
    for i, shape in enumerate(_OUTS):
        args.append(nc.dram_tensor(f"out_{i}_dram", shape, _mybir.dt.float32, kind="ExternalOutput").ap())
    backbone(nc, *args)
    r = _run(nc, [arrays], core_ids=[0])
    return tuple(r.results[0][f"out_{i}_dram"] for i in range(len(_OUTS)))
```

```python
from contextlib import ExitStack

import concourse.bass as bass
from concourse import mybir

F32 = mybir.dt.float32
F32R = mybir.dt.float32r
ALU = mybir.AluOpType
ACT = mybir.ActivationFunctionType
AX_X = mybir.AxisListType.X

P = 128
D = 2048
DEPTH = 2
CTX, LAT = 128, 256
TOK = CTX + LAT
GROUPS = ((0, 0, CTX), (1, CTX, TOK))
DT = D // P
HD = 64
HEADS, KV_HEADS = 16, 4
IN_W = 3072
D_FF = 4 * D
TAPS = 31
POOL_WINDOWS = (2, 4, 8, 16)
EPS = 1e-6
SCALE = HD ** -0.5

Q0, K0, V0, PU0, CA0, CG0 = 0, 8, 10, 12, 16, 20

SLOTS = 4
UC = 256
CHUNK = 8
CHUNKS = D_FF // P // CHUNK

Q_IN, Q_OUT, Q_MLP = 0, 12, 20
Q_CHUNK = 8
Q_LAYER = Q_MLP + CHUNKS * Q_CHUNK
B_IN, B_OUT, B_MLP = 0, 12, 28
B_CHUNK = 12
B_LAYER = B_MLP + CHUNKS * B_CHUNK

ADA_BLOCKS = 6 * D // UC
SH1, SC1, G1, SH2, SC2, G2 = (DT * i for i in range(6))
ADA_CU, ADA_QKV, ADA_MIX, ADA_OUT = 16, 20, 28, 44

C_HALF = TAPS // 2
CONV_PAD = C_HALF + CTX + 2 * C_HALF + LAT + C_HALF
CONV_LAT = CTX + 2 * C_HALF
CONV_OUT = CONV_LAT + LAT
P_HALF = max(POOL_WINDOWS) // 2
POOL_PAD = P_HALF + CTX + 2 * P_HALF + LAT + P_HALF
POOL_LAT = P_HALF + CTX + 2 * P_HALF

BANK_SUM, BANK_VAR, BANK_ADA, BANK_MOD = 4, 5, 6, 7

G_PRE1, G_POST1, G_PRE2, G_POST2 = 0, 16, 32, 48
POOL_S, CONV_B, LN_G, LN_B = 64, 68, 72, 76
ROWS_A = 80

STEPS = [(pair, what) for pair in range(HEADS // 2) for what in range(3)]


class Chain:

    def __init__(self, engine, sem):
        self.engine, self.sem, self.n = engine, sem, 0

    def mark(self, instruction):
        instruction.then_inc(self.sem, 1)
        self.n = self.n + 1
        return self.n

    def wait(self, mark):
        self.engine.wait_ge(self.sem, mark)

    def link(self, instruction):
        self.wait(self.mark(instruction))


def backbone(nc, x_prompt, x_sample, cache_k, cache_v, c, c_ctx, w_ada, b_ada, g_pre1, g_post1, g_pre2,
             g_post2, w_in, sink, w_pool, pool_scale, conv_dw, conv_b, conv_ln_g, conv_ln_b, w_conv_pw,
             w_out, w_mlp1, w_mlp2, rope_cos, rope_sin, pool_edge, y_prompt, y_sample, new_k, new_v):
    ctx = ExitStack()
    with ctx:
        def sem(name):
            return ctx.enter_context(nc.semaphore(name))

        base = -(-nc.sbuf_base // 32) * 32
        arena_bytes = nc.sbuf_bytes_remaining // 32 * 32 - 32
        ctx.enter_context(nc.sbuf_tensor("arena", [P, arena_bytes // 4], F32))
        top = [0]

        def at(name, shape, dt, offset):
            return nc.alloc_sbuf_tensor_at(name, [P, *shape], dt, offset=base + offset)

        def new(name, shape, dt=F32):
            size = 4
            for n in shape:
                size *= n
            t = at(name, shape, dt, top[0])
            top[0] += -(-size // 32) * 32
            assert top[0] <= arena_bytes, (name, top[0], arena_bytes)
            return t

        x = new("x", [DT, TOK])
        h_hi = new("h_hi", [DT, TOK], F32R)
        h_lo = new("h_lo", [DT, TOK], F32R)
        z_at = top[0]
        z = new("z", [24, TOK])
        t_at = top[0]
        full = new("full", [DT, TOK])
        hid_hi = at("hid_hi", [CHUNK, TOK], F32R, t_at)
        hid_lo = at("hid_lo", [CHUNK, TOK], F32R, t_at + 4 * CHUNK * TOK)
        raw = new("raw", [SLOTS, 4, UC])
        w_hi = new("w_hi", [SLOTS, 4, UC], F32R)
        w_lo = new("w_lo", [SLOTS, 4, UC], F32R)
        ada_raw = new("ada_raw", [SLOTS, 4, UC])
        ident = new("ident", [P])
        ones = new("ones", [P])
        sel = new("sel", [2])
        cond = new("cond", [DT, 32])
        mods = new("mods", [DEPTH, 6 * DT, 2])
        rstd = new("rstd", [TOK])
        ada_s = new("ada_s", [UC])
        pa = new("pa", [DEPTH, ROWS_A])
        pb = new("pb", [DEPTH, 6 * DT])
        pc = new("pc", [DEPTH, 4 * TAPS])
        coef = new("coef", [4, DT, 2])
        masks = new("masks", [2, P])
        sinks = new("sinks", [DEPTH, HEADS])
        nsinks = new("nsinks", [DEPTH, HEADS])
        row_max = new("row_max", [2, 2])
        nbias = new("nbias", [2, 2])
        sink_in = new("sink_in", [2, 2])
        sink_e = new("sink_e", [2, 2])
        row_sum = new("row_sum", [2, 2])
        rden = new("rden", [2, 2])

        def t_off(n):
            return t_at + 4 * n

        prob_n = 2 * 2 * TOK
        glu = at("glu", [4, CONV_PAD], F32, t_off(0))
        conv = at("conv", [4, CONV_OUT], F32, t_off(4 * CONV_PAD))
        act_in = at("act_in", [4, TOK], F32, t_off(0))
        rot = at("rot", [4, LAT], F32, t_off(prob_n))
        ck = at("ck", [256], F32, t_off(prob_n + 4 * LAT))
        k_out = at("k_out", [256], F32, t_off(prob_n + 4 * LAT + 256))
        cos_t = at("cos_t", [LAT], F32, t_off(2 * prob_n))
        sin_t = at("sin_t", [LAT], F32, t_off(2 * prob_n + LAT))
        o_pw = 2 * prob_n + 512
        assert 4 * CONV_PAD + 4 * CONV_OUT <= o_pw and o_pw + 2560 <= DT * TOK
        pw_w = at("pw_w", [4, 512], F32, t_off(o_pw))
        pool_w = at("pool_w", [4, P], F32, t_off(o_pw + 2048))
        rot2 = at("rot2", [4, LAT], F32, t_off(o_pw))
        prob = at("prob", [2, 2, TOK], F32, t_off(0))
        prob_t = at("prob_t", [2, 3, 256], F32, t_off(prob_n))
        mix_t = at("mix_t", [8, TOK], F32, t_off(2 * prob_n))
        pool_a = at("pool_a", [4, POOL_PAD], F32, z_at + 4 * 16 * TOK)
        edge = at("edge", [4, 2, 2, P_HALF], F32, z_at + 4 * (16 * TOK + 4 * POOL_PAD))
        pool_b = at("pool_b", [TOK + 96], F32, z_at + 4 * 22 * TOK)
        conv_odd = at("conv_odd", [1, CONV_OUT], F32, z_at + 4 * (16 * TOK + 4 * POOL_PAD + 128))
        conv_p0 = at("conv_p0", [CONV_OUT], F32, z_at + 4 * 16 * TOK)
        conv_p1 = at("conv_p1", [CONV_OUT], F32, z_at + 4 * (16 * TOK + 416))
        assert 4 * POOL_PAD + 128 + CONV_OUT <= 6 * TOK and POOL_PAD <= TOK + 96
        kd = at("kd", [KV_HEADS, 512], F32, z_at + 4 * 16 * TOK)
        vt = at("vt", [4, 256], F32, z_at + 4 * (16 * TOK + 2048))
        staged = at("staged", [3, D], F32, z_at)
        rows = at("rows", [6, P], F32, z_at + 4 * 16 * TOK)
        cond_t = at("cond_t", [2, 2 * DT], F32, z_at + 4 * 18 * TOK)

        ps = ctx.enter_context(nc.psum_tensor("ps", [P, 8, 512], F32))

        def sems(names):
            return [sem(n) for n in names.split()]

        raw_landed = [sem(f"raw_landed{s}") for s in range(SLOTS)]
        ada_landed = [sem(f"ada_landed{s}") for s in range(SLOTS)]
        hi_ready, lo_ready, unit_used, acc_free = sems("hi_ready lo_ready unit_used acc_free")
        ada_used, ada_copied, ada_turned, mods_ready = sems("ada_used ada_copied ada_turned mods_ready")
        rows_landed, sinks_landed, x_landed, consts_ready = sems("rows_landed sinks_landed x_landed consts_ready")
        rows_turned, cond_raw, cond_sig, cond_ready, x_turned, x_copied = sems(
            "rows_turned cond_raw cond_sig cond_ready x_turned x_copied")
        sq_ready, sq_used, var_ready, std_ready = sems("sq_ready sq_used var_ready std_ready")
        x_updated, full_ready, h_hi_ready, h_ready = sems("x_updated full_ready h_hi_ready h_ready")
        conv_w_landed, pads_ready, sig_ready, conv_ready, ln_sum, cen_ready, csq_ready, csq_used = sems(
            "conv_w_landed pads_ready sig_ready conv_ready ln_sum cen_ready csq_ready csq_used")
        glu_ready, edge_landed, mix_added = sems("glu_ready edge_landed mix_added")
        lnv_ready, lnstd_ready, ln_ready, silu_sig, conv_act, pw_ready, pw_hi, pw_done = sems(
            "lnv_ready lnstd_ready ln_ready silu_sig conv_act pw_ready pw_hi pw_done")
        pool_summed, pooled, pool_mm, pool_hi, pool_done = sems("pool_summed pooled pool_mm pool_hi pool_done")
        rope_landed, cachev_landed, kv_turned, v_ready, ck_turned, kd_ready, kv_out = sems(
            "rope_landed cachev_landed kv_turned v_ready ck_turned kd_ready kv_out")
        s_ready, nb_ready, p_ready, rden_ready, pn_ready, t_ready, pt_ready, o_ready, o_hi, o_done = sems(
            "s_ready nb_ready p_ready rden_ready pn_ready t_ready pt_ready o_ready o_hi o_done")
        sqh_ready, hidh_ready, hid_ready, added = sems("sqh_ready hidh_ready hid_ready added")
        y_turned, y_copied, y_stored = sems("y_turned y_copied y_stored")
        dve_chain, act_chain, pool_chain = sems("dve_chain act_chain pool_chain")

        def quad(layer, phase):
            return layer * Q_LAYER + phase

        def blk(layer, phase):
            return layer * B_LAYER + phase

        def per_token(t, n, lo=0, hi=TOK):
            return t[:, lo:hi].unsqueeze(1).to_broadcast([P, n, hi - lo])

        block = ctx.enter_context(nc.Block())

        @block.sync
        def _(sp):
            def load_unit(j, q, src, wait=True):
                if wait:
                    sp.wait_ge(lo_ready, 4 * q + j - 3)
                sp.dma_start(raw[:, j % 4, :, :], src).then_inc(raw_landed[j % 4], 16)

            def load_ada(layer, m, j, wait=True):
                n = layer * ADA_BLOCKS + m
                if wait:
                    sp.wait_ge(ada_used, 4 * n + j - 3)
                src = w_ada[layer, 512 * j:512 * j + 512, bass.ds(m * UC, UC)]
                sp.dma_start(ada_raw[:, j, :, :], src.rearrange("(k p) n -> p k n", p=P)).then_inc(ada_landed[j], 16)

            def part(w, layer, row, col):
                return w[layer, bass.ds(row, 512), bass.ds(col, UC)].rearrange("(k p) n -> p k n", p=P)

            def load_blocks(layer, w, q, col, ada):
                for j in range(8):
                    load_unit(j, q, part(w, layer, 512 * (j % 4), col + UC * (j // 4)))
                    if ada is not None:
                        load_ada(ada[0], ada[1] + j // 4, j % 4)

            sp.dma_start(staged[:, 0, :], x_prompt[0, :, :]).then_inc(x_landed, 16)
            sp.dma_start(staged[:, 1:3, :], x_sample[0, :, :].rearrange("(b p) n -> p b n", p=P)).then_inc(x_landed, 16)
            for j in range(4):
                load_ada(0, 0, j, wait=False)
            for j in range(4):
                load_unit(j, 0, part(w_in, 0, 512 * j, CA0 * P), wait=False)
            with sp.Fori(1, ADA_CU) as m:
                for j in range(4):
                    load_ada(0, m, j)
            for layer in range(DEPTH):
                first = layer == 0
                if first:
                    for j in range(4):
                        load_ada(0, ADA_CU, j)
                    for j in range(4, 8):
                        load_unit(j, 0, part(w_in, 0, 512 * (j - 4), CA0 * P + UC))
                        load_ada(0, ADA_CU + 1, j - 4)
                    load_blocks(0, w_in, 2, CA0 * P + 2 * UC, (0, ADA_CU + 2))
                else:
                    with sp.Fori(0, 2) as i:
                        load_blocks(layer, w_in, quad(layer, Q_IN) + i * 2, CA0 * P + i * 2 * UC, None)
                for k, tile in enumerate((PU0, K0)):
                    load_blocks(layer, w_in, quad(layer, Q_IN + 4) + k * 2, tile * P, (0, ADA_QKV + k * 2) if first else None)
                with sp.Fori(0, 2) as i:
                    load_blocks(layer, w_in, quad(layer, Q_IN + 8) + i * 2, i * 2 * UC,
                                (0, ADA_QKV + 4 + i * 2) if first else None)

                def load_out(i, half, j):
                    load_unit(j, quad(layer, Q_OUT + 4 * half) + i, part(w_out, layer, D // 2 * (1 - half) + 512 * (j % 2),
                                                                        i * (2 * UC) + UC * (j // 2)))

                def load_pair(i, half, j, m):
                    for k in range(4):
                        load_ada(0, m, k)
                    load_out(i, half, j)
                    for k in range(2):
                        load_ada(0, m + 1, k)
                    load_out(i, half, j + 1)
                    for k in range(2, 4):
                        load_ada(0, m + 1, k)

                if first:
                    for j in range(4):
                        load_out(0, 0, j)
                    with sp.Fori(0, 3) as i:
                        load_pair(i + 1, 0, 0, i * 4 + ADA_MIX)
                        load_pair(i + 1, 0, 2, i * 4 + (ADA_MIX + 2))
                    load_pair(0, 1, 0, ADA_MIX + 12)
                    load_pair(0, 1, 2, ADA_MIX + 14)
                    with sp.Fori(0, 3) as i:
                        for j in range(4):
                            load_ada(0, i + ADA_OUT, j)
                            load_out(i + 1, 1, j)
                    for j in range(4):
                        load_ada(0, ADA_OUT + 3, j)
                else:
                    for half in range(2):
                        with sp.Fori(0, 4) as i:
                            for j in range(4):
                                load_out(i, half, j)
                with sp.Fori(0, CHUNKS) as ch:
                    q = quad(layer, Q_MLP) + ch * Q_CHUNK
                    with sp.Fori(0, 2) as i:
                        load_blocks(layer, w_mlp1, q + i * 2, ch * (CHUNK * P) + i * (2 * UC),
                                    (1, ch * 6 + i * 2) if first else None)
                    with sp.Fori(0, 2) as i:
                        for j in range(8):
                            load_unit(j, q + 4 + i * 2, part(w_mlp2, layer, ch * (CHUNK * P) + 512 * (j % 2),
                                                             i * (4 * UC) + UC * (j // 2)))
                            if first and j < 4:
                                load_ada(1, ch * 6 + 4 + i, j)
            outs = [y_prompt[0, :, :], y_sample[0, 0:P, :], y_sample[0, P:2 * P, :]]
            for b in range(3):
                sp.wait_ge(y_copied, 4 * (b + 1))
                sp.dma_start(outs[b], staged[:, b, :]).then_inc(y_stored, 16)
            sp.wait_ge(y_stored, 48)

        @block.gpsimd
        def _(pool):
            chain = Chain(pool, pool_chain)

            def tiles(w):
                return w.rearrange("(t p) -> t p", p=P)

            for layer in range(DEPTH):
                a = 3 * layer
                for r, n, w in ((0, 16, g_pre1), (16, 16, g_post1), (32, 16, g_pre2), (48, 16, g_post2),
                                (64, 4, pool_scale), (68, 4, conv_b), (72, 4, conv_ln_g), (76, 4, conv_ln_b)):
                    pool.dma_start(rows[r:r + n, a, :], tiles(w[layer])).then_inc(rows_landed, 16)
                pool.dma_start(rows[0:96, a + 1, :], tiles(b_ada[layer])).then_inc(rows_landed, 16)
                pool.dma_start(rows[0:124, a + 2, :], conv_dw[layer].rearrange("k (t p) -> (k t) p", p=P)).then_inc(rows_landed, 16)
                for g, w in enumerate((c_ctx, c[0])):
                    pool.dma_start(rows[80 + 16 * g:96 + 16 * g, a, :], tiles(w)).then_inc(rows_landed, 16)
            pool.dma_start(sinks[:, :, :], sink.unsqueeze(0).to_broadcast([P, DEPTH, HEADS])).then_inc(sinks_landed, 16)

            nc.gpsimd.memset(ones[:, :], 1.0).then_inc(consts_ready, 1)
            nc.gpsimd.memset(cond[:, :, :], 0.0).then_inc(consts_ready, 1)
            chain.link(nc.gpsimd.memset(ident[:, :], 0.0))
            chain.link(nc.gpsimd.memset(sel[:, :], 0.0))
            chain.link(nc.gpsimd.memset(masks[:, :, :], 0.0))
            nc.gpsimd.affine_select(out=ident[:, :], in_=ident[:, :], compare_op=ALU.not_equal, fill=1.0, base=0,
                                    pattern=[[-1, P]], channel_multiplier=1).then_inc(consts_ready, 1)
            for i in range(4):
                chain.link(nc.gpsimd.affine_select(out=sel[:, :], in_=sel[:, :], compare_op=ALU.not_equal, fill=1.0,
                                                   base=-32 * i, pattern=[[-1, 2]], channel_multiplier=1))
            for i in range(2):
                nc.gpsimd.affine_select(out=masks[:, i, :], in_=masks[:, i, :], compare_op=ALU.is_ge,
                                        fill=-1e30 / SCALE, base=0, pattern=[[2 * i - 1, P]],
                                        channel_multiplier=1 - 2 * i).then_inc(consts_ready, 1)
            nc.gpsimd.memset(rden[:, 0, 0:1], 0.0).then_inc(sqh_ready, 1)
            nc.gpsimd.memset(rden[:, 0, 1:2], 0.0).then_inc(hid_ready, 1)
            nc.gpsimd.memset(rden[:, 1, 0:1], 0.0).then_inc(added, 1)
            nc.gpsimd.memset(rden[:, 1, 1:2], 0.0).then_inc(added, 1)

            for layer in range(DEPTH):
                pool.wait_ge(h_ready, (2 * layer + 1) * 8)
                pool.dma_start(pw_w[:, :, :], w_conv_pw[layer].rearrange("(k p) n -> p k n", p=P)).then_inc(conv_w_landed, 16)
                pool.dma_start(pool_w[:, :, :], w_pool[layer].rearrange("g c d -> c g d")).then_inc(conv_w_landed, 16)
                nc.gpsimd.memset(glu[:, :, 0:C_HALF], 0.0).then_inc(pads_ready, 1)
                nc.gpsimd.memset(glu[:, :, C_HALF + CTX:C_HALF + CONV_LAT], 0.0).then_inc(pads_ready, 1)
                nc.gpsimd.memset(glu[:, :, C_HALF + CONV_OUT:CONV_PAD], 0.0).then_inc(pads_ready, 1)
                pool.wait_ge(glu_ready, layer + 1)
                for k in range(TAPS):
                    src, out, w = glu[:, 3, k:k + CONV_OUT], conv[:, 3, :], pc[:, layer, 4 * k + 3:4 * k + 4]
                    if k == 0:
                        chain.link(nc.gpsimd.tensor_scalar(out, src, w, pa[:, layer, CONV_B + 3:CONV_B + 4], ALU.mult, ALU.add))
                    else:
                        product = (conv_p0, conv_p1)[k % 2]
                        chain.link(nc.gpsimd.tensor_scalar(product[:, :], src, w, None, ALU.mult))
                        chain.mark(nc.gpsimd.tensor_tensor(out, out, product[:, :], ALU.add))
                chain.wait(chain.n)
                pool.dma_start(edge[:, :, :, :], pool_edge.unsqueeze(0).to_broadcast([P, 4, 2, 2, P_HALF])).then_inc(edge_landed, 16)
                nc.gpsimd.memset(pool_a[:, :, 0:P_HALF], 0.0).then_inc(conv_ready, 1)
                nc.gpsimd.memset(pool_a[:, :, P_HALF + CTX:POOL_LAT], 0.0)
                nc.gpsimd.memset(pool_a[:, :, POOL_LAT + LAT:POOL_PAD], 0.0)
                pool.wait_ge(acc_free, blk(layer, 6))
                nc.gpsimd.tensor_copy(pool_a[:, :, P_HALF:P_HALF + CTX], z[:, PU0:PU0 + 4, 0:CTX])
                chain.link(nc.gpsimd.tensor_copy(pool_a[:, :, POOL_LAT:POOL_LAT + LAT], z[:, PU0:PU0 + 4, CTX:TOK]))
                pool.wait_ge(edge_landed, 16 * (layer + 1))
                for g, w in enumerate(POOL_WINDOWS):
                    here, there, span = pool_a[:, g, :], pool_b[:, 0:POOL_PAD], 1
                    while span < w:
                        n = POOL_PAD - 2 * span + 1
                        chain.link(nc.gpsimd.tensor_tensor(there[:, 0:n], here[:, 0:n], here[:, span:span + n], ALU.add))
                        here, there, span = there, here, 2 * span
                    if g % 2 == 0:
                        chain.link(nc.gpsimd.tensor_copy(pool_a[:, g, 0:n], pool_b[:, 0:n]))
                    for s, (start, length) in enumerate(((P_HALF, CTX), (POOL_LAT, LAT))):
                        for e, off in enumerate((0, length - P_HALF)):
                            a = start + off - w // 2
                            chain.link(nc.gpsimd.tensor_tensor(pool_a[:, g, a:a + P_HALF], pool_a[:, g, a:a + P_HALF],
                                                               edge[:, g, s, e, :], ALU.mult))
                nc.gpsimd.memset(pool_b[:, 0:1], 0.0).then_inc(pool_summed, 1)
                pool.wait_ge(cen_ready, layer + 1)
                pool.dma_start(cos_t[:, :], rope_cos).then_inc(rope_landed, 16)
                pool.dma_start(sin_t[:, :], rope_sin).then_inc(rope_landed, 16)
                pool.dma_start(ck[:, :], cache_k[0, layer].rearrange("t h d -> t (h d)")).then_inc(rope_landed, 16)
                pool.wait_ge(conv_act, layer + 1)
                pool.dma_start(vt[:, 3, :], cache_v[0, layer].rearrange("t h d -> t (h d)")).then_inc(cachev_landed, 16)
                pool.wait_ge(v_ready, 2 * (layer + 1))
                pool.dma_start(new_k[0, layer].rearrange("t h d -> t (h d)"), k_out[:, :]).then_inc(kv_out, 16)
                pool.dma_start(new_v[0, layer].rearrange("t h d -> t (h d)"), vt[:, 0, :]).then_inc(kv_out, 16)
                for half in range(2):
                    with pool.Fori(0, 4) as i:
                        pool.wait_ge(acc_free, i + blk(layer, B_OUT + 9 + 4 * half))
                        dst = z[:, bass.ds(i * 2 + 8 * half, 2), :]
                        part = mix_t[:, bass.ds(i * 2, 2), :] if half else z[:, bass.ds(i * 2 + 8, 2), :]
                        nc.gpsimd.tensor_tensor(dst, dst, part, ALU.add).then_inc(mix_added, 1)
                pool.wait_ge(x_updated, (2 * layer + 1) * 8)
                chain.link(nc.gpsimd.memset(z[:, 0:16, :], 0.0))
                with pool.Fori(0, CHUNKS) as ch:
                    with pool.Fori(0, 4) as i:
                        hidden = layer * 32 + ch * 4 + i
                        pool.wait_ge(acc_free, blk(layer, B_MLP + 1) + ch * B_CHUNK + i)
                        pool.wait_ge(hid_ready, hidden + 1)
                        nc.gpsimd.tensor_tensor(z[:, 18:20, :], z[:, 16:18, :], z[:, 16:18, :], ALU.mult).then_inc(sqh_ready, 1)
                    with pool.Fori(0, 4) as i:
                        for e in range(2):
                            pool.wait_ge(acc_free, blk(layer, B_MLP + 5 + e) + ch * B_CHUNK + i * 2)
                            dst = z[:, bass.ds(i * 4 + 2 * e, 2), :]
                            nc.gpsimd.tensor_tensor(dst, dst, z[:, 20 + 2 * e:22 + 2 * e, :], ALU.add).then_inc(added, 1)
                pool.wait_ge(added, 64 * (layer + 1) + 2)

        @block.scalar
        def _(act):
            chain = Chain(act, act_chain)

            def w_high(j, q):
                act.wait_ge(raw_landed[j % 4], 16 * (q + (j // 4 + 1)))
                nc.scalar.activation(w_hi[:, j % 4, :, :], raw[:, j % 4, :, :], ACT.Copy).then_inc(hi_ready, 1)

            def eight_units(q, evict, prefetch=8, before=None):
                for j in range(8):
                    if before and j in before:
                        before[j]()
                    act.wait_ge(unit_used, 4 * q + (j + 1))
                    if j in evict:
                        evict[j]()
                    if j < prefetch:
                        w_high(j, q + 1)

            def copy_out(pair, tile):
                nc.scalar.activation(z[:, bass.ds(tile, 2), :], ps[:, 2 * pair:2 * pair + 2, 0:TOK], ACT.Copy).then_inc(acc_free, 1)

            def two_out(tile):
                return {3: lambda: copy_out(0, tile), 7: lambda: copy_out(1, tile + 2)}

            def squares(n, src, ready):
                for i in range(8):
                    ready(i)
                    if n or i >= 2:
                        act.wait_ge(sq_used, max(8 * n, 8 * n + i - 1))
                    nc.scalar.activation(z[:, 20 + 2 * (i % 2):22 + 2 * (i % 2), :], src[:, 2 * i:2 * i + 2, :],
                                         ACT.Square).then_inc(sq_ready, 1)

            def root(n):
                act.wait_ge(var_ready, n + 1)
                nc.scalar.activation(rstd[:, :], rstd[:, :], ACT.Sqrt).then_inc(std_ready, 1)

            def h_high(m):
                for i in range(8):
                    act.wait_ge(full_ready, 8 * m + i + 1)
                    nc.scalar.activation(h_hi[:, 2 * i:2 * i + 2, :], full[:, 2 * i:2 * i + 2, :], ACT.Copy).then_inc(h_hi_ready, 1)

            act.wait_ge(cond_raw, 1)
            nc.scalar.activation(cond_t[:, 1, :], cond_t[:, 0, :], ACT.Sigmoid).then_inc(cond_sig, 1)
            for g in range(12):
                b, j = divmod(g, 4)
                act.wait_ge(x_turned, g + 1)
                nc.scalar.activation(x[:, 4 * j:4 * j + 4, P * b:P * b + P],
                                     ps[:, 2 + g % 2, :].rearrange("p (t n) -> p t n", n=P), ACT.Copy).then_inc(x_copied, 1)
            for j in range(4):
                w_high(j, 0)

            for layer in range(DEPTH):
                if layer == 0:
                    squares(0, x, lambda i: act.wait_ge(x_copied, 12))
                else:
                    squares(4 * layer, x, lambda i: act.wait_ge(x_updated, 8 * (2 * layer - 1) + i + 1))
                root(4 * layer)
                h_high(2 * layer)
                with act.Fori(0, 2) as i:
                    eight_units(quad(layer, Q_IN) + i * 2, two_out(i * 4 + CA0))
                act.wait_ge(acc_free, blk(layer, 4))
                nc.scalar.activation(z[:, CG0:CG0 + 4, :], z[:, CG0:CG0 + 4, :], ACT.Sigmoid).then_inc(sig_ready, 1)
                for k, tile in enumerate((PU0, K0, Q0)):
                    eight_units(quad(layer, Q_IN + 4) + k * 2, two_out(tile))

                def center_squares():
                    act.wait_ge(cen_ready, layer + 1)
                    nc.scalar.activation(z[:, CG0:CG0 + 4, :], act_in[:, :, :], ACT.Square).then_inc(csq_ready, 1)

                def ln_root():
                    act.wait_ge(lnv_ready, layer + 1)
                    nc.scalar.activation(rstd[:, :], rstd[:, :], ACT.Sqrt).then_inc(lnstd_ready, 1)

                def silu_gate():
                    act.wait_ge(ln_ready, layer + 1)
                    nc.scalar.activation(z[:, CG0:CG0 + 4, :], act_in[:, :, :], ACT.Sigmoid).then_inc(silu_sig, 1)

                eight_units(quad(layer, Q_IN + 10), two_out(4), before={2: center_squares, 4: ln_root, 5: silu_gate})
                act.wait_ge(kv_turned, layer + 1)
                act.wait_ge(conv_act, layer + 1)
                nc.scalar.activation(vt[:, 0:2, :], ps[:, 4, :].rearrange("p (b n) -> p b n", n=256), ACT.Copy)
                nc.scalar.activation(vt[:, 2, :], ps[:, 5, 0:256], ACT.Copy).then_inc(v_ready, 1)
                nc.scalar.activation(k_out[:, :], ps[:, 5, 256:512], ACT.Copy).then_inc(v_ready, 1)
                for g in range(4):
                    act.wait_ge(pool_mm, 4 * layer + g + 1)
                    nc.scalar.activation(h_hi[:, 8 + g, :], ps[:, g, 0:TOK], ACT.Copy,
                                         scale=pa[:, layer, POOL_S + g:POOL_S + g + 1]).then_inc(pool_hi, 1)
                for t in range(4):
                    act.wait_ge(pw_ready, 4 * layer + t + 1)
                    nc.scalar.activation(h_hi[:, 12 + t, :], ps[:, t, 0:TOK], ACT.Copy).then_inc(pw_hi, 1)

                def exps(s):
                    pair, what = STEPS[s]
                    n, k, done = (TOK if what else CTX), s % 2, layer * len(STEPS)
                    act.wait_ge(nb_ready, done + s + 1)
                    if done + s >= 2:
                        act.wait_ge(t_ready, done + s - 1)
                    for e in range(2):
                        nc.scalar.activation(prob[:, k, e, 0:n], ps[:, 2 + e, 0:n], ACT.Exp, bias=nbias[:, k, e:e + 1],
                                             scale=SCALE, accum_out=row_sum[:, k, e:e + 1])
                    nc.scalar.activation(sink_e[:, k, :], sink_in[:, k, :], ACT.Exp).then_inc(p_ready, 1)

                def normalise(s):
                    n, k, done = (TOK if STEPS[s][1] else CTX), s % 2, layer * len(STEPS)
                    act.wait_ge(rden_ready, done + s + 1)
                    for e in range(2):
                        last = nc.scalar.activation(prob[:, k, e, 0:n], prob[:, k, e, 0:n], ACT.Copy, scale=rden[:, k, e:e + 1])
                    last.then_inc(pn_ready, 1)

                def out_high(s):
                    pair, what = STEPS[s]
                    act.wait_ge(o_ready, layer * len(STEPS) + s + 1)
                    nc.scalar.activation(h_hi[:, pair, P * what:P * what + P], ps[:, BANK_MOD, 256:384], ACT.Copy).then_inc(o_hi, 1)

                def side_unit(s):
                    u = 2 * STEPS[s][0] + STEPS[s][1] - 1
                    q, j, b = quad(layer, Q_OUT) + u // 4, u % 4, u // 2
                    act.wait_ge(unit_used, 4 * q + j + 1)
                    if u % 2:
                        if b == 4:
                            act.wait_ge(kv_out, 32 * (layer + 1))
                        dst = z[:, 8 + 2 * b:10 + 2 * b, :] if b < 4 else mix_t[:, 2 * b - 8:2 * b - 6, :]
                        nc.scalar.activation(dst, ps[:, 0:2, 0:TOK], ACT.Copy).then_inc(acc_free, 1)
                    w_high(j, q + 1)

                for s in range(len(STEPS) + 1):
                    what = STEPS[s][1] if s < len(STEPS) else 0
                    if what == 2:
                        side_unit(s - 1)
                    if s < len(STEPS):
                        exps(s)
                        normalise(s)
                    if s and not what:
                        side_unit(s - 1)
                    if s:
                        out_high(s - 1)

                def mix_out(pair, tile, b=None):
                    if b is not None:
                        act.wait_ge(mix_added, b)
                    copy_out(pair, tile)

                eight_units(quad(layer, Q_OUT + 4), {2 * k + 1: (lambda k=k: mix_out((k + 1) % 2, 2 * k)) for k in range(4)})
                eight_units(quad(layer, Q_OUT + 6), {2 * k + 1: (lambda k=k: mix_out((k + 1) % 2, 8 + 2 * k, 8 * layer + k + 1)) for k in range(4)})
                squares(4 * layer + 1, z, lambda i: act.wait_ge(mix_added, 8 * layer + i + 1))
                root(4 * layer + 1)
                squares(4 * layer + 2, x, lambda i: act.wait_ge(x_updated, 8 * (2 * layer) + i + 1))
                root(4 * layer + 2)
                h_high(2 * layer + 1)

                def relu_out(pair, tile, ch, b):
                    hidden = ch * 4 + b
                    act.wait_ge(sqh_ready, hidden + (32 * layer + 1))
                    nc.scalar.activation(z[:, 16:18, :], ps[:, 2 * pair:2 * pair + 2, 0:TOK], ACT.Relu).then_inc(acc_free, 1)
                    act.wait_ge(acc_free, blk(layer, B_MLP + 1) + ch * B_CHUNK + b)
                    nc.scalar.activation(hid_hi[:, bass.ds(tile, 2), :], z[:, 16:18, :], ACT.Square).then_inc(hidh_ready, 1)

                def sum_out(pair, n):
                    act.wait_ge(added, n + 1)
                    nc.scalar.activation(z[:, 20 + 2 * pair:22 + 2 * pair, :], ps[:, 2 * pair:2 * pair + 2, 0:TOK],
                                         ACT.Copy).then_inc(acc_free, 1)

                def up(ch, q):
                    with act.Fori(0, 2) as i:
                        eight_units(q + i * 2, {3: lambda: relu_out(0, i * 4, ch, i * 2),
                                                7: lambda: relu_out(1, i * 4 + 2, ch, i * 2 + 1)})

                def down(ch, q, i, prefetch=8):
                    n = 64 * layer + ch * 8 + i * 4
                    eight_units(q + 4 + i * 2, {2 * k + 1: (lambda k=k: sum_out(k % 2, n + k)) for k in range(4)}, prefetch)

                last = layer == DEPTH - 1
                with act.Fori(0, CHUNKS - 1 if last else CHUNKS) as ch:
                    q = quad(layer, Q_MLP) + ch * Q_CHUNK
                    up(ch, q)
                    with act.Fori(0, 2) as i:
                        down(ch, q, i)
                if last:
                    ch, q = CHUNKS - 1, quad(layer, Q_MLP) + (CHUNKS - 1) * Q_CHUNK
                    up(ch, q)
                    down(ch, q, 0)
                    down(ch, q, 1, prefetch=4)
                squares(4 * layer + 3, z, lambda i: act.wait_ge(added, 64 * (layer + 1) + 2))
                root(4 * layer + 3)
            for g in range(12):
                b, j = divmod(g, 4)
                act.wait_ge(y_turned, g + 1)
                nc.scalar.activation(staged[:, b, 512 * j:512 * j + 512], ps[:, g % 4, :], ACT.Copy).then_inc(y_copied, 1)

        @block.vector
        def _(dve):
            chain = Chain(dve, dve_chain)

            def w_low(j, q):
                dve.wait_ge(hi_ready, 4 * q + (j + 1))
                nc.vector.tensor_tensor(w_lo[:, j % 4, :, :], raw[:, j % 4, :, :], w_hi[:, j % 4, :, :].bitcast(F32),
                                        ALU.subtract).then_inc(lo_ready, 1)

            def ada_copy(n):
                dve.wait_ge(ada_used, 4 * n + 4)
                nc.vector.tensor_copy(ada_s[:, :], ps[:, BANK_ADA, 0:UC]).then_inc(ada_copied, 1)

            def ada_mods(layer, m, n):
                dve.wait_ge(ada_turned, n + 1)
                nc.vector.tensor_tensor(mods[:, layer, bass.ds(m * 2, 2), :],
                                        ps[:, BANK_MOD, 0:4].rearrange("p (t g) -> p t g", g=2),
                                        pb[:, layer, bass.ds(m * 2, 2)].unsqueeze(2).to_broadcast([P, 2, 2]),
                                        ALU.add).then_inc(mods_ready, 1)

            def eight_units(q, before=None, after=None, prefetch=8):
                for j in range(8):
                    for f in (before or {}).get(j, ()):
                        f()
                    if j < prefetch:
                        w_low(j, q + 1)
                    for f in (after or {}).get(j, ()):
                        f()

            def ada_pair(layer, m):
                n = layer * ADA_BLOCKS + m
                return ({3: [lambda: ada_copy(n)], 4: [lambda: ada_mods(layer, m, n)], 7: [lambda: ada_copy(n + 1)]},
                        {7: [lambda: ada_mods(layer, m + 1, n + 1)]})

            def inverse_root(n):
                dve.wait_ge(sq_used, 8 * (n + 1))
                nc.vector.tensor_scalar(rstd[:, :], ps[:, BANK_SUM, 0:TOK], 1.0 / D, EPS, ALU.mult, ALU.add).then_inc(var_ready, 1)
                dve.wait_ge(std_ready, n + 1)
                chain.link(nc.vector.reciprocal(rstd[:, :], rstd[:, :]))

            def residual(r, k):
                def normal(i):
                    t = z[:, 2 * i:2 * i + 2, :]
                    return chain.mark(nc.vector.tensor_tensor(t, t, per_token(rstd, 2), ALU.mult))

                marks = [normal(0)]
                for i in range(8):
                    if i < 7:
                        marks.append(normal(i + 1))
                    chain.wait(marks[i])
                    for t in (2 * i, 2 * i + 1):
                        for g, a, b in GROUPS:
                            last = nc.vector.scalar_tensor_tensor(out=x[:, t, a:b], in0=z[:, t, a:b], scalar=coef[:, k, t, g:g + 1],
                                                                  in1=x[:, t, a:b], op0=ALU.mult, op1=ALU.add)
                    last.then_inc(x_updated, 1)

            def build_h(m, layer, k, shift):
                def normal(i):
                    return chain.mark(nc.vector.tensor_tensor(full[:, 2 * i:2 * i + 2, :], x[:, 2 * i:2 * i + 2, :],
                                                              per_token(rstd, 2), ALU.mult))

                def low(i):
                    dve.wait_ge(h_hi_ready, 8 * m + i + 1)
                    nc.vector.tensor_tensor(h_lo[:, 2 * i:2 * i + 2, :], full[:, 2 * i:2 * i + 2, :],
                                            h_hi[:, 2 * i:2 * i + 2, :].bitcast(F32), ALU.subtract).then_inc(h_ready, 1)

                marks = [normal(0)]
                for i in range(8):
                    if i < 7:
                        marks.append(normal(i + 1))
                    chain.wait(marks[i])
                    for t in (2 * i, 2 * i + 1):
                        for g, a, b in GROUPS:
                            last = nc.vector.tensor_scalar(full[:, t, a:b], full[:, t, a:b], coef[:, k, t, g:g + 1],
                                                           mods[:, layer, shift + t, g:g + 1], ALU.mult, ALU.add)
                    last.then_inc(full_ready, 1)
                    if i:
                        low(i - 1)
                low(7)

            def gain(k, layer, g0):
                return pa[:, layer, g0:g0 + DT].unsqueeze(2).to_broadcast([P, DT, 2])

            def scale_coef(k, layer, sc, g0):
                chain.link(nc.vector.scalar_tensor_tensor(out=coef[:, k, :, :], in0=mods[:, layer, sc:sc + DT, :], scalar=1.0,
                                                          in1=gain(k, layer, g0), op0=ALU.add, op1=ALU.mult))

            def gate_coef(k, layer, g, g0):
                chain.link(nc.vector.tensor_tensor(coef[:, k, :, :], mods[:, layer, g:g + DT, :], gain(k, layer, g0), ALU.mult))

            dve.wait_ge(rows_turned, 1)
            nc.vector.tensor_copy(cond_t[:, 0, :], ps[:, 0, 80:112]).then_inc(cond_raw, 1)
            for layer in range(DEPTH):
                nc.vector.tensor_copy(pa[:, layer, :], ps[:, layer, 0:ROWS_A])
                nc.vector.tensor_copy(pb[:, layer, :], ps[:, layer, 128:224])
                chain.link(nc.vector.tensor_copy(pc[:, layer, :], ps[:, layer, 256:380]))
            dve.wait_ge(consts_ready, 5)
            dve.wait_ge(cond_sig, 1)
            for g in range(2):
                last = nc.vector.tensor_tensor(cond[:, :, g], cond_t[:, 0, DT * g:DT * g + DT], cond_t[:, 1, DT * g:DT * g + DT], ALU.mult)
            last.then_inc(cond_ready, 1)
            dve.wait_ge(sinks_landed, 16)
            chain.link(nc.vector.tensor_scalar(nsinks[:, :, :], sinks[:, :, :], -1.0, None, ALU.mult))
            for j in range(4):
                w_low(j, 0)
            with dve.Fori(0, ADA_CU) as m:
                ada_copy(m)
                ada_mods(0, m, m)

            for layer in range(DEPTH):
                first = layer == 0
                n_mods = ADA_BLOCKS * layer
                dve.wait_ge(mods_ready, n_mods + ADA_CU)
                scale_coef(0, layer, SC1, G_PRE1)
                inverse_root(4 * layer)
                build_h(2 * layer, layer, 0, SH1)
                with dve.Fori(0, 2) as i:
                    eight_units(quad(layer, Q_IN) + i * 2, *(ada_pair(0, i * 2 + ADA_CU) if first else ()))
                dve.wait_ge(sig_ready, layer + 1)
                dve.wait_ge(pads_ready, 3 * (layer + 1))
                chain.link(nc.vector.tensor_tensor(glu[:, :, C_HALF:C_HALF + CTX], z[:, CA0:CA0 + 4, 0:CTX], z[:, CG0:CG0 + 4, 0:CTX], ALU.mult))
                chain.link(nc.vector.tensor_tensor(glu[:, :, C_HALF + CONV_LAT:C_HALF + CONV_OUT], z[:, CA0:CA0 + 4, CTX:TOK],
                                                   z[:, CG0:CG0 + 4, CTX:TOK], ALU.mult))

                nc.vector.memset(row_max[:, 0, :], 0.0).then_inc(glu_ready, 1)

                n0 = chain.n
                with dve.Fori(0, 3) as i:
                    chain.n = n0 + i * (TAPS + 1)
                    done = conv[:, bass.ds(i, 1), :]
                    marks = []

                    def tap(k):
                        src, out = glu[:, bass.ds(i, 1), k:k + CONV_OUT], conv_odd[:, :, :] if k % 2 else done
                        w = pc[:, layer, bass.ds(i + 4 * k, 1)]
                        if k >= 2:
                            chain.wait(marks[k - 2])
                            op = nc.vector.scalar_tensor_tensor(out=out, in0=src, scalar=w, in1=out, op0=ALU.mult, op1=ALU.add)
                        elif k == 1:
                            op = nc.vector.tensor_scalar(out, src, w, None, ALU.mult)
                        else:
                            op = nc.vector.tensor_scalar(out, src, w, pa[:, layer, bass.ds(i + CONV_B, 1)], ALU.mult, ALU.add)
                        marks.append(chain.mark(op))
                        if k == TAPS - 1:
                            chain.wait(marks[k])
                            chain.link(nc.vector.tensor_tensor(done, done, conv_odd[:, :, :], ALU.add))

                    before, after = ada_pair(0, i * 2 + ADA_QKV) if first else ({}, {})
                    for j in range(8):
                        after[j] = [(lambda k=k: tap(k)) for k in range(4 * j, min(4 * j + 4, TAPS))] + list(after.get(j, []))
                    eight_units(quad(layer, Q_IN + 4) + i * 2, before, after)
                chain.n = n0 + 3 * (TAPS + 1)
                nc.vector.memset(row_max[:, 0, :], 0.0).then_inc(conv_ready, 1)

                def pool_means():
                    dve.wait_ge(pool_summed, layer + 1)
                    for g, w in enumerate(POOL_WINDOWS):
                        for start, a, b in ((P_HALF, 0, CTX), (POOL_LAT, CTX, TOK)):
                            o = start - w // 2
                            last = nc.vector.scalar_tensor_tensor(out=z[:, PU0 + g, a:b], in0=pool_a[:, g, o:o + b - a], scalar=1.0 / w,
                                                                  in1=z[:, PU0 + g, a:b], op0=ALU.mult, op1=ALU.subtract)
                    last.then_inc(pooled, 1)

                def center():
                    dve.wait_ge(ln_sum, layer + 1)
                    chain.link(nc.vector.tensor_scalar(rstd[:, :], ps[:, BANK_SUM, 0:TOK], 1.0 / 512, None, ALU.mult))
                    nc.vector.tensor_tensor(act_in[:, :, 0:CTX], conv[:, :, 0:CTX], per_token(rstd, 4, 0, CTX), ALU.subtract)
                    nc.vector.tensor_tensor(act_in[:, :, CTX:TOK], conv[:, :, CONV_LAT:CONV_OUT], per_token(rstd, 4, CTX, TOK),
                                            ALU.subtract).then_inc(cen_ready, 1)

                def variance():
                    dve.wait_ge(csq_used, layer + 1)
                    nc.vector.tensor_scalar(rstd[:, :], ps[:, BANK_VAR, 0:TOK], 1.0 / 512, EPS, ALU.mult, ALU.add).then_inc(lnv_ready, 1)

                def layer_norm():
                    dve.wait_ge(lnstd_ready, layer + 1)
                    chain.link(nc.vector.reciprocal(rstd[:, :], rstd[:, :]))
                    chain.link(nc.vector.tensor_tensor(act_in[:, :, :], act_in[:, :, :], per_token(rstd, 4), ALU.mult))
                    for t in range(4):
                        last = nc.vector.tensor_scalar(act_in[:, t, :], act_in[:, t, :], pa[:, layer, LN_G + t:LN_G + t + 1],
                                                       pa[:, layer, LN_B + t:LN_B + t + 1], ALU.mult, ALU.add)
                    last.then_inc(ln_ready, 1)

                def silu():
                    dve.wait_ge(silu_sig, layer + 1)
                    nc.vector.tensor_tensor(act_in[:, :, :], act_in[:, :, :], z[:, CG0:CG0 + 4, :], ALU.mult).then_inc(conv_act, 1)

                before, after = ada_pair(0, ADA_QKV + 6) if first else ({}, {})
                for j, f in ((1, center), (1, pool_means), (3, variance), (4, layer_norm), (5, silu)):
                    before[j] = [f] + list(before.get(j, []))
                eight_units(quad(layer, Q_IN + 10), before, after)

                swap = [p ^ 16 for p in range(32)]

                def rope(a, b, scratch):
                    zz, rr = z[:, a:b, CTX:TOK], scratch[:, 0:b - a, :]
                    return (lambda: chain.link(nc.vector.stream_shuffle(rr, zz, swap)),
                            lambda: chain.link(nc.vector.tensor_tensor(rr, rr, per_token(sin_t, b - a, 0, LAT), ALU.mult)),
                            lambda: chain.link(nc.vector.tensor_tensor(zz, zz, per_token(cos_t, b - a, 0, LAT), ALU.mult)),
                            lambda: chain.link(nc.vector.tensor_tensor(zz, zz, rr, ALU.add)))

                dve.wait_ge(rope_landed, 48 * (layer + 1))
                dve.wait_ge(kv_turned, layer + 1)
                for op in rope(K0, K0 + 2, rot):
                    op()
                kdv = kd[:, :, :].rearrange("p (t s) n -> p t s n", s=2)
                for a in range(2):
                    for b in range(2):
                        nc.vector.tensor_copy(kdv[64 * b:64 * b + 64, :, a, 0:TOK], z[64 * a:64 * a + 64, K0:K0 + 2, :])
                for g in range(4):
                    dve.wait_ge(pool_hi, 4 * layer + g + 1)
                    nc.vector.scalar_tensor_tensor(out=h_lo[:, 8 + g, :], in0=ps[:, g, 0:TOK],
                                                   scalar=pa[:, layer, POOL_S + g:POOL_S + g + 1],
                                                   in1=h_hi[:, 8 + g, :].bitcast(F32), op0=ALU.mult, op1=ALU.subtract).then_inc(pool_done, 1)
                for op in rope(Q0, Q0 + 4, rot):
                    op()
                late_rope = rope(Q0 + 4, Q0 + 8, rot2)
                dve.wait_ge(ck_turned, layer + 1)
                for a in range(2):
                    for b in range(2):
                        last = nc.vector.tensor_copy(kdv[64 * b:64 * b + 64, :, a, TOK:512],
                                                     ps[64 * a:64 * a + 64, BANK_MOD, 256:512].rearrange("p (t n) -> p t n", n=P))
                last.then_inc(kd_ready, 1)
                for t in range(4):
                    dve.wait_ge(pw_hi, 4 * layer + t + 1)
                    nc.vector.tensor_tensor(h_lo[:, 12 + t, :], ps[:, t, 0:TOK], h_hi[:, 12 + t, :].bitcast(F32), ALU.subtract).then_inc(pw_done, 1)

                done = layer * len(STEPS)

                def stats(s):
                    pair, what = STEPS[s]
                    k = s % 2
                    dve.wait_ge(s_ready, done + s + 1)
                    n = TOK if what else CTX
                    if what:
                        m = ps[:, 2:4, (P if what == 1 else 0):][:, :, 0:P]
                        chain.link(nc.vector.tensor_tensor(m, m, masks[:, what - 1, :].unsqueeze(1).to_broadcast([P, 2, P]), ALU.add))
                    chain.link(nc.vector.reduce_max(row_max[:, k, :], ps[:, 2:4, 0:n], AX_X))
                    chain.link(nc.vector.scalar_tensor_tensor(out=nbias[:, k, :], in0=row_max[:, k, :], scalar=-SCALE,
                                                              in1=nsinks[:, layer, 2 * pair:2 * pair + 2], op0=ALU.mult, op1=ALU.min))
                    nc.vector.tensor_tensor(sink_in[:, k, :], nbias[:, k, :], sinks[:, layer, 2 * pair:2 * pair + 2], ALU.add).then_inc(nb_ready, 1)

                def denominator(s):
                    k = s % 2
                    dve.wait_ge(p_ready, done + s + 1)
                    chain.link(nc.vector.tensor_tensor(row_sum[:, k, :], row_sum[:, k, :], sink_e[:, k, :], ALU.add))
                    nc.vector.reciprocal(rden[:, k, :], row_sum[:, k, :]).then_inc(rden_ready, 1)

                def turned_out(s):
                    pair, what = STEPS[s]
                    dve.wait_ge(t_ready, done + s + 1)
                    if what:
                        nc.vector.tensor_copy(prob_t[:, s % 2, 0:2, :], ps[:, 4, :].rearrange("p (b n) -> p b n", n=256))
                        nc.vector.tensor_copy(prob_t[:, s % 2, 2, :], ps[:, 5, 0:256]).then_inc(pt_ready, 1)
                    else:
                        nc.vector.tensor_copy(prob_t[:, s % 2, 0, :], ps[:, 4, 0:256]).then_inc(pt_ready, 1)

                def out_low(s):
                    pair, what = STEPS[s]
                    dve.wait_ge(o_hi, done + s + 1)
                    cols = slice(P * what, P * what + P)
                    nc.vector.tensor_tensor(h_lo[:, pair, cols], ps[:, BANK_MOD, 256:384], h_hi[:, pair, cols].bitcast(F32),
                                            ALU.subtract).then_inc(o_done, 1)

                def side_low(s):
                    u = 2 * STEPS[s][0] + STEPS[s][1] - 1
                    w_low(u % 4, quad(layer, Q_OUT + 1) + u // 4)

                for s in range(len(STEPS) + 1):
                    what = STEPS[s][1] if s < len(STEPS) else 0
                    m = ADA_MIX + 2 * (s // 3) + (0 if what == 1 else -1)
                    ada = first and s and what != 2
                    if s == 2:
                        dve.wait_ge(kv_out, 32 * (layer + 1))
                    if ada and not what:
                        ada_copy(m)
                    late = what == 1 or (what == 2 and not first)
                    if s and not late:
                        turned_out(s - 1)
                    if what == 2:
                        side_low(s - 1)
                    if s < len(STEPS):
                        stats(s)
                    if ada and what:
                        ada_copy(m)
                    if late:
                        turned_out(s - 1)
                    if s < len(STEPS):
                        denominator(s)
                    if ada:
                        ada_mods(0, m, m)
                    if s in (4, 5, 7, 8):
                        late_rope[(4, 5, 7, 8).index(s)]()
                    if s == 8:
                        nc.vector.memset(rden[:, 1, :], 0.0).then_inc(kd_ready, 1)
                    if s:
                        out_low(s - 1)
                    if s and not what:
                        side_low(s - 1)

                with dve.Fori(0, 2) as i:
                    eight_units(quad(layer, Q_OUT + 4) + i * 2, *(ada_pair(0, i * 2 + ADA_OUT) if first else ()))
                dve.wait_ge(mods_ready, n_mods + ADA_BLOCKS)
                gate_coef(1, layer, G1, G_POST1)
                scale_coef(2, layer, SC2, G_PRE2)
                gate_coef(3, layer, G2, G_POST2)
                inverse_root(4 * layer + 1)
                residual(2 * layer, 1)
                inverse_root(4 * layer + 2)
                dve.wait_ge(x_updated, 8 * (2 * layer + 1))
                build_h(2 * layer + 1, layer, 2, SH2)

                def hidden_low(tile, n):
                    dve.wait_ge(hidh_ready, n + 1)
                    dve.wait_ge(sqh_ready, n + 2)
                    nc.vector.tensor_tensor(hid_lo[:, bass.ds(tile, 2), :], z[:, 18:20, :], hid_hi[:, bass.ds(tile, 2), :].bitcast(F32),
                                            ALU.subtract).then_inc(hid_ready, 1)

                def up(ch, q):
                    with dve.Fori(0, 2) as i:
                        before, after = ada_pair(1, ch * 6 + i * 2) if first else ({}, {})
                        n = ch * 4 + i * 2 + 32 * layer
                        after[3] = [lambda: hidden_low(i * 4, n)]
                        after[7] = [lambda: hidden_low(i * 4 + 2, n + 1)] + list(after.get(7, []))
                        eight_units(q + i * 2, before, after)

                def down(ch, q, i, prefetch=8):
                    m = ch * 6 + i + 4
                    n = m + ADA_BLOCKS
                    before = {4: [lambda: ada_copy(n)], 6: [lambda: ada_mods(1, m, n)]} if first else {}
                    eight_units(q + 4 + i * 2, before, {}, prefetch)

                last_layer = layer == DEPTH - 1
                with dve.Fori(0, CHUNKS - 1 if last_layer else CHUNKS) as ch:
                    q = quad(layer, Q_MLP) + ch * Q_CHUNK
                    up(ch, q)
                    with dve.Fori(0, 2) as i:
                        down(ch, q, i)
                if last_layer:
                    ch, q = CHUNKS - 1, quad(layer, Q_MLP) + (CHUNKS - 1) * Q_CHUNK
                    up(ch, q)
                    down(ch, q, 0)
                    down(ch, q, 1, prefetch=4)
                inverse_root(4 * layer + 3)
                residual(2 * layer + 1, 3)
                dve.wait_ge(x_updated, 8 * (2 * layer + 2))

        @block.tensor
        def _(pe):
            def unit(j, q, pair, kt, hi, lo, begin, end):
                pe.wait_ge(lo_ready, 4 * q + (j + 1))
                for k in range(4):
                    for t in range(2):
                        for i, (w, v) in enumerate(((w_hi, hi), (w_hi, lo), (w_lo, hi))):
                            last = nc.tensor.matmul(ps[:, 2 * pair + t, 0:TOK], w[:, j % 4, k, P * t:P * t + P], v[:, kt + k, :],
                                                    start=begin and k == 0 and i == 0, stop=end and k == 3 and i == 2)
                last.then_inc(unit_used, 1)

            def ada_unit(n, j):
                pe.wait_ge(ada_landed[j], 16 * (n + 1))
                if j == 0 and not (isinstance(n, int) and n == 0):
                    pe.wait_ge(ada_copied, n)
                for g in range(4):
                    last = nc.tensor.matmul(ps[32 * g:32 * g + 32, BANK_ADA, 0:UC], cond[:, 4 * j + g, :], ada_raw[:, j, g, :],
                                            start=j == 0, stop=j == 3)
                last.then_inc(ada_used, 1)

            def ada_turn(n):
                pe.wait_ge(ada_copied, n + 1)
                if not (isinstance(n, int) and n == 0):
                    pe.wait_ge(mods_ready, n)
                for t in range(2):
                    last = nc.tensor.matmul(ps[:, BANK_MOD, 2 * t:2 * t + 2], ada_s[:, P * t:P * t + P], sel[:, :],
                                            start=True, stop=True)
                last.then_inc(ada_turned, 1)

            def ada_beside(m, j):
                if j == 3:
                    ada_turn(m)
                for n, u in {0: ((0, 0), (0, 1)), 1: ((0, 2),), 2: ((0, 3),), 3: ((1, 0),), 4: ((1, 1),),
                             5: ((1, 2),), 6: ((1, 3),), 7: ()}[j]:
                    ada_unit(m + n, u)
                if j == 7:
                    ada_turn(m + 1)

            def two_blocks(q, b, ada=None, h_base=None, after=None):
                for j in range(8):
                    if j % 4 == 0 and not (isinstance(b, int) and b + j // 4 <= 1):
                        pe.wait_ge(acc_free, b + (j // 4 - 1))
                    if h_base is not None and j < 4:
                        pe.wait_ge(h_ready, h_base + 2 * j + 2)
                    unit(j, q, j // 4, 4 * (j % 4), h_hi, h_lo, j % 4 == 0, j % 4 == 3)
                    if ada is not None:
                        ada_beside(ada, j)
                    if after and j in after:
                        after[j]()

            def sum_pair(n, i):
                pe.wait_ge(sq_ready, 8 * n + i + 1)
                for t in range(2):
                    last = nc.tensor.matmul(ps[:, BANK_SUM, 0:TOK], ones[:, :], z[:, 20 + 2 * (i % 2) + t, :],
                                            start=i == 0 and t == 0, stop=i == 7 and t == 1)
                last.then_inc(sq_used, 1)

            def sum_squares(n):
                for i in range(8):
                    sum_pair(n, i)

            pe.wait_ge(consts_ready, 5)
            pe.wait_ge(rows_landed, 16 * 12 * DEPTH)
            for layer in range(DEPTH):
                for i, n in enumerate((112, 96, 124)):
                    last = nc.tensor.transpose(ps[:, layer, P * i:P * i + n], rows[0:n, 3 * layer + i, :], ident[0:n, 0:n])
            last.then_inc(rows_turned, 1)
            pe.wait_ge(x_landed, 32)
            for g in range(12):
                b, j = divmod(g, 4)
                if g >= 2:
                    pe.wait_ge(x_copied, g - 1)
                for t in range(4):
                    last = nc.tensor.transpose(ps[:, 2 + g % 2, P * t:P * t + P], staged[:, b, P * (4 * j + t):P * (4 * j + t + 1)], ident[:, :])
                last.then_inc(x_turned, 1)
            pe.wait_ge(cond_ready, 1)
            for m in range(8):
                for j in range(4):
                    ada_unit(m, j)
                sum_pair(0, m)
                ada_turn(m)
            with pe.Fori(8, ADA_CU) as m:
                for j in range(4):
                    ada_unit(m, j)
                ada_turn(m)

            for layer in range(DEPTH):
                first = layer == 0
                if first:
                    two_blocks(0, 0, ADA_CU, 0)
                    two_blocks(2, 2, ADA_CU + 2)
                else:
                    sum_squares(4 * layer)
                    with pe.Fori(0, 2) as i:
                        two_blocks(quad(layer, Q_IN) + i * 2, blk(layer, B_IN) + i * 2, None, 16 * layer)
                with pe.Fori(0, 3) as i:
                    two_blocks(quad(layer, Q_IN + 4) + i * 2, blk(layer, B_IN + 4) + i * 2, i * 2 + ADA_QKV if first else None)

                def ln_sums():
                    pe.wait_ge(conv_ready, 2 * (layer + 1))
                    for a, b, src in ((0, CTX, 0), (CTX, TOK, CONV_LAT)):
                        for t in range(4):
                            last = nc.tensor.matmul(ps[:, BANK_SUM, a:b], ones[:, :], conv[:, t, src:src + b - a], start=t == 0, stop=t == 3)
                    last.then_inc(ln_sum, 1)

                def ln_squares():
                    pe.wait_ge(csq_ready, layer + 1)
                    for t in range(4):
                        last = nc.tensor.matmul(ps[:, BANK_VAR, 0:TOK], ones[:, :], z[:, CG0 + t, :], start=t == 0, stop=t == 3)
                    last.then_inc(csq_used, 1)

                two_blocks(quad(layer, Q_IN + 10), blk(layer, B_IN + 10), ADA_QKV + 6 if first else None,
                           after={0: ln_sums, 2: ln_squares})
                pe.wait_ge(lnv_ready, layer + 1)
                for i in range(2):
                    for b in range(3):
                        nc.tensor.transpose(ps[:, 4 + b // 2, 256 * (b % 2) + P * i:256 * (b % 2) + P * i + P],
                                            z[:, V0 + i, P * b:P * b + P], ident[:, :])
                    last = nc.tensor.transpose(ps[:, 5, 256 + P * i:256 + P * i + P], z[:, K0 + i, 0:P], ident[:, :])
                last.then_inc(kv_turned, 1)
                pe.wait_ge(pooled, layer + 1)
                pe.wait_ge(conv_w_landed, 32 * (layer + 1))
                for g in range(4):
                    pe.wait_ge(acc_free, blk(layer, B_OUT) - (1 if g < 2 else 0))
                    nc.tensor.matmul(ps[:, g, 0:TOK], pool_w[:, g, :], z[:, PU0 + g, :], start=True, stop=True).then_inc(pool_mm, 1)
                pe.wait_ge(rope_landed, 48 * (layer + 1))
                pe.wait_ge(mods_ready, ADA_MIX if first else DEPTH * ADA_BLOCKS)
                for i in range(2):
                    last = nc.tensor.transpose(ps[:, BANK_MOD, 256 + P * i:256 + P * i + P], ck[:, P * i:P * i + P], ident[:, :])
                last.then_inc(ck_turned, 1)
                pe.wait_ge(conv_act, layer + 1)
                for t in range(4):
                    pe.wait_ge(pool_done, 4 * layer + t + 1)
                    for k in range(4):
                        last = nc.tensor.matmul(ps[:, t, 0:TOK], pw_w[:, k, P * t:P * t + P], act_in[:, k, :], start=k == 0, stop=k == 3)
                    last.then_inc(pw_ready, 1)

                done = layer * len(STEPS)

                def scores(s):
                    pair, what = STEPS[s]
                    a, b = (TOK - LAT, 512) if what else (0, CTX)
                    if s:
                        pe.wait_ge(p_ready, done + s)
                    for e in range(2):
                        half = slice(64 * e, 64 * e + 64)
                        last = nc.tensor.matmul(ps[:, 2 + e, 0:b - a], z[half, pair, P * what:P * what + P],
                                                kd[half, pair // 2, a:b], start=True, stop=True)
                    last.then_inc(s_ready, 1)

                def turn(s):
                    pair, what = STEPS[s]
                    pe.wait_ge(pn_ready, done + s + 1)
                    if done + s >= 1:
                        pe.wait_ge(pt_ready, done + s)
                    for kb in range(3 if what else 1):
                        for e in range(2):
                            o = 256 * (kb % 2) + P * e
                            last = nc.tensor.transpose(ps[:, 4 + kb // 2, o:o + P], prob[:, s % 2, e, P * kb:P * kb + P], ident[:, :])
                    last.then_inc(t_ready, 1)

                def mix(s):
                    pair, what = STEPS[s]
                    kv = pair // 2
                    blocks = (1, 2, 3) if what else (0,)
                    pe.wait_ge(pt_ready, done + s + 1)
                    if done + s >= 1:
                        pe.wait_ge(o_done, done + s)
                    if first:
                        pe.wait_ge(mods_ready, ADA_MIX + 2 * ((s + 1) // 3) + min((s + 1) % 3, 1))
                    for e in range(2):
                        for i, vb in enumerate(blocks):
                            last = nc.tensor.matmul(ps[64 * e:64 * e + 64, BANK_MOD, 256:384], vt[:, vb, HD * kv:HD * kv + HD],
                                                    prob_t[:, s % 2, i, P * e:P * e + P], start=i == 0, stop=i == len(blocks) - 1)
                    last.then_inc(o_ready, 1)

                def side_unit(s):
                    u = 2 * STEPS[s][0] + STEPS[s][1] - 1
                    if u % 2 == 0:
                        pe.wait_ge(acc_free, blk(layer, B_OUT) + u // 2)
                    unit(u % 4, quad(layer, Q_OUT) + u // 4, 0, 8 + 4 * (u % 2), h_hi, h_lo, u % 2 == 0, u % 2 == 1)

                pe.wait_ge(kd_ready, 2 * layer + 1)
                pe.wait_ge(pw_done, 4 * (layer + 1))
                pe.wait_ge(v_ready, 2 * (layer + 1))
                pe.wait_ge(cachev_landed, 16 * (layer + 1))
                for s in range(len(STEPS) + 1):
                    what = STEPS[s][1] if s < len(STEPS) else 0
                    m = ADA_MIX + 2 * (s // 3)
                    if s == 12:
                        pe.wait_ge(kd_ready, 2 * layer + 2)
                    late = what == 1 or (what == 2 and not first)
                    if s and not late:
                        turn(s - 1)
                    if s < len(STEPS):
                        scores(s)
                    if late:
                        turn(s - 1)
                    if what:
                        side_unit(s)
                    if first and s >= 2:
                        pe.wait_ge(o_done, done + s - 1)
                    if first and what == 1:
                        ada_turn(m)
                    if first and s < len(STEPS):
                        for block, k in (((m, 0), (m, 1), (m, 2), (m, 3)), ((m + 1, 0), (m + 1, 1)), ((m + 1, 2), (m + 1, 3)))[what]:
                            ada_unit(block, k)
                    if first and s and not what:
                        ada_turn(m - 1)
                    if s:
                        mix(s - 1)
                with pe.Fori(0, 2) as i:
                    q, b = quad(layer, Q_OUT + 4) + i * 2, blk(layer, B_OUT + 8) + i * 4
                    for j in range(8):
                        if j % 2 == 0:
                            pe.wait_ge(acc_free, b + (j // 2 - 1))
                        if j < 2:
                            pe.wait_ge(o_done, done + 12 * (j + 1))
                        unit(j, q, (j // 2 + 1) % 2, 4 * (j % 2), h_hi, h_lo, j % 2 == 0, j % 2 == 1)
                        if first:
                            ada_beside(i * 2 + ADA_OUT, j)
                sum_squares(4 * layer + 1)
                sum_squares(4 * layer + 2)
                with pe.Fori(0, CHUNKS) as ch:
                    q, b = quad(layer, Q_MLP) + ch * Q_CHUNK, blk(layer, B_MLP) + ch * B_CHUNK
                    with pe.Fori(0, 2) as i:
                        two_blocks(q + i * 2, b + i * 2, ch * 6 + i * 2 + ADA_BLOCKS if first else None, 16 * layer + 8)
                    with pe.Fori(0, 2) as i:
                        n = ch * 6 + i + (4 + ADA_BLOCKS)
                        for j in range(8):
                            if j % 2 == 0:
                                pe.wait_ge(acc_free, b + i * 4 + (4 + j // 2 - 1))
                            if j < 2:
                                pe.wait_ge(hid_ready, ch * 4 + (32 * layer + 1 + 2 * (j + 1)))
                            unit(j, q + 4 + i * 2, j // 2 % 2, 4 * (j % 2), hid_hi, hid_lo, j % 2 == 0, j % 2 == 1)
                            if first and j < 4:
                                ada_unit(n, j)
                            if first and j == 5:
                                ada_turn(n)
                sum_squares(4 * layer + 3)
            pe.wait_ge(x_updated, 32)
            for g in range(12):
                b, j = divmod(g, 4)
                if g >= 4:
                    pe.wait_ge(y_copied, g - 3)
                for t in range(4):
                    last = nc.tensor.transpose(ps[:, g % 4, P * t:P * t + P], x[:, 4 * j + t, P * b:P * b + P], ident[:, :])
                last.then_inc(y_turned, 1)


_INS = ["x_prompt", "x_sample", "cache_k", "cache_v", "c", "c_ctx", "w_ada", "b_ada", "g_pre1", "g_post1", "g_pre2",
        "g_post2", "w_in", "sink", "w_pool", "pool_scale", "conv_dw", "conv_b", "conv_ln_g", "conv_ln_b", "w_conv_pw",
        "w_out", "w_mlp1", "w_mlp2"]
_OUTS = [(1, CTX, D), (1, LAT, D), (1, DEPTH, CTX, KV_HEADS, HD), (1, DEPTH, CTX, KV_HEADS, HD)]


def shape_tables():
    import numpy as np

    grid_w, quarter = 64, HD // 4
    inv_freq = (1.0 / (np.float32(10000.0) ** (np.arange(quarter, dtype=np.float32) / np.float32(quarter)))).astype(np.float32)
    token = np.arange(LAT)
    pos = np.stack([token // grid_w, token % grid_w]).astype(np.float32)
    cos, sin = np.empty((P, LAT), np.float32), np.empty((P, LAT), np.float32)
    for p in range(P):
        angle = pos[p % HD // (HD // 2)] * inv_freq[p % quarter]
        cos[p] = np.cos(angle)
        sin[p] = np.sin(angle) * (-1 if p % (2 * quarter) < quarter else 1)
    edge = np.ones((4, 2, 2, P_HALF), np.float32)
    for g, w in enumerate(POOL_WINDOWS):
        for s, length in enumerate((CTX, LAT)):
            for e, first in enumerate((0, length - P_HALF)):
                t = first + np.arange(P_HALF)
                edge[g, s, e] = w / (np.clip(t - w // 2 + w, 0, length) - np.clip(t - w // 2, 0, length))
    return {"rope_cos": cos, "rope_sin": sin, "pool_edge": edge}


def kernel(**inputs):
    import numpy as _np
    import concourse.bacc as _bacc
    from concourse import mybir as _mybir
    from concourse.bass_utils import run_bass_kernel_spmd as _run

    nc = _bacc.Bacc("TRN2", target_bir_lowering=False, num_devices=1)
    arrays, args = {}, []
    for name, a in [(n, inputs[n]) for n in _INS] + list(shape_tables().items()):
        a = _np.ascontiguousarray(a)
        arrays[f"in_{name}_dram"] = a
        args.append(nc.dram_tensor(f"in_{name}_dram", a.shape, _mybir.dt.from_np(a.dtype), kind="ExternalInput").ap())
    for i, shape in enumerate(_OUTS):
        args.append(nc.dram_tensor(f"out_{i}_dram", shape, _mybir.dt.float32, kind="ExternalOutput").ap())
    backbone(nc, *args)
    r = _run(nc, [arrays], core_ids=[0])
    return tuple(r.results[0][f"out_{i}_dram"] for i in range(len(_OUTS)))
```

```python
from contextlib import ExitStack

import concourse.bass as bass
from concourse import mybir

F32 = mybir.dt.float32
F32R = mybir.dt.float32r
ALU = mybir.AluOpType
ACT = mybir.ActivationFunctionType
AX_X = mybir.AxisListType.X

P = 128
D = 2048
DEPTH = 2
CTX, LAT = 128, 256
TOK = CTX + LAT
GROUPS = ((0, 0, CTX), (1, CTX, TOK))
DT = D // P
HD = 64
HEADS, KV_HEADS = 16, 4
D_FF = 4 * D
TAPS = 31
POOL_WINDOWS = (2, 4, 8, 16)
EPS = 1e-6
SCALE = HD ** -0.5

Q0, K0, V0, PU0, CA0, CG0 = 0, 8, 10, 12, 16, 20

SLOTS = 4
UC = 256
CHUNK = 8
CHUNKS = D_FF // P // CHUNK

Q_IN, Q_OUT, Q_MLP = 0, 12, 20
Q_CHUNK = 8
Q_LAYER = Q_MLP + CHUNKS * Q_CHUNK
B_IN, B_OUT, B_MLP = 0, 12, 28
B_CHUNK = 12
B_LAYER = B_MLP + CHUNKS * B_CHUNK

ADA_BLOCKS = 6 * D // UC
SH1, SC1, G1, SH2, SC2, G2 = (DT * i for i in range(6))
ADA_CU, ADA_QKV, ADA_MIX, ADA_OUT = 16, 20, 28, 44

ADA_OF_QUAD = {1: 0, 2: 1, 3: 2, 5: 3, 6: 4, 7: 5}

C_HALF = TAPS // 2
CONV_PAD = C_HALF + CTX + 2 * C_HALF + LAT + C_HALF
CONV_LAT = CTX + 2 * C_HALF
CONV_OUT = CONV_LAT + LAT
P_HALF = max(POOL_WINDOWS) // 2
POOL_PAD = P_HALF + CTX + 2 * P_HALF + LAT + P_HALF
POOL_LAT = P_HALF + CTX + 2 * P_HALF

BANK_SUM, BANK_VAR, BANK_ADA, BANK_MOD = 4, 5, 6, 7

G_PRE1, G_POST1, G_PRE2, G_POST2 = 0, 16, 32, 48
POOL_S, CONV_B, LN_G, LN_B = 64, 68, 72, 76
ROWS_A = 80

STEPS = [(pair, what) for pair in range(HEADS // 2) for what in range(3)]


class Chain:

    def __init__(self, engine, sem):
        self.engine, self.sem, self.n = engine, sem, 0

    def mark(self, instruction):
        instruction.then_inc(self.sem, 1)
        self.n = self.n + 1
        return self.n

    def wait(self, mark):
        self.engine.wait_ge(self.sem, mark)

    def link(self, instruction):
        self.wait(self.mark(instruction))


def backbone(nc, x_prompt, x_sample, cache_k, cache_v, c, c_ctx, w_ada, b_ada, g_pre1, g_post1, g_pre2,
             g_post2, w_in, sink, w_pool, pool_scale, conv_dw, conv_b, conv_ln_g, conv_ln_b, w_conv_pw,
             w_out, w_mlp1, w_mlp2, rope_cos, rope_sin, pool_edge, y_prompt, y_sample, new_k, new_v):
    ctx = ExitStack()
    with ctx:
        def sem(name):
            return ctx.enter_context(nc.semaphore(name))

        base = -(-nc.sbuf_base // 32) * 32
        arena_bytes = nc.sbuf_bytes_remaining // 32 * 32 - 32
        ctx.enter_context(nc.sbuf_tensor("arena", [P, arena_bytes // 4], F32))
        top = [0]

        def at(name, shape, dt, offset):
            return nc.alloc_sbuf_tensor_at(name, [P, *shape], dt, offset=base + offset)

        def new(name, shape, dt=F32):
            size = 4
            for n in shape:
                size *= n
            t = at(name, shape, dt, top[0])
            top[0] += -(-size // 32) * 32
            assert top[0] <= arena_bytes, (name, top[0], arena_bytes)
            return t

        x = new("x", [DT, TOK])
        h_hi = new("h_hi", [DT, TOK], F32R)
        h_lo = new("h_lo", [DT, TOK], F32R)
        z_at = top[0]
        z = new("z", [24, TOK])
        t_at = top[0]
        full = new("full", [DT, TOK])
        hid_hi = at("hid_hi", [CHUNK, TOK], F32R, t_at)
        hid_lo = at("hid_lo", [CHUNK, TOK], F32R, t_at + 4 * CHUNK * TOK)
        raw = new("raw", [SLOTS, 4, UC])
        w_hi = new("w_hi", [SLOTS, 4, UC], F32R)
        w_lo = new("w_lo", [SLOTS, 4, UC], F32R)
        ada_raw = new("ada_raw", [SLOTS, 4, UC])
        ident = new("ident", [P])
        ones = new("ones", [P])
        sel = new("sel", [2])
        cond = new("cond", [DT, 32])
        mods = new("mods", [DEPTH, 6 * DT, 2])
        sums_at = top[0]
        ada_sums = new("ada_sums", [2, 2, UC])
        rstd = at("rstd", [TOK], F32, sums_at)
        ada_s = at("ada_s", [UC], F32, sums_at + 4 * TOK)
        masks = at("masks", [2, P], F32, sums_at + 4 * (TOK + UC))
        pa = new("pa", [DEPTH, ROWS_A])
        pb = new("pb", [DEPTH, 6 * DT])
        pc = new("pc", [DEPTH, 4 * TAPS])
        coef = new("coef", [4, DT, 2])
        sinks = new("sinks", [DEPTH, HEADS])
        nsinks = new("nsinks", [DEPTH, HEADS])
        row_max = new("row_max", [2, 2])
        nbias = new("nbias", [2, 2])
        sink_in = new("sink_in", [2, 2])
        sink_e = new("sink_e", [2, 2])
        row_sum = new("row_sum", [2, 2])
        rden = new("rden", [2, 2])

        def t_off(n):
            return t_at + 4 * n

        prob_n = 2 * 2 * TOK
        glu = at("glu", [4, CONV_PAD], F32, t_off(0))
        conv = at("conv", [4, CONV_OUT], F32, t_off(4 * CONV_PAD))
        centered_sq = at("centered_sq", [4, TOK], F32, t_off(4 * CONV_PAD))
        act_in = at("act_in", [4, TOK], F32, t_off(0))
        rot = at("rot", [4, LAT], F32, t_off(prob_n))
        ck = at("ck", [256], F32, t_off(prob_n + 4 * LAT))
        k_out = at("k_out", [256], F32, t_off(prob_n + 4 * LAT + 256))
        cos_t = at("cos_t", [LAT], F32, t_off(2 * prob_n))
        sin_t = at("sin_t", [LAT], F32, t_off(2 * prob_n + LAT))
        o_pw = 2 * prob_n + 512
        assert 4 * CONV_PAD + 4 * CONV_OUT <= o_pw and o_pw + 2560 <= DT * TOK
        pw_w = at("pw_w", [4, 512], F32, t_off(o_pw))
        pool_w = at("pool_w", [4, P], F32, t_off(o_pw + 2048))
        rot2 = at("rot2", [4, LAT], F32, t_off(o_pw))
        prob = at("prob", [2, 2, TOK], F32, t_off(0))
        prob_t = at("prob_t", [2, 3, 256], F32, t_off(prob_n))
        mix_t = at("mix_t", [8, TOK], F32, t_off(2 * prob_n))
        pool_a = at("pool_a", [4, POOL_PAD], F32, z_at + 4 * 16 * TOK)
        edge = at("edge", [4, 2, 2, P_HALF], F32, z_at + 4 * (16 * TOK + 4 * POOL_PAD))
        pool_b = at("pool_b", [TOK + 96], F32, z_at + 4 * 22 * TOK)
        conv_odd = at("conv_odd", [1, CONV_OUT], F32, z_at + 4 * (16 * TOK + 4 * POOL_PAD + 128))
        conv_p0 = at("conv_p0", [CONV_OUT], F32, z_at + 4 * 16 * TOK)
        conv_p1 = at("conv_p1", [CONV_OUT], F32, z_at + 4 * (16 * TOK + 416))
        assert 4 * POOL_PAD + 128 + CONV_OUT <= 6 * TOK and POOL_PAD <= TOK + 96
        kd = at("kd", [KV_HEADS, 512], F32, z_at + 4 * 16 * TOK)
        vt = at("vt", [4, 256], F32, z_at + 4 * (16 * TOK + 2048))
        staged = at("staged", [3, D], F32, z_at)
        rows = at("rows", [6, P], F32, z_at + 4 * 16 * TOK)
        cond_t = at("cond_t", [2, 2 * DT], F32, z_at + 4 * 18 * TOK)
        c_rows = at("c_rows", [P], F32, z_at + 4 * 19 * TOK)
        y_rows = at("y_rows", [3, D], F32, t_off(0))

        ps = ctx.enter_context(nc.psum_tensor("ps", [P, 8, 512], F32))

        def sems(names):
            return [sem(n) for n in names.split()]

        raw_landed = [sem(f"raw_landed{s}") for s in range(SLOTS)]
        ada_landed = [sem(f"ada_landed{s}") for s in range(SLOTS)]
        hi_ready, lo_ready, unit_used, acc_free = sems("hi_ready lo_ready unit_used acc_free")
        ada_used, ada_copied, ada_turned, mods_ready = sems("ada_used ada_copied ada_turned mods_ready")
        rows_landed, sinks_landed, x_landed, consts_ready = sems("rows_landed sinks_landed x_landed consts_ready")
        rows_turned, cond_raw, cond_sig, cond_ready, x_turned, x_copied = sems(
            "rows_turned cond_raw cond_sig cond_ready x_turned x_copied")
        sq_ready, sq_used, var_ready, std_ready = sems("sq_ready sq_used var_ready std_ready")
        x_updated, full_ready, h_hi_ready, h_ready = sems("x_updated full_ready h_hi_ready h_ready")
        conv_w_landed, pads_ready, sig_ready, conv_ready, ln_sum, cen_ready, csq_ready, csq_used = sems(
            "conv_w_landed pads_ready sig_ready conv_ready ln_sum cen_ready csq_ready csq_used")
        glu_ready, edge_landed, mix_added = sems("glu_ready edge_landed mix_added")
        masks_ready = sem("masks_ready")
        psq_ready, psq_added, psq_summed, rstd_ready, z_scaled, x_scaled = sems(
            "psq_ready psq_added psq_summed rstd_ready z_scaled x_scaled")
        lnv_ready, lnstd_ready, ln_ready, silu_sig, conv_act, pw_ready, pw_hi, pw_done = sems(
            "lnv_ready lnstd_ready ln_ready silu_sig conv_act pw_ready pw_hi pw_done")
        pool_summed, pooled, pool_mm, pool_hi, pool_done = sems("pool_summed pooled pool_mm pool_hi pool_done")
        rope_landed, cachev_landed, kv_turned, v_ready, ck_turned, kd_ready, kv_out = sems(
            "rope_landed cachev_landed kv_turned v_ready ck_turned kd_ready kv_out")
        s_ready, nb_ready, p_ready, rden_ready, pn_ready, t_ready, pt_ready, o_ready, o_hi, o_done = sems(
            "s_ready nb_ready p_ready rden_ready pn_ready t_ready pt_ready o_ready o_hi o_done")
        sqh_ready, hidh_ready, hid_ready, added = sems("sqh_ready hidh_ready hid_ready added")
        y_turned, y_copied, y_stored, c_landed, c_turned = sems("y_turned y_copied y_stored c_landed c_turned")
        dve_chain, pool_chain = sems("dve_chain pool_chain")

        def quad(layer, phase):
            return layer * Q_LAYER + phase

        def blk(layer, phase):
            return layer * B_LAYER + phase

        def per_token(t, n, lo=0, hi=TOK):
            return t[:, lo:hi].unsqueeze(1).to_broadcast([P, n, hi - lo])

        block = ctx.enter_context(nc.Block())

        @block.sync
        def _(sp):
            def load_unit(j, q, src, wait=True):
                if wait:
                    sp.wait_ge(lo_ready, 4 * q + j - 3)
                sp.dma_start(raw[:, j % 4, :, :], src).then_inc(raw_landed[j % 4], 16)

            def load_ada(layer, m, j, wait=True):
                n = layer * ADA_BLOCKS + m
                if wait:
                    sp.wait_ge(ada_used, 4 * n + j - 3)
                src = w_ada[layer, 512 * j:512 * j + 512, bass.ds(m * UC, UC)]
                sp.dma_start(ada_raw[:, j, :, :], src.rearrange("(k p) n -> p k n", p=P)).then_inc(ada_landed[j], 16)

            def part(w, layer, row, col):
                return w[layer, bass.ds(row, 512), bass.ds(col, UC)].rearrange("(k p) n -> p k n", p=P)

            def load_blocks(layer, w, q, col, ada):
                for j in range(8):
                    load_unit(j, q, part(w, layer, 512 * (j % 4), col + UC * (j // 4)))
                    if ada is not None:
                        load_ada(ada[0], ada[1] + j // 4, j % 4)

            for g, w in enumerate((c_ctx, c[0])):
                sp.dma_start(c_rows[DT * g:DT * g + DT, :], w.rearrange("(t p) -> t p", p=P)).then_inc(c_landed, 16)
            sp.dma_start(staged[:, 0, :], x_prompt[0, :, :]).then_inc(x_landed, 16)
            sp.dma_start(staged[:, 1:3, :], x_sample[0, :, :].rearrange("(b p) n -> p b n", p=P)).then_inc(x_landed, 16)
            for j in range(4):
                load_ada(0, 0, j, wait=False)
            for j in range(4):
                load_unit(j, 0, part(w_in, 0, 512 * j, CA0 * P), wait=False)
            with sp.Fori(1, ADA_CU) as m:
                for j in range(4):
                    load_ada(0, m, j)
            for layer in range(DEPTH):
                first = layer == 0
                if first:
                    for j in range(4):
                        load_ada(0, ADA_CU, j)
                    for j in range(4, 8):
                        load_unit(j, 0, part(w_in, 0, 512 * (j - 4), CA0 * P + UC))
                        load_ada(0, ADA_CU + 1, j - 4)
                    load_blocks(0, w_in, 2, CA0 * P + 2 * UC, (0, ADA_CU + 2))
                else:
                    with sp.Fori(0, 2) as i:
                        load_blocks(layer, w_in, quad(layer, Q_IN) + i * 2, CA0 * P + i * 2 * UC, None)
                for k, tile in enumerate((PU0, K0)):
                    load_blocks(layer, w_in, quad(layer, Q_IN + 4) + k * 2, tile * P, (0, ADA_QKV + k * 2) if first else None)
                with sp.Fori(0, 2) as i:
                    load_blocks(layer, w_in, quad(layer, Q_IN + 8) + i * 2, i * 2 * UC,
                                (0, ADA_QKV + 4 + i * 2) if first else None)

                def load_out(i, half, j):
                    load_unit(j, quad(layer, Q_OUT + 4 * half) + i, part(w_out, layer, D // 2 * (1 - half) + 512 * (j % 2),
                                                                        i * (2 * UC) + UC * (j // 2)))

                def load_pair(i, half, j, m):
                    for k in range(4):
                        load_ada(0, m, k)
                    load_out(i, half, j)
                    for k in range(2):
                        load_ada(0, m + 1, k)
                    load_out(i, half, j + 1)
                    for k in range(2, 4):
                        load_ada(0, m + 1, k)

                if first:
                    for j in range(4):
                        load_out(0, 0, j)
                    with sp.Fori(0, 3) as i:
                        load_pair(i + 1, 0, 0, i * 4 + ADA_MIX)
                        load_pair(i + 1, 0, 2, i * 4 + (ADA_MIX + 2))
                    load_pair(0, 1, 0, ADA_MIX + 12)
                    load_pair(0, 1, 2, ADA_MIX + 14)
                    with sp.Fori(0, 3) as i:
                        for j in range(4):
                            load_ada(0, i + ADA_OUT, j)
                            load_out(i + 1, 1, j)
                    for j in range(4):
                        load_ada(0, ADA_OUT + 3, j)
                else:
                    for half in range(2):
                        with sp.Fori(0, 4) as i:
                            for j in range(4):
                                load_out(i, half, j)
                with sp.Fori(0, CHUNKS) as ch:
                    for k in range(Q_CHUNK):
                        q = quad(layer, Q_MLP + k) + ch * Q_CHUNK
                        for j in range(4):
                            if k < 4:
                                src = part(w_mlp1, layer, 512 * j, ch * (CHUNK * P) + UC * k)
                            else:
                                src = part(w_mlp2, layer, ch * (CHUNK * P) + 512 * (j % 2), 2 * UC * (k - 4) + UC * (j // 2))
                            load_unit(j, q, src)
                            if first and k % 4:
                                load_ada(1, ch * 6 + ADA_OF_QUAD[k], j)
            outs = [y_prompt[0, :, :], y_sample[0, 0:P, :], y_sample[0, P:2 * P, :]]
            for g in range(12):
                j, b = divmod(g, 3)
                sp.wait_ge(y_copied, g + 1)
                sp.dma_start(outs[b][:, 512 * j:512 * j + 512], y_rows[:, b, 512 * j:512 * j + 512]).then_inc(y_stored, 16)
            sp.wait_ge(y_stored, 16 * 12)

        @block.gpsimd
        def _(pool):
            chain = Chain(pool, pool_chain)

            nc.gpsimd.memset(ones[:, :], 1.0).then_inc(consts_ready, 1)
            nc.gpsimd.memset(cond[:, :, :], 0.0).then_inc(consts_ready, 1)
            chain.link(nc.gpsimd.memset(ident[:, :], 0.0))
            chain.link(nc.gpsimd.memset(sel[:, :], 0.0))
            for i in range(4):
                chain.link(nc.gpsimd.affine_select(out=sel[:, :], in_=sel[:, :], compare_op=ALU.not_equal, fill=1.0,
                                                   base=-32 * i, pattern=[[-1, 2]], channel_multiplier=1))
            nc.gpsimd.affine_select(out=ident[:, :], in_=ident[:, :], compare_op=ALU.not_equal, fill=1.0, base=0,
                                    pattern=[[-1, P]], channel_multiplier=1).then_inc(consts_ready, 1)
            nc.gpsimd.memset(rden[:, 0, 0:1], 0.0).then_inc(sqh_ready, 1)
            nc.gpsimd.memset(rden[:, 0, 1:2], 0.0).then_inc(hid_ready, 1)
            nc.gpsimd.memset(rden[:, 1, 0:1], 0.0).then_inc(added, 1)
            nc.gpsimd.memset(rden[:, 1, 1:2], 0.0).then_inc(added, 1)

            def scale_rest(n, out, src, signal, first):
                pool.wait_ge(rstd_ready, n + 1)
                for i in range(first, 8):
                    nc.gpsimd.tensor_tensor(out[:, 2 * i:2 * i + 2, :], src[:, 2 * i:2 * i + 2, :], per_token(rstd, 2),
                                            ALU.mult).then_inc(signal, 1)

            def add_squares(u, i):
                pool.wait_ge(psq_ready, 8 * u + i + 1)
                if i > 1:
                    pool.wait_ge(psq_added, 6 * u + i - 1)
                nc.gpsimd.tensor_tensor(z[:, 16:18, :], z[:, 16:18, :], z[:, 18:20, :], ALU.add).then_inc(psq_added, 1)

            for layer in range(DEPTH):
                scale_rest(4 * layer, full, x, x_scaled, 1)
                pool.wait_ge(h_ready, (2 * layer + 1) * 8)
                pool.dma_start(pw_w[:, :, :], w_conv_pw[layer].rearrange("(k p) n -> p k n", p=P)).then_inc(conv_w_landed, 16)
                pool.dma_start(pool_w[:, :, :], w_pool[layer].rearrange("g c d -> c g d")).then_inc(conv_w_landed, 16)
                nc.gpsimd.memset(glu[:, :, 0:C_HALF], 0.0).then_inc(pads_ready, 1)
                nc.gpsimd.memset(glu[:, :, C_HALF + CTX:C_HALF + CONV_LAT], 0.0).then_inc(pads_ready, 1)
                nc.gpsimd.memset(glu[:, :, C_HALF + CONV_OUT:CONV_PAD], 0.0).then_inc(pads_ready, 1)
                pool.wait_ge(mods_ready, ADA_CU if layer == 0 else 2 * ADA_BLOCKS)
                chain.link(nc.gpsimd.memset(masks[:, :, :], 0.0))
                for i in range(2):
                    nc.gpsimd.affine_select(out=masks[:, i, :], in_=masks[:, i, :], compare_op=ALU.is_ge,
                                            fill=-1e30 / SCALE, base=0, pattern=[[2 * i - 1, P]],
                                            channel_multiplier=1 - 2 * i).then_inc(masks_ready, 1)
                pool.wait_ge(glu_ready, layer + 1)
                for k in range(TAPS):
                    src, out, w = glu[:, 3, k:k + CONV_OUT], conv[:, 3, :], pc[:, layer, 4 * k + 3:4 * k + 4]
                    if k == 0:
                        chain.link(nc.gpsimd.tensor_scalar(out, src, w, pa[:, layer, CONV_B + 3:CONV_B + 4], ALU.mult, ALU.add))
                    else:
                        product = (conv_p0, conv_p1)[k % 2]
                        chain.link(nc.gpsimd.tensor_scalar(product[:, :], src, w, None, ALU.mult))
                        chain.mark(nc.gpsimd.tensor_tensor(out, out, product[:, :], ALU.add))
                chain.wait(chain.n)
                pool.dma_start(edge[:, :, :, :], pool_edge.unsqueeze(0).to_broadcast([P, 4, 2, 2, P_HALF])).then_inc(edge_landed, 16)
                nc.gpsimd.memset(pool_a[:, :, 0:P_HALF], 0.0).then_inc(conv_ready, 1)
                nc.gpsimd.memset(pool_a[:, :, P_HALF + CTX:POOL_LAT], 0.0)
                nc.gpsimd.memset(pool_a[:, :, POOL_LAT + LAT:POOL_PAD], 0.0)
                pool.wait_ge(acc_free, blk(layer, 6))
                nc.gpsimd.tensor_copy(pool_a[:, :, P_HALF:P_HALF + CTX], z[:, PU0:PU0 + 4, 0:CTX])
                chain.link(nc.gpsimd.tensor_copy(pool_a[:, :, POOL_LAT:POOL_LAT + LAT], z[:, PU0:PU0 + 4, CTX:TOK]))
                pool.wait_ge(edge_landed, 16 * (layer + 1))
                for g, w in enumerate(POOL_WINDOWS):
                    here, there, span = pool_a[:, g, :], pool_b[:, 0:POOL_PAD], 1
                    while span < w:
                        n = POOL_PAD - 2 * span + 1
                        chain.link(nc.gpsimd.tensor_tensor(there[:, 0:n], here[:, 0:n], here[:, span:span + n], ALU.add))
                        here, there, span = there, here, 2 * span
                    if g % 2 == 0:
                        chain.link(nc.gpsimd.tensor_copy(pool_a[:, g, 0:n], pool_b[:, 0:n]))
                    for s, (start, length) in enumerate(((P_HALF, CTX), (POOL_LAT, LAT))):
                        for e, off in enumerate((0, length - P_HALF)):
                            a = start + off - w // 2
                            chain.link(nc.gpsimd.tensor_tensor(pool_a[:, g, a:a + P_HALF], pool_a[:, g, a:a + P_HALF],
                                                               edge[:, g, s, e, :], ALU.mult))
                nc.gpsimd.memset(pool_b[:, 0:1], 0.0).then_inc(pool_summed, 1)
                pool.wait_ge(csq_used, layer + 1)
                pool.dma_start(cos_t[:, :], rope_cos).then_inc(rope_landed, 16)
                pool.dma_start(sin_t[:, :], rope_sin).then_inc(rope_landed, 16)
                pool.dma_start(ck[:, :], cache_k[0, layer].rearrange("t h d -> t (h d)")).then_inc(rope_landed, 16)
                pool.wait_ge(conv_act, layer + 1)
                pool.dma_start(vt[:, 3, :], cache_v[0, layer].rearrange("t h d -> t (h d)")).then_inc(cachev_landed, 16)
                pool.wait_ge(v_ready, 2 * (layer + 1))
                pool.dma_start(new_k[0, layer].rearrange("t h d -> t (h d)"), k_out[:, :]).then_inc(kv_out, 16)
                pool.dma_start(new_v[0, layer].rearrange("t h d -> t (h d)"), vt[:, 0, :]).then_inc(kv_out, 16)
                for k in range(8):
                    pool.wait_ge(acc_free, blk(layer, B_OUT + 9) + k)
                    dst = z[:, 2 * k:2 * k + 2, :]
                    part = z[:, 2 * k + 8:2 * k + 10, :] if k < 4 else mix_t[:, 2 * k - 8:2 * k - 6, :]
                    nc.gpsimd.tensor_tensor(dst, dst, part, ALU.add).then_inc(mix_added, 1)
                    if k >= 2:
                        add_squares(2 * layer, k - 1)
                scale_rest(4 * layer + 1, z, z, z_scaled, 2)
                scale_rest(4 * layer + 2, full, x, x_scaled, 1)
                pool.wait_ge(x_updated, (2 * layer + 1) * 8)
                chain.link(nc.gpsimd.memset(z[:, 0:16, :], 0.0))

                def hidden_squares(ch):
                    with pool.Fori(0, 4) as i:
                        hidden = ch * 4 + i + layer * 32
                        pool.wait_ge(acc_free, ch * B_CHUNK + i + blk(layer, B_MLP + 1))
                        pool.wait_ge(hid_ready, hidden + 1)
                        nc.gpsimd.tensor_tensor(z[:, 18:20, :], z[:, 16:18, :], z[:, 16:18, :], ALU.mult).then_inc(sqh_ready, 1)

                with pool.Fori(0, CHUNKS - 1) as ch:
                    hidden_squares(ch)
                    with pool.Fori(0, 4) as i:
                        for e in range(2):
                            pool.wait_ge(acc_free, blk(layer, B_MLP + 5 + e) + ch * B_CHUNK + i * 2)
                            dst = z[:, bass.ds(i * 4 + 2 * e, 2), :]
                            nc.gpsimd.tensor_tensor(dst, dst, z[:, 20 + 2 * e:22 + 2 * e, :], ALU.add).then_inc(added, 1)
                hidden_squares(CHUNKS - 1)
                for k in range(8):
                    pool.wait_ge(acc_free, blk(layer, B_MLP + 5) + (CHUNKS - 1) * B_CHUNK + k)
                    dst, e = z[:, 2 * k:2 * k + 2, :], 2 * (k % 2)
                    nc.gpsimd.tensor_tensor(dst, dst, z[:, 20 + e:22 + e, :], ALU.add).then_inc(added, 1)
                    if k >= 2:
                        add_squares(2 * layer + 1, k - 1)
                scale_rest(4 * layer + 3, z, z, z_scaled, 2)

        @block.scalar
        def _(act):
            def w_high(j, q):
                act.wait_ge(raw_landed[j % 4], 16 * (q + (j // 4 + 1)))
                nc.scalar.activation(w_hi[:, j % 4, :, :], raw[:, j % 4, :, :], ACT.Copy).then_inc(hi_ready, 1)

            def eight_units(q, evict, prefetch=8, before=None):
                for j in range(8):
                    if before and j in before:
                        before[j]()
                    act.wait_ge(unit_used, 4 * q + (j + 1))
                    if j in evict:
                        evict[j]()
                    if j < prefetch:
                        w_high(j, q + 1)

            def copy_out(pair, tile):
                nc.scalar.activation(z[:, bass.ds(tile, 2), :], ps[:, 2 * pair:2 * pair + 2, 0:TOK], ACT.Copy).then_inc(acc_free, 1)

            def two_out(tile):
                return {3: lambda: copy_out(0, tile), 7: lambda: copy_out(1, tile + 2)}

            def squares(n, src, ready):
                for i in range(8):
                    ready(i)
                    if n or i >= 2:
                        act.wait_ge(sq_used, max(8 * n, 8 * n + i - 1))
                    nc.scalar.activation(z[:, 20 + 2 * (i % 2):22 + 2 * (i % 2), :], src[:, 2 * i:2 * i + 2, :],
                                         ACT.Square).then_inc(sq_ready, 1)

            def result_squares(u, i):
                if i >= 2:
                    act.wait_ge(psq_added, 6 * u + i - 1)
                to = {0: 16, 7: 20}.get(i, 18)
                nc.scalar.activation(z[:, to:to + 2, :], z[:, 2 * i:2 * i + 2, :], ACT.Square).then_inc(psq_ready, 1)

            def root(n):
                act.wait_ge(var_ready, n + 1)
                nc.scalar.activation(rstd[:, :], rstd[:, :], ACT.Sqrt).then_inc(std_ready, 1)

            def h_high(m):
                for i in range(8):
                    act.wait_ge(full_ready, 8 * m + i + 1)
                    nc.scalar.activation(h_hi[:, 2 * i:2 * i + 2, :], full[:, 2 * i:2 * i + 2, :], ACT.Copy).then_inc(h_hi_ready, 1)

            def tiles(w):
                return w.rearrange("(t p) -> t p", p=P)

            for layer in range(DEPTH):
                a = 3 * layer
                for r, n, w in ((0, 16, g_pre1), (16, 16, g_post1), (32, 16, g_pre2), (48, 16, g_post2),
                                (64, 4, pool_scale), (68, 4, conv_b), (72, 4, conv_ln_g), (76, 4, conv_ln_b)):
                    act.dma_start(rows[r:r + n, a, :], tiles(w[layer])).then_inc(rows_landed, 16)
                act.dma_start(rows[0:96, a + 1, :], tiles(b_ada[layer])).then_inc(rows_landed, 16)
                act.dma_start(rows[0:124, a + 2, :], conv_dw[layer].rearrange("k (t p) -> (k t) p", p=P)).then_inc(rows_landed, 16)
            act.dma_start(sinks[:, :, :], sink.unsqueeze(0).to_broadcast([P, DEPTH, HEADS])).then_inc(sinks_landed, 16)
            act.wait_ge(cond_raw, 1)
            nc.scalar.activation(cond_t[:, 1, :], cond_t[:, 0, :], ACT.Sigmoid).then_inc(cond_sig, 1)
            for g in range(12):
                b, j = divmod(g, 4)
                act.wait_ge(x_turned, g + 1)
                nc.scalar.activation(x[:, 4 * j:4 * j + 4, P * b:P * b + P],
                                     ps[:, 2 + g % 2, :].rearrange("p (t n) -> p t n", n=P), ACT.Copy).then_inc(x_copied, 1)
            for j in range(4):
                w_high(j, 0)

            for layer in range(DEPTH):
                if layer == 0:
                    squares(0, x, lambda i: act.wait_ge(x_copied, 12))
                else:
                    squares(2 * layer, x, lambda i: act.wait_ge(x_updated, 8 * (2 * layer - 1) + i + 1))
                root(4 * layer)
                h_high(2 * layer)
                with act.Fori(0, 2) as i:
                    eight_units(quad(layer, Q_IN) + i * 2, two_out(i * 4 + CA0))
                act.wait_ge(acc_free, blk(layer, 4))
                nc.scalar.activation(z[:, CG0:CG0 + 4, :], z[:, CG0:CG0 + 4, :], ACT.Sigmoid).then_inc(sig_ready, 1)
                for k, tile in enumerate((PU0, K0, Q0)):
                    eight_units(quad(layer, Q_IN + 4) + k * 2, two_out(tile))

                def center_squares():
                    act.wait_ge(cen_ready, layer + 1)
                    nc.scalar.activation(centered_sq[:, :, :], act_in[:, :, :], ACT.Square).then_inc(csq_ready, 1)

                def ln_root():
                    act.wait_ge(lnv_ready, layer + 1)
                    nc.scalar.activation(rstd[:, :], rstd[:, :], ACT.Sqrt).then_inc(lnstd_ready, 1)

                def silu_gate():
                    act.wait_ge(ln_ready, layer + 1)
                    act.wait_ge(pooled, layer + 1)
                    nc.scalar.activation(z[:, CG0:CG0 + 4, :], act_in[:, :, :], ACT.Sigmoid).then_inc(silu_sig, 1)

                eight_units(quad(layer, Q_IN + 10), two_out(4), before={2: center_squares, 4: ln_root, 5: silu_gate})
                for g in range(4):
                    act.wait_ge(pool_mm, 4 * layer + g + 1)
                    nc.scalar.activation(h_hi[:, 8 + g, :], ps[:, g, 0:TOK], ACT.Copy,
                                         scale=pa[:, layer, POOL_S + g:POOL_S + g + 1]).then_inc(pool_hi, 1)
                act.wait_ge(kv_turned, layer + 1)
                act.wait_ge(conv_act, layer + 1)
                nc.scalar.activation(vt[:, 0:2, :], ps[:, 4, :].rearrange("p (b n) -> p b n", n=256), ACT.Copy)
                nc.scalar.activation(vt[:, 2, :], ps[:, 5, 0:256], ACT.Copy).then_inc(v_ready, 1)
                nc.scalar.activation(k_out[:, :], ps[:, 5, 256:512], ACT.Copy).then_inc(v_ready, 1)
                for t in range(4):
                    act.wait_ge(pw_ready, 4 * layer + t + 1)
                    nc.scalar.activation(h_hi[:, 12 + t, :], ps[:, t, 0:TOK], ACT.Copy).then_inc(pw_hi, 1)

                def exps(s):
                    pair, what = STEPS[s]
                    n, k, done = (TOK if what else CTX), s % 2, layer * len(STEPS)
                    act.wait_ge(nb_ready, done + s + 1)
                    if done + s >= 2:
                        act.wait_ge(t_ready, done + s - 1)
                    for e in range(2):
                        nc.scalar.activation(prob[:, k, e, 0:n], ps[:, 2 + e, 0:n], ACT.Exp, bias=nbias[:, k, e:e + 1],
                                             scale=SCALE, accum_out=row_sum[:, k, e:e + 1])
                    nc.scalar.activation(sink_e[:, k, :], sink_in[:, k, :], ACT.Exp).then_inc(p_ready, 1)

                def normalise(s):
                    n, k, done = (TOK if STEPS[s][1] else CTX), s % 2, layer * len(STEPS)
                    act.wait_ge(rden_ready, done + s + 1)
                    for e in range(2):
                        last = nc.scalar.activation(prob[:, k, e, 0:n], prob[:, k, e, 0:n], ACT.Copy, scale=rden[:, k, e:e + 1])
                    last.then_inc(pn_ready, 1)

                def out_high(s):
                    pair, what = STEPS[s]
                    act.wait_ge(o_ready, layer * len(STEPS) + s + 1)
                    nc.scalar.activation(h_hi[:, pair, P * what:P * what + P], ps[:, BANK_MOD, 256:384], ACT.Copy).then_inc(o_hi, 1)

                def side_unit(s):
                    u = 2 * STEPS[s][0] + STEPS[s][1] - 1
                    q, j, b = quad(layer, Q_OUT) + u // 4, u % 4, u // 2
                    act.wait_ge(unit_used, 4 * q + j + 1)
                    if u % 2:
                        if b == 4:
                            act.wait_ge(kv_out, 32 * (layer + 1))
                        dst = z[:, 8 + 2 * b:10 + 2 * b, :] if b < 4 else mix_t[:, 2 * b - 8:2 * b - 6, :]
                        nc.scalar.activation(dst, ps[:, 0:2, 0:TOK], ACT.Copy).then_inc(acc_free, 1)
                    w_high(j, q + 1)

                for s in range(len(STEPS) + 1):
                    what = STEPS[s][1] if s < len(STEPS) else 0
                    if what == 2:
                        side_unit(s - 1)
                    if s < len(STEPS):
                        exps(s)
                        normalise(s)
                    if s and not what:
                        side_unit(s - 1)
                    if s:
                        out_high(s - 1)

                def mix_square(i):
                    act.wait_ge(mix_added, 8 * layer + i + 1)
                    result_squares(2 * layer, i)

                def mix_out(k):
                    if k >= 4:
                        act.wait_ge(mix_added, 8 * layer + k - 3)
                    copy_out((k + 1) % 2, 2 * k)
                    if k:
                        mix_square(k - 1)

                eight_units(quad(layer, Q_OUT + 4), {2 * k + 1: (lambda k=k: mix_out(k)) for k in range(4)})
                eight_units(quad(layer, Q_OUT + 6), {2 * k + 1: (lambda k=k: mix_out(k + 4)) for k in range(4)})
                mix_square(7)
                root(4 * layer + 1)
                squares(2 * layer + 1, x, lambda i: act.wait_ge(x_updated, 8 * (2 * layer) + i + 1))
                root(4 * layer + 2)
                h_high(2 * layer + 1)

                def relu_out(pair, tile, ch, b):
                    hidden = ch * 4 + b
                    act.wait_ge(sqh_ready, hidden + (32 * layer + 1))
                    nc.scalar.activation(z[:, 16:18, :], ps[:, 2 * pair:2 * pair + 2, 0:TOK], ACT.Relu).then_inc(acc_free, 1)
                    act.wait_ge(acc_free, blk(layer, B_MLP + 1) + ch * B_CHUNK + b)
                    nc.scalar.activation(hid_hi[:, bass.ds(tile, 2), :], z[:, 16:18, :], ACT.Square).then_inc(hidh_ready, 1)

                def sum_out(pair, n):
                    act.wait_ge(added, n + 1)
                    nc.scalar.activation(z[:, 20 + 2 * pair:22 + 2 * pair, :], ps[:, 2 * pair:2 * pair + 2, 0:TOK],
                                         ACT.Copy).then_inc(acc_free, 1)

                def up(ch, q):
                    with act.Fori(0, 2) as i:
                        eight_units(q + i * 2, {3: lambda: relu_out(0, i * 4, ch, i * 2),
                                                7: lambda: relu_out(1, i * 4 + 2, ch, i * 2 + 1)})

                def down(ch, q, i, prefetch=8):
                    n = 64 * layer + ch * 8 + i * 4
                    eight_units(q + 4 + i * 2, {2 * k + 1: (lambda k=k: sum_out(k % 2, n + k)) for k in range(4)}, prefetch)

                def last_down(ch, q, i, prefetch):
                    def out(k):
                        sum_out(k % 2, 64 * layer + ch * 8 + k)
                        if k:
                            act.wait_ge(added, 64 * layer + ch * 8 + k + 2)
                            result_squares(2 * layer + 1, k - 1)

                    eight_units(q + 4 + i * 2, {2 * k + 1: (lambda k=k: out(4 * i + k)) for k in range(4)}, prefetch)

                with act.Fori(0, CHUNKS - 1) as ch:
                    q = quad(layer, Q_MLP) + ch * Q_CHUNK
                    up(ch, q)
                    with act.Fori(0, 2) as i:
                        down(ch, q, i)
                ch, q = CHUNKS - 1, quad(layer, Q_MLP) + (CHUNKS - 1) * Q_CHUNK
                up(ch, q)
                act.wait_ge(hid_ready, 32 * (layer + 1) + 1)
                last_down(ch, q, 0, 8)
                last_down(ch, q, 1, 4 if layer == DEPTH - 1 else 8)
                act.wait_ge(added, 64 * (layer + 1) + 2)
                result_squares(2 * layer + 1, 7)
                root(4 * layer + 3)
            for g in range(12):
                j, b = divmod(g, 3)
                act.wait_ge(y_turned, g + 1)
                nc.scalar.activation(y_rows[:, b, 512 * j:512 * j + 512], ps[:, g % 4, :], ACT.Copy).then_inc(y_copied, 1)

        @block.vector
        def _(dve):
            chain = Chain(dve, dve_chain)

            def w_low(j, q):
                dve.wait_ge(hi_ready, 4 * q + (j + 1))
                nc.vector.tensor_tensor(w_lo[:, j % 4, :, :], raw[:, j % 4, :, :], w_hi[:, j % 4, :, :].bitcast(F32),
                                        ALU.subtract).then_inc(lo_ready, 1)

            def ada_copy(n):
                dve.wait_ge(ada_used, 4 * n + 4)
                nc.vector.tensor_copy(ada_s[:, :], ps[:, BANK_ADA, 0:UC]).then_inc(ada_copied, 1)

            def ada_mods(layer, m, n):
                dve.wait_ge(ada_turned, n + 1)
                nc.vector.tensor_tensor(mods[:, layer, bass.ds(m * 2, 2), :],
                                        ps[:, BANK_MOD, 0:4].rearrange("p (t g) -> p t g", g=2),
                                        pb[:, layer, bass.ds(m * 2, 2)].unsqueeze(2).to_broadcast([P, 2, 2]),
                                        ALU.add).then_inc(mods_ready, 1)

            def eight_units(q, before=None, after=None, prefetch=8):
                for j in range(8):
                    for f in (before or {}).get(j, ()):
                        f()
                    if j < prefetch:
                        w_low(j, q + 1)
                    for f in (after or {}).get(j, ()):
                        f()

            def ada_pair(layer, m):
                n = layer * ADA_BLOCKS + m
                return ({3: [lambda: ada_copy(n)], 4: [lambda: ada_mods(layer, m, n)], 7: [lambda: ada_copy(n + 1)]},
                        {7: [lambda: ada_mods(layer, m + 1, n + 1)]})

            def inverse_root(n):
                if n % 2:
                    dve.wait_ge(psq_summed, n // 2 + 1)
                else:
                    dve.wait_ge(sq_used, 8 * (n // 2 + 1))
                nc.vector.tensor_scalar(rstd[:, :], ps[:, BANK_SUM, 0:TOK], 1.0 / D, EPS, ALU.mult, ALU.add).then_inc(var_ready, 1)
                dve.wait_ge(std_ready, n + 1)
                nc.vector.reciprocal(rstd[:, :], rstd[:, :]).then_inc(rstd_ready, 1)
                dve.wait_ge(rstd_ready, n + 1)

            def scaled(out, src, i):
                t = slice(2 * i, 2 * i + 2)
                return chain.mark(nc.vector.tensor_tensor(out[:, t, :], src[:, t, :], per_token(rstd, 2), ALU.mult))

            def residual(r, k):
                for i in range(8):
                    if i < 2:
                        chain.wait(scaled(z, z, i))
                    else:
                        dve.wait_ge(z_scaled, 6 * r + i - 1)
                    for t in (2 * i, 2 * i + 1):
                        for g, a, b in GROUPS:
                            last = nc.vector.scalar_tensor_tensor(out=x[:, t, a:b], in0=z[:, t, a:b], scalar=coef[:, k, t, g:g + 1],
                                                                  in1=x[:, t, a:b], op0=ALU.mult, op1=ALU.add)
                    last.then_inc(x_updated, 1)

            def build_h(m, layer, k, shift):
                def low(i):
                    dve.wait_ge(h_hi_ready, 8 * m + i + 1)
                    nc.vector.tensor_tensor(h_lo[:, 2 * i:2 * i + 2, :], full[:, 2 * i:2 * i + 2, :],
                                            h_hi[:, 2 * i:2 * i + 2, :].bitcast(F32), ALU.subtract).then_inc(h_ready, 1)

                mark = scaled(full, x, 0)
                for i in range(8):
                    if i == 0:
                        chain.wait(mark)
                    else:
                        dve.wait_ge(x_scaled, 7 * m + i)
                    for t in (2 * i, 2 * i + 1):
                        for g, a, b in GROUPS:
                            last = nc.vector.tensor_scalar(full[:, t, a:b], full[:, t, a:b], coef[:, k, t, g:g + 1],
                                                           mods[:, layer, shift + t, g:g + 1], ALU.mult, ALU.add)
                    last.then_inc(full_ready, 1)
                    if i % 2:
                        low(i - 1)
                        low(i)

            def gain(k, layer, g0):
                return pa[:, layer, g0:g0 + DT].unsqueeze(2).to_broadcast([P, DT, 2])

            def scale_coef(k, layer, sc, g0):
                chain.link(nc.vector.scalar_tensor_tensor(out=coef[:, k, :, :], in0=mods[:, layer, sc:sc + DT, :], scalar=1.0,
                                                          in1=gain(k, layer, g0), op0=ALU.add, op1=ALU.mult))

            def gate_coef(k, layer, g, g0):
                chain.link(nc.vector.tensor_tensor(coef[:, k, :, :], mods[:, layer, g:g + DT, :], gain(k, layer, g0), ALU.mult))

            dve.wait_ge(c_turned, 1)
            nc.vector.tensor_copy(cond_t[:, 0, :], ps[:, BANK_SUM, 0:2 * DT]).then_inc(cond_raw, 1)
            dve.wait_ge(consts_ready, 3)
            dve.wait_ge(cond_sig, 1)
            for g in range(2):
                last = nc.vector.tensor_tensor(cond[:, :, g], cond_t[:, 0, DT * g:DT * g + DT], cond_t[:, 1, DT * g:DT * g + DT], ALU.mult)
            last.then_inc(cond_ready, 1)
            dve.wait_ge(rows_turned, 1)
            for layer in range(DEPTH):
                nc.vector.tensor_copy(pa[:, layer, :], ps[:, layer, 0:ROWS_A])
                nc.vector.tensor_copy(pb[:, layer, :], ps[:, layer, 128:224])
                chain.link(nc.vector.tensor_copy(pc[:, layer, :], ps[:, layer, 256:380]))
            dve.wait_ge(sinks_landed, 16)
            chain.link(nc.vector.tensor_scalar(nsinks[:, :, :], sinks[:, :, :], -1.0, None, ALU.mult))
            for j in range(4):
                w_low(j, 0)
            for a, b in ((0, 4), (4, 8)):
                with dve.Fori(a, b) as m:
                    ada_copy(m)
                    ada_mods(0, m, m)
                if a == 0:
                    inverse_root(0)
                    chain.wait(scaled(full, x, 0))
            dve.wait_ge(x_scaled, 7)
            n0 = chain.n
            with dve.Fori(0, 8) as i:
                chain.n = n0 + i
                ada_copy(i + 8)
                ada_mods(0, i + 8, i + 8)
                dve.wait_ge(mods_ready, i + 9)
                chain.link(nc.vector.scalar_tensor_tensor(
                    out=coef[:, 0, bass.ds(i * 2, 2), :], in0=mods[:, 0, bass.ds(i * 2 + SC1, 2), :], scalar=1.0,
                    in1=pa[:, 0, bass.ds(i * 2 + G_PRE1, 2)].unsqueeze(2).to_broadcast([P, 2, 2]), op0=ALU.add, op1=ALU.mult))
                for t in range(2):
                    for g, a, b in GROUPS:
                        last = nc.vector.tensor_scalar(full[:, bass.ds(i * 2 + t, 1), a:b], full[:, bass.ds(i * 2 + t, 1), a:b],
                                                       coef[:, 0, bass.ds(i * 2 + t, 1), g], mods[:, 0, bass.ds(i * 2 + t, 1), g],
                                                       ALU.mult, ALU.add)
                last.then_inc(full_ready, 1)
                dve.wait_ge(h_hi_ready, i + 1)
                nc.vector.tensor_tensor(h_lo[:, bass.ds(i * 2, 2), :], full[:, bass.ds(i * 2, 2), :],
                                        h_hi[:, bass.ds(i * 2, 2), :].bitcast(F32), ALU.subtract).then_inc(h_ready, 1)
            chain.n = n0 + 8

            for layer in range(DEPTH):
                first = layer == 0
                n_mods = ADA_BLOCKS * layer
                if not first:
                    dve.wait_ge(mods_ready, 2 * ADA_BLOCKS)
                    scale_coef(0, layer, SC1, G_PRE1)
                    inverse_root(4 * layer)
                    build_h(2 * layer, layer, 0, SH1)
                with dve.Fori(0, 2) as i:
                    eight_units(quad(layer, Q_IN) + i * 2, *(ada_pair(0, i * 2 + ADA_CU) if first else ()))
                dve.wait_ge(sig_ready, layer + 1)
                dve.wait_ge(pads_ready, 3 * (layer + 1))
                chain.link(nc.vector.tensor_tensor(glu[:, :, C_HALF:C_HALF + CTX], z[:, CA0:CA0 + 4, 0:CTX], z[:, CG0:CG0 + 4, 0:CTX], ALU.mult))
                chain.link(nc.vector.tensor_tensor(glu[:, :, C_HALF + CONV_LAT:C_HALF + CONV_OUT], z[:, CA0:CA0 + 4, CTX:TOK],
                                                   z[:, CG0:CG0 + 4, CTX:TOK], ALU.mult))

                nc.vector.memset(row_max[:, 0, :], 0.0).then_inc(glu_ready, 1)

                n0 = chain.n
                with dve.Fori(0, 3) as i:
                    chain.n = n0 + i * (TAPS + 1)
                    done = conv[:, bass.ds(i, 1), :]
                    marks = []

                    def tap(k):
                        src, out = glu[:, bass.ds(i, 1), k:k + CONV_OUT], conv_odd[:, :, :] if k % 2 else done
                        w = pc[:, layer, bass.ds(i + 4 * k, 1)]
                        if k >= 2:
                            chain.wait(marks[k - 2])
                            op = nc.vector.scalar_tensor_tensor(out=out, in0=src, scalar=w, in1=out, op0=ALU.mult, op1=ALU.add)
                        elif k == 1:
                            op = nc.vector.tensor_scalar(out, src, w, None, ALU.mult)
                        else:
                            op = nc.vector.tensor_scalar(out, src, w, pa[:, layer, bass.ds(i + CONV_B, 1)], ALU.mult, ALU.add)
                        marks.append(chain.mark(op))
                        if k == TAPS - 1:
                            chain.wait(marks[k])
                            chain.link(nc.vector.tensor_tensor(done, done, conv_odd[:, :, :], ALU.add))

                    before, after = ada_pair(0, i * 2 + ADA_QKV) if first else ({}, {})
                    for j in range(8):
                        after[j] = [(lambda k=k: tap(k)) for k in range(4 * j, min(4 * j + 4, TAPS))] + list(after.get(j, []))
                    eight_units(quad(layer, Q_IN + 4) + i * 2, before, after)
                chain.n = n0 + 3 * (TAPS + 1)
                nc.vector.memset(row_max[:, 0, :], 0.0).then_inc(conv_ready, 1)

                def pool_means():
                    dve.wait_ge(pool_summed, layer + 1)
                    for g, w in enumerate(POOL_WINDOWS):
                        for start, a, b in ((P_HALF, 0, CTX), (POOL_LAT, CTX, TOK)):
                            o = start - w // 2
                            last = nc.vector.scalar_tensor_tensor(out=z[:, PU0 + g, a:b], in0=pool_a[:, g, o:o + b - a], scalar=1.0 / w,
                                                                  in1=z[:, PU0 + g, a:b], op0=ALU.mult, op1=ALU.subtract)
                    last.then_inc(pooled, 1)

                def center():
                    dve.wait_ge(ln_sum, layer + 1)
                    chain.link(nc.vector.tensor_scalar(rstd[:, :], ps[:, BANK_SUM, 0:TOK], 1.0 / 512, None, ALU.mult))
                    nc.vector.tensor_tensor(act_in[:, :, 0:CTX], conv[:, :, 0:CTX], per_token(rstd, 4, 0, CTX), ALU.subtract)
                    nc.vector.tensor_tensor(act_in[:, :, CTX:TOK], conv[:, :, CONV_LAT:CONV_OUT], per_token(rstd, 4, CTX, TOK),
                                            ALU.subtract).then_inc(cen_ready, 1)

                def variance():
                    dve.wait_ge(csq_used, layer + 1)
                    nc.vector.tensor_scalar(rstd[:, :], ps[:, BANK_VAR, 0:TOK], 1.0 / 512, EPS, ALU.mult, ALU.add).then_inc(lnv_ready, 1)

                def layer_norm():
                    dve.wait_ge(lnstd_ready, layer + 1)
                    chain.link(nc.vector.reciprocal(rstd[:, :], rstd[:, :]))
                    chain.link(nc.vector.tensor_tensor(act_in[:, :, :], act_in[:, :, :], per_token(rstd, 4), ALU.mult))
                    for t in range(4):
                        last = nc.vector.tensor_scalar(act_in[:, t, :], act_in[:, t, :], pa[:, layer, LN_G + t:LN_G + t + 1],
                                                       pa[:, layer, LN_B + t:LN_B + t + 1], ALU.mult, ALU.add)
                    last.then_inc(ln_ready, 1)

                def silu():
                    dve.wait_ge(silu_sig, layer + 1)
                    nc.vector.tensor_tensor(act_in[:, :, :], act_in[:, :, :], z[:, CG0:CG0 + 4, :], ALU.mult).then_inc(conv_act, 1)

                swap = [p ^ 16 for p in range(32)]

                def rope(a, b, scratch):
                    zz, rr = z[:, a:b, CTX:TOK], scratch[:, 0:b - a, :]
                    return (lambda: chain.link(nc.vector.stream_shuffle(rr, zz, swap)),
                            lambda: chain.link(nc.vector.tensor_tensor(rr, rr, per_token(sin_t, b - a, 0, LAT), ALU.mult)),
                            lambda: chain.link(nc.vector.tensor_tensor(zz, zz, per_token(cos_t, b - a, 0, LAT), ALU.mult)),
                            lambda: chain.link(nc.vector.tensor_tensor(zz, zz, rr, ALU.add)))

                kdv = kd[:, :, :].rearrange("p (t s) n -> p t s n", s=2)

                def rope_keys():
                    dve.wait_ge(rope_landed, 48 * (layer + 1))
                    for op in rope(K0, K0 + 2, rot):
                        op()

                def copy_keys():
                    for a in range(2):
                        for b in range(2):
                            nc.vector.tensor_copy(kdv[64 * b:64 * b + 64, :, a, 0:TOK], z[64 * a:64 * a + 64, K0:K0 + 2, :])

                before, after = ada_pair(0, ADA_QKV + 6) if first else ({}, {})
                for j, f in ((1, center), (3, variance), (3, pool_means), (4, layer_norm), (5, silu), (6, rope_keys), (7, copy_keys)):
                    before[j] = list(before.get(j, [])) + [f]
                eight_units(quad(layer, Q_IN + 10), before, after)

                for g in range(4):
                    dve.wait_ge(pool_hi, 4 * layer + g + 1)
                    nc.vector.scalar_tensor_tensor(out=h_lo[:, 8 + g, :], in0=ps[:, g, 0:TOK],
                                                   scalar=pa[:, layer, POOL_S + g:POOL_S + g + 1],
                                                   in1=h_hi[:, 8 + g, :].bitcast(F32), op0=ALU.mult, op1=ALU.subtract).then_inc(pool_done, 1)
                for op in rope(Q0, Q0 + 4, rot):
                    op()
                late_rope = rope(Q0 + 4, Q0 + 8, rot2)
                dve.wait_ge(ck_turned, layer + 1)
                for a in range(2):
                    for b in range(2):
                        last = nc.vector.tensor_copy(kdv[64 * b:64 * b + 64, :, a, TOK:512],
                                                     ps[64 * a:64 * a + 64, BANK_MOD, 256:512].rearrange("p (t n) -> p t n", n=P))
                last.then_inc(kd_ready, 1)
                for t in range(4):
                    dve.wait_ge(pw_hi, 4 * layer + t + 1)
                    nc.vector.tensor_tensor(h_lo[:, 12 + t, :], ps[:, t, 0:TOK], h_hi[:, 12 + t, :].bitcast(F32), ALU.subtract).then_inc(pw_done, 1)

                dve.wait_ge(masks_ready, 2 * (layer + 1))
                done = layer * len(STEPS)

                def stats(s):
                    pair, what = STEPS[s]
                    k = s % 2
                    dve.wait_ge(s_ready, done + s + 1)
                    n = TOK if what else CTX
                    if what:
                        m = ps[:, 2:4, (P if what == 1 else 0):][:, :, 0:P]
                        chain.link(nc.vector.tensor_tensor(m, m, masks[:, what - 1, :].unsqueeze(1).to_broadcast([P, 2, P]), ALU.add))
                    chain.link(nc.vector.reduce_max(row_max[:, k, :], ps[:, 2:4, 0:n], AX_X))
                    chain.link(nc.vector.scalar_tensor_tensor(out=nbias[:, k, :], in0=row_max[:, k, :], scalar=-SCALE,
                                                              in1=nsinks[:, layer, 2 * pair:2 * pair + 2], op0=ALU.mult, op1=ALU.min))
                    nc.vector.tensor_tensor(sink_in[:, k, :], nbias[:, k, :], sinks[:, layer, 2 * pair:2 * pair + 2], ALU.add).then_inc(nb_ready, 1)

                def denominator(s):
                    k = s % 2
                    dve.wait_ge(p_ready, done + s + 1)
                    chain.link(nc.vector.tensor_tensor(row_sum[:, k, :], row_sum[:, k, :], sink_e[:, k, :], ALU.add))
                    nc.vector.reciprocal(rden[:, k, :], row_sum[:, k, :]).then_inc(rden_ready, 1)

                def turned_out(s):
                    pair, what = STEPS[s]
                    dve.wait_ge(t_ready, done + s + 1)
                    if what:
                        nc.vector.tensor_copy(prob_t[:, s % 2, 0:2, :], ps[:, 4, :].rearrange("p (b n) -> p b n", n=256))
                        nc.vector.tensor_copy(prob_t[:, s % 2, 2, :], ps[:, 5, 0:256]).then_inc(pt_ready, 1)
                    else:
                        nc.vector.tensor_copy(prob_t[:, s % 2, 0, :], ps[:, 4, 0:256]).then_inc(pt_ready, 1)

                def out_low(s):
                    pair, what = STEPS[s]
                    dve.wait_ge(o_hi, done + s + 1)
                    cols = slice(P * what, P * what + P)
                    nc.vector.tensor_tensor(h_lo[:, pair, cols], ps[:, BANK_MOD, 256:384], h_hi[:, pair, cols].bitcast(F32),
                                            ALU.subtract).then_inc(o_done, 1)

                def side_low(s):
                    u = 2 * STEPS[s][0] + STEPS[s][1] - 1
                    w_low(u % 4, quad(layer, Q_OUT + 1) + u // 4)

                for s in range(len(STEPS) + 1):
                    what = STEPS[s][1] if s < len(STEPS) else 0
                    m = ADA_MIX + 2 * (s // 3) + (0 if what == 1 else -1)
                    ada = first and s and what != 2
                    if s == 2:
                        dve.wait_ge(kv_out, 32 * (layer + 1))
                    if ada and not what:
                        ada_copy(m)
                    late = what == 1 or (what == 2 and not first)
                    if s and not late:
                        turned_out(s - 1)
                    if what == 2:
                        side_low(s - 1)
                    if s < len(STEPS):
                        stats(s)
                    if ada and what:
                        ada_copy(m)
                    if late:
                        turned_out(s - 1)
                    if s < len(STEPS):
                        denominator(s)
                    if ada:
                        ada_mods(0, m, m)
                    if s in (4, 5, 7, 8):
                        late_rope[(4, 5, 7, 8).index(s)]()
                    if s == 8:
                        nc.vector.memset(rden[:, 1, :], 0.0).then_inc(kd_ready, 1)
                    if s:
                        out_low(s - 1)
                    if s and not what:
                        side_low(s - 1)

                with dve.Fori(0, 2) as i:
                    eight_units(quad(layer, Q_OUT + 4) + i * 2, *(ada_pair(0, i * 2 + ADA_OUT) if first else ()))
                dve.wait_ge(mods_ready, n_mods + ADA_BLOCKS)
                gate_coef(1, layer, G1, G_POST1)
                scale_coef(2, layer, SC2, G_PRE2)
                gate_coef(3, layer, G2, G_POST2)
                inverse_root(4 * layer + 1)
                residual(2 * layer, 1)
                inverse_root(4 * layer + 2)
                dve.wait_ge(x_updated, 8 * (2 * layer + 1))
                build_h(2 * layer + 1, layer, 2, SH2)

                def hidden_low(tile, n):
                    dve.wait_ge(hidh_ready, n + 1)
                    dve.wait_ge(sqh_ready, n + 2)
                    nc.vector.tensor_tensor(hid_lo[:, bass.ds(tile, 2), :], z[:, 18:20, :], hid_hi[:, bass.ds(tile, 2), :].bitcast(F32),
                                            ALU.subtract).then_inc(hid_ready, 1)

                def ada_products(ch, block, j, mark0):
                    n, k0 = ch * 6 + (ADA_BLOCKS + block), mark0 + 28 * block + 7 * j
                    dve.wait_ge(ada_landed[j], 16 * (n + 1))
                    if j == 0:
                        dve.wait_ge(ada_turned, n - 1)
                    for o in range(8):
                        k, g = divmod(o, 2)
                        out = ada_sums[:, block % 2, g, :]
                        if o == 1 and j:
                            dve.wait_ge(ada_used, 4 * n + j)
                        elif o > 1 or j:
                            dve.wait_ge(dve_chain, k0 + (o - 1 if o > 1 else 0))
                        if j or k:
                            op = nc.vector.scalar_tensor_tensor(out=out, in0=ada_raw[:, j, k, :], scalar=cond[:, 4 * j + k, g:g + 1],
                                                                in1=out, op0=ALU.mult, op1=ALU.add)
                        else:
                            op = nc.vector.tensor_scalar(out, ada_raw[:, j, k, :], cond[:, 4 * j + k, g:g + 1], None, ALU.mult)
                        op.then_inc(ada_used if o == 7 else dve_chain, 1)

                def mlp_quad(ch, k, mark0, prefetch=4):
                    for j in range(4):
                        if k == 3 and j == 3:
                            hidden_low(2 * k, ch * 4 + (k + 32 * layer))
                        if j < prefetch:
                            w_low(j, ch * Q_CHUNK + quad(layer, Q_MLP + k + 1))
                        if k < 3 and j == 3:
                            hidden_low(2 * k, ch * 4 + (k + 32 * layer))
                        if first and k + 1 in ADA_OF_QUAD:
                            ada_products(ch, ADA_OF_QUAD[k + 1], j, mark0)
                        if first and k in ADA_OF_QUAD and j == 3:
                            m = ch * 6 + ADA_OF_QUAD[k]
                            ada_mods(1, m, m + ADA_BLOCKS)

                last_layer = layer == DEPTH - 1
                n0 = chain.n
                with dve.Fori(0, CHUNKS - 1 if last_layer else CHUNKS) as ch:
                    for k in range(Q_CHUNK):
                        mlp_quad(ch, k, ch * 168 + n0)
                if first:
                    chain.n = n0 + CHUNKS * 168
                if last_layer:
                    for k in range(Q_CHUNK):
                        mlp_quad(CHUNKS - 1, k, 0, prefetch=0 if k == Q_CHUNK - 1 else 4)
                inverse_root(4 * layer + 3)
                residual(2 * layer + 1, 3)
                dve.wait_ge(x_updated, 8 * (2 * layer + 2))

        @block.tensor
        def _(pe):
            def unit(j, q, pair, kt, hi, lo, begin, end):
                pe.wait_ge(lo_ready, 4 * q + (j + 1))
                for k in range(4):
                    for t in range(2):
                        for i, (w, v) in enumerate(((w_hi, hi), (w_hi, lo), (w_lo, hi))):
                            last = nc.tensor.matmul(ps[:, 2 * pair + t, 0:TOK], w[:, j % 4, k, P * t:P * t + P], v[:, kt + k, :],
                                                    start=begin and k == 0 and i == 0, stop=end and k == 3 and i == 2)
                last.then_inc(unit_used, 1)

            def ada_unit(n, j):
                pe.wait_ge(ada_landed[j], 16 * (n + 1))
                if j == 0 and not (isinstance(n, int) and n == 0):
                    pe.wait_ge(ada_copied, n)
                for g in range(4):
                    last = nc.tensor.matmul(ps[32 * g:32 * g + 32, BANK_ADA, 0:UC], cond[:, 4 * j + g, :], ada_raw[:, j, g, :],
                                            start=j == 0, stop=j == 3)
                last.then_inc(ada_used, 1)

            def ada_turn(n):
                pe.wait_ge(ada_copied, n + 1)
                if not (isinstance(n, int) and n == 0):
                    pe.wait_ge(mods_ready, n)
                for t in range(2):
                    last = nc.tensor.matmul(ps[:, BANK_MOD, 2 * t:2 * t + 2], ada_s[:, P * t:P * t + P], sel[:, :],
                                            start=True, stop=True)
                last.then_inc(ada_turned, 1)

            def ada_beside(m, j):
                if j == 3:
                    ada_turn(m)
                for n, u in {0: ((0, 0), (0, 1)), 1: ((0, 2),), 2: ((0, 3),), 3: ((1, 0),), 4: ((1, 1),),
                             5: ((1, 2),), 6: ((1, 3),), 7: ()}[j]:
                    ada_unit(m + n, u)
                if j == 7:
                    ada_turn(m + 1)

            def turn_sums(n, buffer):
                pe.wait_ge(ada_used, 4 * n + 4)
                pe.wait_ge(mods_ready, n)
                for t in range(2):
                    for g in range(2):
                        last = nc.tensor.matmul(ps[:, BANK_MOD, 2 * t + g:2 * t + g + 1], ada_sums[:, buffer, g, P * t:P * t + P],
                                                ones[:, 0:1], start=True, stop=True)
                last.then_inc(ada_turned, 1)

            def two_blocks(q, b, ada=None, h_base=None, after=None):
                for j in range(8):
                    if j % 4 == 0 and not (isinstance(b, int) and b + j // 4 <= 1):
                        pe.wait_ge(acc_free, b + (j // 4 - 1))
                    if h_base is not None and j < 4:
                        pe.wait_ge(h_ready, h_base + 2 * j + 2)
                    unit(j, q, j // 4, 4 * (j % 4), h_hi, h_lo, j % 4 == 0, j % 4 == 3)
                    if ada is not None:
                        ada_beside(ada, j)
                    if after and j in after:
                        after[j]()

            def sum_pair(n, i):
                pe.wait_ge(sq_ready, 8 * n + i + 1)
                for t in range(2):
                    last = nc.tensor.matmul(ps[:, BANK_SUM, 0:TOK], ones[:, :], z[:, 20 + 2 * (i % 2) + t, :],
                                            start=i == 0 and t == 0, stop=i == 7 and t == 1)
                last.then_inc(sq_used, 1)

            def sum_squares(n):
                for i in range(8):
                    sum_pair(n, i)

            def sum_result_squares(u):
                for i, t in enumerate((16, 17, 20, 21)):
                    if i == 0:
                        pe.wait_ge(psq_added, 6 * (u + 1))
                    if i == 2:
                        pe.wait_ge(psq_ready, 8 * (u + 1))
                    last = nc.tensor.matmul(ps[:, BANK_SUM, 0:TOK], ones[:, :], z[:, t, :], start=i == 0, stop=i == 3)
                last.then_inc(psq_summed, 1)

            pe.wait_ge(consts_ready, 3)
            pe.wait_ge(c_landed, 32)
            nc.tensor.transpose(ps[:, BANK_SUM, 0:2 * DT], c_rows[0:2 * DT, :], ident[0:2 * DT, 0:2 * DT]).then_inc(c_turned, 1)
            pe.wait_ge(x_landed, 32)
            for g in range(12):
                b, j = divmod(g, 4)
                if g >= 2:
                    pe.wait_ge(x_copied, g - 1)
                for t in range(4):
                    last = nc.tensor.transpose(ps[:, 2 + g % 2, P * t:P * t + P], staged[:, b, P * (4 * j + t):P * (4 * j + t + 1)], ident[:, :])
                last.then_inc(x_turned, 1)
            pe.wait_ge(cond_ready, 1)
            for m in range(4):
                for j in range(4):
                    ada_unit(m, j)
                if m == 0:
                    pe.wait_ge(rows_landed, 16 * 10 * DEPTH)
                    for layer in range(DEPTH):
                        for i, n in enumerate((ROWS_A, 96, 124)):
                            last = nc.tensor.transpose(ps[:, layer, P * i:P * i + n], rows[0:n, 3 * layer + i, :], ident[0:n, 0:n])
                    last.then_inc(rows_turned, 1)
                sum_pair(0, 2 * m)
                sum_pair(0, 2 * m + 1)
                ada_turn(m)
            with pe.Fori(4, ADA_CU) as m:
                for j in range(4):
                    ada_unit(m, j)
                ada_turn(m)

            for layer in range(DEPTH):
                first = layer == 0
                if first:
                    two_blocks(0, 0, ADA_CU, 0)
                    two_blocks(2, 2, ADA_CU + 2)
                else:
                    sum_squares(2 * layer)
                    with pe.Fori(0, 2) as i:
                        two_blocks(quad(layer, Q_IN) + i * 2, blk(layer, B_IN) + i * 2, None, 16 * layer)
                with pe.Fori(0, 3) as i:
                    two_blocks(quad(layer, Q_IN + 4) + i * 2, blk(layer, B_IN + 4) + i * 2, i * 2 + ADA_QKV if first else None)

                def ln_sums():
                    pe.wait_ge(conv_ready, 2 * (layer + 1))
                    for a, b, src in ((0, CTX, 0), (CTX, TOK, CONV_LAT)):
                        for t in range(4):
                            last = nc.tensor.matmul(ps[:, BANK_SUM, a:b], ones[:, :], conv[:, t, src:src + b - a], start=t == 0, stop=t == 3)
                    last.then_inc(ln_sum, 1)

                def ln_squares():
                    pe.wait_ge(csq_ready, layer + 1)
                    for t in range(4):
                        last = nc.tensor.matmul(ps[:, BANK_VAR, 0:TOK], ones[:, :], centered_sq[:, t, :], start=t == 0, stop=t == 3)
                    last.then_inc(csq_used, 1)

                two_blocks(quad(layer, Q_IN + 10), blk(layer, B_IN + 10), ADA_QKV + 6 if first else None,
                           after={0: ln_sums, 2: ln_squares})
                pe.wait_ge(lnv_ready, layer + 1)
                for i in range(2):
                    for b in range(3):
                        nc.tensor.transpose(ps[:, 4 + b // 2, 256 * (b % 2) + P * i:256 * (b % 2) + P * i + P],
                                            z[:, V0 + i, P * b:P * b + P], ident[:, :])
                    last = nc.tensor.transpose(ps[:, 5, 256 + P * i:256 + P * i + P], z[:, K0 + i, 0:P], ident[:, :])
                last.then_inc(kv_turned, 1)
                pe.wait_ge(pooled, layer + 1)
                pe.wait_ge(conv_w_landed, 32 * (layer + 1))
                for g in range(4):
                    pe.wait_ge(acc_free, blk(layer, B_OUT) - (1 if g < 2 else 0))
                    nc.tensor.matmul(ps[:, g, 0:TOK], pool_w[:, g, :], z[:, PU0 + g, :], start=True, stop=True).then_inc(pool_mm, 1)
                pe.wait_ge(rope_landed, 48 * (layer + 1))
                pe.wait_ge(mods_ready, ADA_MIX if first else DEPTH * ADA_BLOCKS)
                for i in range(2):
                    last = nc.tensor.transpose(ps[:, BANK_MOD, 256 + P * i:256 + P * i + P], ck[:, P * i:P * i + P], ident[:, :])
                last.then_inc(ck_turned, 1)
                pe.wait_ge(conv_act, layer + 1)
                for t in range(4):
                    pe.wait_ge(pool_done, 4 * layer + t + 1)
                    for k in range(4):
                        last = nc.tensor.matmul(ps[:, t, 0:TOK], pw_w[:, k, P * t:P * t + P], act_in[:, k, :], start=k == 0, stop=k == 3)
                    last.then_inc(pw_ready, 1)

                done = layer * len(STEPS)

                def scores(s):
                    pair, what = STEPS[s]
                    a, b = (TOK - LAT, 512) if what else (0, CTX)
                    if s:
                        pe.wait_ge(p_ready, done + s)
                    for e in range(2):
                        half = slice(64 * e, 64 * e + 64)
                        last = nc.tensor.matmul(ps[:, 2 + e, 0:b - a], z[half, pair, P * what:P * what + P],
                                                kd[half, pair // 2, a:b], start=True, stop=True)
                    last.then_inc(s_ready, 1)

                def turn(s):
                    pair, what = STEPS[s]
                    pe.wait_ge(pn_ready, done + s + 1)
                    if done + s >= 1:
                        pe.wait_ge(pt_ready, done + s)
                    for kb in range(3 if what else 1):
                        for e in range(2):
                            o = 256 * (kb % 2) + P * e
                            last = nc.tensor.transpose(ps[:, 4 + kb // 2, o:o + P], prob[:, s % 2, e, P * kb:P * kb + P], ident[:, :])
                    last.then_inc(t_ready, 1)

                def mix(s):
                    pair, what = STEPS[s]
                    kv = pair // 2
                    blocks = (1, 2, 3) if what else (0,)
                    pe.wait_ge(pt_ready, done + s + 1)
                    if done + s >= 1:
                        pe.wait_ge(o_done, done + s)
                    if first:
                        pe.wait_ge(mods_ready, ADA_MIX + 2 * ((s + 1) // 3) + min((s + 1) % 3, 1))
                    for e in range(2):
                        for i, vb in enumerate(blocks):
                            last = nc.tensor.matmul(ps[64 * e:64 * e + 64, BANK_MOD, 256:384], vt[:, vb, HD * kv:HD * kv + HD],
                                                    prob_t[:, s % 2, i, P * e:P * e + P], start=i == 0, stop=i == len(blocks) - 1)
                    last.then_inc(o_ready, 1)

                def side_unit(s):
                    u = 2 * STEPS[s][0] + STEPS[s][1] - 1
                    if u % 2 == 0:
                        pe.wait_ge(acc_free, blk(layer, B_OUT) + u // 2)
                    unit(u % 4, quad(layer, Q_OUT) + u // 4, 0, 8 + 4 * (u % 2), h_hi, h_lo, u % 2 == 0, u % 2 == 1)

                pe.wait_ge(kd_ready, 2 * layer + 1)
                pe.wait_ge(pw_done, 4 * (layer + 1))
                pe.wait_ge(v_ready, 2 * (layer + 1))
                pe.wait_ge(cachev_landed, 16 * (layer + 1))
                for s in range(len(STEPS) + 1):
                    what = STEPS[s][1] if s < len(STEPS) else 0
                    m = ADA_MIX + 2 * (s // 3)
                    if s == 12:
                        pe.wait_ge(kd_ready, 2 * layer + 2)
                    late = what == 1 or (what == 2 and not first)
                    if s and not late:
                        turn(s - 1)
                    if s < len(STEPS):
                        scores(s)
                    if late:
                        turn(s - 1)
                    if what:
                        side_unit(s)
                    if first and s >= 2:
                        pe.wait_ge(o_done, done + s - 1)
                    if first and what == 1:
                        ada_turn(m)
                    if first and s < len(STEPS):
                        for block, k in (((m, 0), (m, 1), (m, 2), (m, 3)), ((m + 1, 0), (m + 1, 1)), ((m + 1, 2), (m + 1, 3)))[what]:
                            ada_unit(block, k)
                    if first and s and not what:
                        ada_turn(m - 1)
                    if s:
                        mix(s - 1)
                with pe.Fori(0, 2) as i:
                    q, b = quad(layer, Q_OUT + 4) + i * 2, blk(layer, B_OUT + 8) + i * 4
                    for j in range(8):
                        if j % 2 == 0:
                            pe.wait_ge(acc_free, b + (j // 2 - 1))
                        if j < 2:
                            pe.wait_ge(o_done, done + 12 * (j + 1))
                        unit(j, q, (j // 2 + 1) % 2, 4 * (j % 2), h_hi, h_lo, j % 2 == 0, j % 2 == 1)
                        if first:
                            ada_beside(i * 2 + ADA_OUT, j)
                sum_result_squares(2 * layer)
                sum_squares(2 * layer + 1)
                with pe.Fori(0, CHUNKS) as ch:
                    for k in range(Q_CHUNK):
                        q, b = ch * Q_CHUNK + quad(layer, Q_MLP + k), ch * B_CHUNK + blk(layer, B_MLP)
                        for j in range(4):
                            if k < 4:
                                if j == 0:
                                    pe.wait_ge(acc_free, b + (k - 1))
                                if k == 0:
                                    pe.wait_ge(h_ready, 16 * layer + 8 + 2 * j + 2)
                                unit(j, q, k % 2, 4 * j, h_hi, h_lo, j == 0, j == 3)
                            else:
                                if j % 2 == 0:
                                    pe.wait_ge(acc_free, b + (4 + 2 * (k - 4) + j // 2 - 1))
                                if k == 4 and j < 2:
                                    pe.wait_ge(hid_ready, ch * 4 + (32 * layer + 1 + 2 * (j + 1)))
                                unit(j, q, j // 2, 4 * (j % 2), hid_hi, hid_lo, j % 2 == 0, j % 2 == 1)
                            if first and k in ADA_OF_QUAD and j == 2:
                                turn_sums(ch * 6 + (ADA_OF_QUAD[k] + ADA_BLOCKS), ADA_OF_QUAD[k] % 2)
                sum_result_squares(2 * layer + 1)
            for g in range(12):
                j, b = divmod(g, 3)
                pe.wait_ge(x_updated, 24 + 2 * j + 2)
                if g >= 4:
                    pe.wait_ge(y_copied, g - 3)
                for t in range(4):
                    last = nc.tensor.transpose(ps[:, g % 4, P * t:P * t + P], x[:, 4 * j + t, P * b:P * b + P], ident[:, :])
                last.then_inc(y_turned, 1)


_INS = ["x_prompt", "x_sample", "cache_k", "cache_v", "c", "c_ctx", "w_ada", "b_ada", "g_pre1", "g_post1", "g_pre2",
        "g_post2", "w_in", "sink", "w_pool", "pool_scale", "conv_dw", "conv_b", "conv_ln_g", "conv_ln_b", "w_conv_pw",
        "w_out", "w_mlp1", "w_mlp2"]
_OUTS = [(1, CTX, D), (1, LAT, D), (1, DEPTH, CTX, KV_HEADS, HD), (1, DEPTH, CTX, KV_HEADS, HD)]


def shape_tables():
    import numpy as np

    grid_w, quarter = 64, HD // 4
    inv_freq = (1.0 / (np.float32(10000.0) ** (np.arange(quarter, dtype=np.float32) / np.float32(quarter)))).astype(np.float32)
    token = np.arange(LAT)
    pos = np.stack([token // grid_w, token % grid_w]).astype(np.float32)
    cos, sin = np.empty((P, LAT), np.float32), np.empty((P, LAT), np.float32)
    for p in range(P):
        angle = pos[p % HD // (HD // 2)] * inv_freq[p % quarter]
        cos[p] = np.cos(angle)
        sin[p] = np.sin(angle) * (-1 if p % (2 * quarter) < quarter else 1)
    edge = np.ones((4, 2, 2, P_HALF), np.float32)
    for g, w in enumerate(POOL_WINDOWS):
        for s, length in enumerate((CTX, LAT)):
            for e, first in enumerate((0, length - P_HALF)):
                t = first + np.arange(P_HALF)
                edge[g, s, e] = w / (np.clip(t - w // 2 + w, 0, length) - np.clip(t - w // 2, 0, length))
    return {"rope_cos": cos, "rope_sin": sin, "pool_edge": edge}


def kernel(**inputs):
    import numpy as _np
    import concourse.bacc as _bacc
    from concourse import mybir as _mybir
    from concourse.bass_utils import run_bass_kernel_spmd as _run

    nc = _bacc.Bacc("TRN2", target_bir_lowering=False, num_devices=1)
    arrays, args = {}, []
    for name, a in [(n, inputs[n]) for n in _INS] + list(shape_tables().items()):
        a = _np.ascontiguousarray(a)
        arrays[f"in_{name}_dram"] = a
        args.append(nc.dram_tensor(f"in_{name}_dram", a.shape, _mybir.dt.from_np(a.dtype), kind="ExternalInput").ap())
    for i, shape in enumerate(_OUTS):
        args.append(nc.dram_tensor(f"out_{i}_dram", shape, _mybir.dt.float32, kind="ExternalOutput").ap())
    backbone(nc, *args)
    r = _run(nc, [arrays], core_ids=[0])
    return tuple(r.results[0][f"out_{i}_dram"] for i in range(len(_OUTS)))
```
